# Optimizing a Trainium2 kernel written in Bass

```python
import jax, jax.numpy as jnp
from jax import lax
import numpy as np

D_MODEL = 1024
BATCH = 1
SEQ = 512
DEPTH = 1
DEC_BATCH = 8
DEC_SEQ = 16
PAST_LEN = 1024

CHUNK = 64
EPS = 1e-6
SSM_EXPAND = 2
SSM_INNER = SSM_EXPAND * D_MODEL
SSM_HEADDIM = 64
SSM_HEADS = SSM_INNER // SSM_HEADDIM
SSM_GROUPS = 4
SSM_STATE = 128
CONV_WIDTH = 4
CONV_DIM = SSM_INNER + 2 * SSM_GROUPS * SSM_STATE
ATTN_HEADS = 16
ATTN_KV_HEADS = 2
HEAD_DIM = 64
ATTN_REP = ATTN_HEADS // ATTN_KV_HEADS
ATTN_WIDTH = ATTN_HEADS * HEAD_DIM
IDX_HEADS = 8
IDX_DIM = 64
IDX_SCALE = (IDX_HEADS * IDX_DIM) ** -0.5
TOPK_MAX = 256
Q_BLOCK = 128
MOE_GROUPS = 4
EXPERTS_PER_GROUP = 8
N_EXPERTS = MOE_GROUPS * EXPERTS_PER_GROUP
EXPERT_FF = 256
TOPK_IN_GROUP = 2
N_BRANCHES = 2
PROJ_SIZES = (SSM_INNER, CONV_DIM, SSM_HEADS,
              ATTN_WIDTH, ATTN_KV_HEADS * HEAD_DIM, ATTN_KV_HEADS * HEAD_DIM,
              IDX_HEADS * IDX_DIM, IDX_DIM, IDX_HEADS,
              N_BRANCHES * D_MODEL)
PROJ_WIDTH = 9064

kernel_name = "hybrid_ssd_dsa_hiermoe_stream_step"

def rmsnorm(x, g):
    xf = x.astype(jnp.float32)
    y = xf * lax.rsqrt(jnp.mean(xf * xf, axis=-1, keepdims=True) + EPS)
    return (y * g.astype(jnp.float32)).astype(x.dtype)

def causal_conv(xbc, conv_state, w, b):
    T = xbc.shape[1]
    xp = jnp.concatenate([conv_state.astype(xbc.dtype), xbc], axis=1)
    y = b + xp[:, 0:T] * w[0]
    for tap in range(1, CONV_WIDTH):
        y = y + xp[:, tap:tap + T] * w[tap]
    return y, xp[:, -(CONV_WIDTH - 1):]

def ssd_scan(x, dt, A, Bm, Cm, state0, chunk):
    b, T, H, P = x.shape
    G, N = Bm.shape[2], Bm.shape[3]
    R = H // G
    nc = T // chunk
    f32 = jnp.float32
    xc = (x.astype(f32) * dt[..., None]).reshape(b, nc, chunk, G, R, P)
    ac = (dt * A).reshape(b, nc, chunk, G, R)
    Bc = Bm.astype(f32).reshape(b, nc, chunk, G, N)
    Cc = Cm.astype(f32).reshape(b, nc, chunk, G, N)
    causal = jnp.tril(jnp.ones((chunk, chunk), bool))[None, :, :, None, None]

    def chunk_step(state, inp):
        xk, ak, bk, ck = inp
        a_cum = jnp.cumsum(ak, axis=1)
        seg = a_cum[:, :, None] - a_cum[:, None, :]
        decay = jnp.where(causal, jnp.exp(jnp.where(causal, seg, 0.0)), 0.0)
        cb = jnp.einsum('blgn,bsgn->blsg', ck, bk)
        y = jnp.einsum('blsg,blsgr,bsgrp->blgrp', cb, decay, xk)
        y = y + jnp.einsum('blgn,bgrpn,blgr->blgrp', ck, state, jnp.exp(a_cum))
        to_end = jnp.exp(a_cum[:, -1:] - a_cum)
        state = (state * jnp.exp(a_cum[:, -1])[..., None, None]
                 + jnp.einsum('blgn,blgr,blgrp->bgrpn', bk, to_end, xk))
        return state, y

    s0 = state0.astype(f32).reshape(b, G, R, P, N)
    inputs = (jnp.moveaxis(xc, 1, 0), jnp.moveaxis(ac, 1, 0),
              jnp.moveaxis(Bc, 1, 0), jnp.moveaxis(Cc, 1, 0))
    final, ys = lax.scan(chunk_step, s0, inputs)
    y = jnp.moveaxis(ys, 0, 1).reshape(b, T, H, P)
    return y, final.reshape(b, H, P, N)

def dsa_attention(q, k_all, v_all, qi, kidx_all, wi, past_len):
    b, T = q.shape[0], q.shape[1]
    L = k_all.shape[1]
    topk = min(TOPK_MAX, L // 4)
    qblk = min(Q_BLOCK, T)
    nblk = T // qblk
    f32 = jnp.float32
    key_chunk = jnp.arange(L) // CHUNK
    kidx_f = kidx_all.astype(f32)

    def block(args):
        qb, qib, wib, start = args
        q_chunk = (past_len + start + jnp.arange(qblk)) // CHUNK
        adm = key_chunk[None, :] <= q_chunk[:, None]
        dots = jnp.einsum('bqhd,bsd->bqhs', qib.astype(f32), kidx_f)
        iscore = jnp.einsum('bqh,bqhs->bqs', wib.astype(f32) * IDX_SCALE, jax.nn.relu(dots))
        iscore = jnp.where(adm[None], iscore, -jnp.inf)
        _, sel = lax.top_k(iscore, topk)
        valid = (sel // CHUNK) <= q_chunk[None, :, None]
        k_sel = jax.vmap(lambda kk, ii: kk[ii])(k_all, sel)
        v_sel = jax.vmap(lambda vv, ii: vv[ii])(v_all, sel)
        qg = qb.reshape(b, qblk, ATTN_KV_HEADS, ATTN_REP, HEAD_DIM).astype(f32)
        s = jnp.einsum('bqgrd,bqkgd->bqgrk', qg, k_sel.astype(f32)) * (HEAD_DIM ** -0.5)
        s = jnp.where(valid[:, :, None, None, :], s, -jnp.inf)
        p = jax.nn.softmax(s, axis=-1)
        o = jnp.einsum('bqgrk,bqkgd->bqgrd', p, v_sel.astype(f32))
        return o.reshape(b, qblk, ATTN_WIDTH).astype(qb.dtype)

    def to_blocks(a):
        return jnp.moveaxis(a.reshape((b, nblk, qblk) + a.shape[2:]), 1, 0)

    out = lax.map(block, (to_blocks(q), to_blocks(qi), to_blocks(wi), jnp.arange(nblk) * qblk))
    return jnp.moveaxis(out, 0, 1).reshape(b, T, ATTN_WIDTH)

def mixer_sublayer(x, conv_state, ssm_state, k_past, v_past, kidx_past,
                   norm_g, w_in, conv_w, conv_b, dt_bias, A_log, D_skip,
                   ssm_norm_g, w_ssm_out, w_attn_out, w_o):
    b, T, _ = x.shape
    past_len = k_past.shape[1]
    f32 = jnp.float32
    h = rmsnorm(x, norm_g)
    proj = h @ w_in
    split_points = tuple(int(s) for s in np.cumsum(PROJ_SIZES)[:-1])
    z, xbc, dt_raw, q, k, v, qi, ki, wi, g = jnp.split(proj, split_points, axis=-1)

    xbc, conv_new = causal_conv(xbc, conv_state, conv_w, conv_b)
    xbc = jax.nn.silu(xbc)
    xs, Bm, Cm = jnp.split(xbc, (SSM_INNER, SSM_INNER + SSM_GROUPS * SSM_STATE), axis=-1)
    xs = xs.reshape(b, T, SSM_HEADS, SSM_HEADDIM)
    dt = jax.nn.softplus(dt_raw.astype(f32) + dt_bias.astype(f32))
    A = -jnp.exp(A_log.astype(f32))
    y_ssd, ssm_new = ssd_scan(xs, dt, A,
                              Bm.reshape(b, T, SSM_GROUPS, SSM_STATE),
                              Cm.reshape(b, T, SSM_GROUPS, SSM_STATE),
                              ssm_state, min(CHUNK, T))
    y_ssd = y_ssd + D_skip.astype(f32)[:, None] * xs.astype(f32)
    y_ssd = y_ssd.reshape(b, T, SSM_INNER).astype(x.dtype)
    y_ssd = rmsnorm(y_ssd * jax.nn.silu(z), ssm_norm_g)
    branch_a = y_ssd @ w_ssm_out

    k = k.reshape(b, T, ATTN_KV_HEADS, HEAD_DIM)
    v = v.reshape(b, T, ATTN_KV_HEADS, HEAD_DIM)
    k_all = jnp.concatenate([k_past.astype(k.dtype), k], axis=1)
    v_all = jnp.concatenate([v_past.astype(v.dtype), v], axis=1)
    kidx_all = jnp.concatenate([kidx_past.astype(ki.dtype), ki], axis=1)
    o = dsa_attention(q.reshape(b, T, ATTN_HEADS, HEAD_DIM), k_all, v_all,
                      qi.reshape(b, T, IDX_HEADS, IDX_DIM), kidx_all, wi, past_len)
    branch_b = o @ w_attn_out

    gates = jax.nn.sigmoid(g.astype(f32)).reshape(b, T, N_BRANCHES, D_MODEL)
    merged = (gates[:, :, 0] * branch_a.astype(f32)
              + gates[:, :, 1] * branch_b.astype(f32)).astype(x.dtype)
    return x + merged @ w_o, k, v, ki, conv_new, ssm_new

def moe_sublayer(x, norm_g, w_router_group, b_router_group, w_router_expert,
                 b_router_expert, w1, w3, w2):
    f32 = jnp.float32
    h = rmsnorm(x, norm_g)
    glog = (h @ w_router_group).astype(f32) + b_router_group.astype(f32)
    gprob = jax.nn.softmax(glog, axis=-1)
    gsel = jnp.argmax(glog, axis=-1)
    p_group = jnp.take_along_axis(gprob, gsel[:, None], axis=-1)
    elog = ((h @ w_router_expert).astype(f32) + b_router_expert.astype(f32)).reshape(
        -1, MOE_GROUPS, EXPERTS_PER_GROUP)
    elog_g = jnp.take_along_axis(elog, gsel[:, None, None], axis=1)[:, 0]
    top_v, top_i = lax.top_k(elog_g, TOPK_IN_GROUP)
    top_w = jax.nn.softmax(top_v, axis=-1) * p_group
    eid = gsel[:, None] * EXPERTS_PER_GROUP + top_i
    combine = jnp.sum(jax.nn.one_hot(eid, N_EXPERTS, dtype=f32) * top_w[..., None], axis=1)
    y = jnp.zeros(x.shape, f32)
    for e in range(N_EXPERTS):
        he = jax.nn.silu(h @ w1[e]) * (h @ w3[e])
        y = y + combine[:, e:e + 1] * (he @ w2[e]).astype(f32)
    return x + y.astype(x.dtype)

def setup_inputs(seed: int = 0) -> dict:
    key = jax.random.key(seed)
    ks = jax.random.split(key, 32)
    f32 = jnp.float32
    nrm = lambda k, shape, s: jax.random.normal(k, shape, f32) * s
    dt_init = jnp.exp(jax.random.uniform(ks[10], (SSM_HEADS,), f32, np.log(1e-3), np.log(1e-1)))
    return {
        "x_prompt": nrm(ks[0], (BATCH, SEQ, D_MODEL), 1.0),
        "x_sample": nrm(ks[1], (DEC_BATCH, DEC_SEQ, D_MODEL), 1.0),
        "cache_k": nrm(ks[2], (DEC_BATCH, PAST_LEN, ATTN_KV_HEADS, HEAD_DIM), 1.0),
        "cache_v": nrm(ks[3], (DEC_BATCH, PAST_LEN, ATTN_KV_HEADS, HEAD_DIM), 1.0),
        "cache_kidx": nrm(ks[4], (DEC_BATCH, PAST_LEN, IDX_DIM), 1.0),
        "state_conv": nrm(ks[5], (DEC_BATCH, CONV_WIDTH - 1, CONV_DIM), 1.0),
        "state_ssm": nrm(ks[6], (DEC_BATCH, SSM_HEADS, SSM_HEADDIM, SSM_STATE), 0.3),
        "norm_mix_g": 1.0 + nrm(ks[7], (D_MODEL,), 0.02),
        "w_in": nrm(ks[8], (D_MODEL, PROJ_WIDTH), D_MODEL ** -0.5),
        "conv_w": nrm(ks[9], (CONV_WIDTH, CONV_DIM), CONV_WIDTH ** -0.5),
        "conv_b": nrm(ks[11], (CONV_DIM,), 0.01),
        "dt_bias": dt_init + jnp.log(-jnp.expm1(-dt_init)),
        "A_log": jnp.log(jax.random.uniform(ks[12], (SSM_HEADS,), f32, 1.0, 16.0)),
        "D_skip": 1.0 + nrm(ks[13], (SSM_HEADS,), 0.02),
        "ssm_norm_g": 1.0 + nrm(ks[14], (SSM_INNER,), 0.02),
        "w_ssm_out": nrm(ks[15], (SSM_INNER, D_MODEL), SSM_INNER ** -0.5),
        "w_attn_out": nrm(ks[16], (ATTN_WIDTH, D_MODEL), ATTN_WIDTH ** -0.5),
        "w_o": nrm(ks[17], (D_MODEL, D_MODEL), D_MODEL ** -0.5),
        "norm_moe_g": 1.0 + nrm(ks[18], (D_MODEL,), 0.02),
        "w_router_group": nrm(ks[19], (D_MODEL, MOE_GROUPS), D_MODEL ** -0.5),
        "b_router_group": nrm(ks[20], (MOE_GROUPS,), 0.01),
        "w_router_expert": nrm(ks[21], (D_MODEL, N_EXPERTS), D_MODEL ** -0.5),
        "b_router_expert": nrm(ks[22], (N_EXPERTS,), 0.01),
        "w1": nrm(ks[23], (N_EXPERTS, D_MODEL, EXPERT_FF), D_MODEL ** -0.5),
        "w3": nrm(ks[24], (N_EXPERTS, D_MODEL, EXPERT_FF), D_MODEL ** -0.5),
        "w2": nrm(ks[25], (N_EXPERTS, EXPERT_FF, D_MODEL), EXPERT_FF ** -0.5),
        "norm_final_g": 1.0 + nrm(ks[26], (D_MODEL,), 0.02),
    }

def reference(x_prompt, x_sample, cache_k, cache_v, cache_kidx, state_conv, state_ssm,
              norm_mix_g, w_in, conv_w, conv_b, dt_bias, A_log, D_skip, ssm_norm_g,
              w_ssm_out, w_attn_out, w_o, norm_moe_g, w_router_group, b_router_group,
              w_router_expert, b_router_expert, w1, w3, w2, norm_final_g):
    b, T, D = x_prompt.shape
    db, ts = x_sample.shape[0], x_sample.shape[1]
    dtype = x_prompt.dtype
    zero_conv = jnp.zeros((b, CONV_WIDTH - 1, CONV_DIM), dtype)
    zero_ssm = jnp.zeros((b, SSM_HEADS, SSM_HEADDIM, SSM_STATE), jnp.float32)
    empty_kv = jnp.zeros((b, 0, ATTN_KV_HEADS, HEAD_DIM), dtype)
    empty_kidx = jnp.zeros((b, 0, IDX_DIM), dtype)
    mix_w = (norm_mix_g, w_in, conv_w, conv_b, dt_bias, A_log, D_skip,
             ssm_norm_g, w_ssm_out, w_attn_out, w_o)
    xp, xs = x_prompt, x_sample
    for layer in range(DEPTH):
        xp, kp, vp, kip, cp, sp = mixer_sublayer(xp, zero_conv, zero_ssm, empty_kv, empty_kv,
                                                 empty_kidx, *mix_w)
        xs, ksn, vsn, kisn, csn, ssn = mixer_sublayer(xs, state_conv, state_ssm, cache_k,
                                                      cache_v, cache_kidx, *mix_w)
        tokens = jnp.concatenate([xp.reshape(b * T, D), xs.reshape(db * ts, D)], axis=0)
        tokens = moe_sublayer(tokens, norm_moe_g, w_router_group, b_router_group,
                              w_router_expert, b_router_expert, w1, w3, w2)
        xp = tokens[:b * T].reshape(b, T, D)
        xs = tokens[b * T:].reshape(db, ts, D)
    y_prompt = rmsnorm(xp, norm_final_g)
    y_sample = rmsnorm(xs, norm_final_g)
    return (y_prompt, y_sample, kp, vp, kip, cp, sp, ksn, vsn, kisn, csn, ssn)


_drawn_inputs = setup_inputs


def setup_inputs(seed=0):
    import zlib

    import numpy as np

    out = dict(_drawn_inputs(seed))
    spreads = {}
    factors = {'conv_b': 3.399,
     'D_skip': 2.774,
     'ssm_norm_g': 2.808,
     'b_router_group': 18.801,
     'b_router_expert': 14.746,
     'norm_final_g': 7.827,
     'norm_moe_g': 2.993}
    for name, (base, spread) in spreads.items():
        noise = np.random.default_rng([zlib.crc32(name.encode()), seed]).standard_normal(out[name].shape)
        drawn = base * np.exp(spread * noise) if base else spread * noise
        out[name] = __import__('jax').numpy.asarray(drawn.astype(out[name].dtype))
    for name, factor in factors.items():
        out[name] = (out[name] * factor).astype(out[name].dtype)
    return out
```

```python
from contextlib import ExitStack

import concourse.bass as bass
from concourse import mybir

F32 = mybir.dt.float32
ALU = mybir.AluOpType
ACT = mybir.ActivationFunctionType
AX = mybir.AxisListType

P = 128
D = 1024
KD = D // P
TP = 512
SB, SQ = 8, 16
T = TP + SB * SQ
NT = T // P
SMP = NT - 1
PAST = 1024
KEYS = PAST + SQ
KJ = PAST // P
EPS = 1e-6
INNER, HEADS, HP, GROUPS, NS = 2048, 32, 64, 4, 128
HG = HEADS // GROUPS
CD = INNER + 2 * GROUPS * NS
CT = CD // P
CW = 4
AH, AKV, HD = 16, 2, 64
AR = AH // AKV
IH, IDIM = 8, 64
IDX_SCALE = (IH * IDIM) ** -0.5
TOPK_P, TOPK_S = 128, 256
CHUNK = 64
ATT_SCALE = HD ** -0.5
MG, ME = 4, 8
NE = MG * ME
FF = 256
Z0 = 0
X0 = INNER
B0 = X0 + INNER
C0 = B0 + GROUPS * NS
DT0 = X0 + CD
Q0 = DT0 + HEADS
K0 = Q0 + AH * HD
V0 = K0 + AKV * HD
QI0 = V0 + AKV * HD
KI0 = QI0 + IH * IDIM
WI0 = KI0 + IDIM
G0 = WI0 + IH
SK, SV, SKI, SWI, SDT, SW = 0, 128, 256, 320, 328, 360
NEG = -1.0e30
NOTADM = -1.0e38
TAKEN = -3.0e38
CUT = -2.0e38


class Banks:

    def __init__(self):
        self.job, self.turn = {}, {}
        self.full, self.free = [0] * 8, [0] * 8
        self.last = [None] * 8

    def add(self, key, pool, readers=1, width=1):
        assert key not in self.job, key
        i = self.turn.get(pool, 0)
        self.turn[pool] = i + 1
        b = pool[i % len(pool)]
        before = sorted({self.last[c] for c in range(b, b + width) if self.last[c]})
        self.full[b] += 1
        self.free[b] += readers
        for c in range(b, b + width):
            self.last[c] = (b, self.free[b])
        self.job[key] = (b, self.full[b], before, self.free[b])


class Ring:

    def __init__(self, slots):
        self.slots, self.job, self.order, self.loads = slots, {}, [], [0] * slots

    def add(self, key, used, parts):
        s = len(self.order) % self.slots
        self.loads[s] += 16 * len(parts)
        self.job[key] = (s, self.loads[s])
        self.order.append((key, used, parts))


def plan_banks():
    b = Banks()
    any8 = tuple(range(8))
    for i in range(2):
        b.add(("par", i), any8)
    for tt in range(NT):
        for c in range(2):
            b.add(("hT", tt, c), any8)
    for tt in range(NT):
        b.add(("kv", tt), any8)
    for c in range(2):
        for t in range(4 * c, 4 * c + 4):
            b.add(("q", t), any8)
        b.add(("qS", c), any8)
    for t in range(4):
        b.add(("qi", t), any8)
    b.add(("qiS",), any8)
    for i in range(4):
        b.add(("kT", i), any8)
    for i in range(1, 4):
        for h in range(IH):
            b.add(("pd", i, h), any8)
    b.add(("wc",), (3,))
    for i in range(3):
        b.add(("di", i), (0, 1, 2))
    work = (3, 4, 5, 6, 7)
    for s in range(SB + 2):
        if s < SB:
            b.add(("kx", s, 0), work)
            b.add(("kx", s, 1), work)
        if 1 <= s <= SB:
            for c in range(3):
                b.add(("dd", s - 1, c), work)
    for tt in range(NT):
        b.add(("ac", tt), any8)
        b.add(("ae", tt), any8, readers=2)
    for g in range(GROUPS):
        plan_group(b, g)
    for i in range(NT - 1):
        for h in range(AH + 1):
            if h < AH:
                b.add(("s", i, h), (0, 1, 2))
            if h > 0:
                b.add(("pT", i, h - 1), (3, 4, 5))
                if (h - 1) % AR == 0:
                    b.add(("o", i, (h - 1) // AR), (6, 7))
        for c in range(2):
            b.add(("oT", i, c), (3, 4, 5))
    for s in range(SB):
        b.add(("kc", s, 0), (6, 7))
        b.add(("kc", s, 1), (6, 7))
        for g in range(AKV):
            b.add(("ds", s, g), (0, 3), width=3)
        for g in range(AKV):
            for c in range(3):
                b.add(("pt", s, g, c), (6, 7))
        b.add(("do", s), (6, 7))
        b.add(("dT", s), (6, 7))
    for n in range(2):
        for what in ("ga", "gb", "a", "b"):
            for c in range(4):
                b.add((what, n, c), (0, 1, 2, 3))
            b.add((what + "S", n), (4, 5, 6, 7))
    for tt in range(NT):
        for n in range(2):
            b.add(("x1", tt, n), any8)
    for tt in range(NT):
        for c in range(2):
            b.add(("h2", tt, c), any8)
    for tt in range(NT):
        b.add(("rt", tt), any8)
    for e in range(NE):
        b.add(("heS", e), (4,), readers=2)
        for j in range(4):
            b.add(("he", e, j), (0, 1, 2, 3))
        for tt in range(NT):
            for n in range(2):
                b.add(("y", e, tt, n), (5, 6, 7))
    return b


def plan_group(b, g):
    lo, hi = (0, 1, 2, 3), (4, 5, 6, 7)
    b.add(("cT", g), hi)
    b.add(("xbcS", g, 0), hi)
    for j in range(4):
        b.add(("xbc", g, j), lo)
    b.add(("xbcS", g, 1), hi)
    for j in range(4, 6):
        b.add(("xbc", g, j), lo)
    for j in range(4):
        b.add(("z", g, j), lo)
    b.add(("zS", g), hi)
    b.add(("cO", g, 0), hi)
    b.add(("cO", g, 1), hi)
    b.add(("bt", g, 0), hi)
    b.add(("bt", g, 1), hi)
    for tt in range(NT):
        b.add(("xt", g, tt), lo)
        b.add(("cb", g, tt), hi)
        for i in range(2):
            b.add(("sg", g, tt, i), lo)
        b.add(("eb", g, tt), hi)
        if 0 < tt < SMP:
            b.add(("yi", g, tt), lo)
        if tt < SMP:
            b.add(("st", g, tt), hi)
        b.add(("yo", g, tt), lo)
    b.add(("so", g), hi)
    for j in range(4):
        for i in range(2):
            b.add(("s0", g, j, i), lo)
        for i in range(2):
            b.add(("sn", g, j, i), hi)
        b.add(("ys", g, j), lo)
    for i in range(2):
        b.add(("ss", g, i), hi)


def hybrid_layer(nc, x_prompt, x_sample, cache_k, cache_v, cache_kidx, state_conv, state_ssm,
                 norm_mix_g, w_in, conv_w, conv_b, dt_bias, A_log, D_skip, ssm_norm_g,
                 w_ssm_out, w_attn_out, w_o, norm_moe_g, w_router_group, b_router_group,
                 w_router_expert, b_router_expert, w1, w3, w2, norm_final_g,
                 y_prompt, y_sample, k_prompt, v_prompt, kidx_prompt, conv_prompt, ssm_prompt,
                 k_sample, v_sample, kidx_sample, conv_sample, ssm_sample):
    banks = plan_banks()
    w_in_r = w_in.rearrange("(k p) n -> p k n", p=P)

    ring = Ring(3)

    def cols(a, n, at=0):
        return (lambda s: s[:, :, at:at + n], w_in_r[:, :, a:a + n])

    ring.add(("small",), ("kv", NT - 1), [cols(K0, 256), cols(KI0, 72, SKI), cols(DT0, 32, SDT)])
    for c in range(2):
        ring.add(("wq", c), ("qS", c), [
            (lambda s, k=k, g=g: s[:, k, :].rearrange("p (t g d) -> p g t d", g=AKV, d=HD)[:, g, :, :],
             w_in[k * P:(k + 1) * P, Q0 + g * AR * HD + c * 256:Q0 + g * AR * HD + c * 256 + 256]
             .rearrange("p (t d) -> p t d", d=HD))
            for k in range(KD) for g in range(AKV)])
    ring.add(("wqi",), ("qiS",), [cols(QI0, 512)])
    for g in range(GROUPS):
        ring.add(("wx", g), ("xbc", g, 3), [cols(X0 + 512 * g, 512)])
        ring.add(("wbc", g), ("xbc", g, 5), [cols(B0 + NS * g, NS), cols(C0 + NS * g, NS, NS)])
        ring.add(("wz", g), ("zS", g), [cols(Z0 + 512 * g, 512)])
    wso_r = w_ssm_out.rearrange("(k p) n -> p k n", p=P)
    for n in range(2):
        ring.add(("wga", n), ("gaS", n), [cols(G0 + 512 * n, 512)])
        ring.add(("wgb", n), ("gbS", n), [cols(G0 + D + 512 * n, 512)])
        for c in range(2):
            ring.add(("wso", n, c), ("aS", n), [(lambda s: s[:, :, :], wso_r[:, 8 * c:8 * c + 8, 512 * n:512 * n + 512])])
        ring.add(("wao", n), ("bS", n), [
            (lambda s, g=g: s[g * HD:(g + 1) * HD, :, :],
             w_attn_out[g * AR * HD:(g + 1) * AR * HD, 512 * n:512 * n + 512].rearrange("(t d) n -> d t n", d=HD))
            for g in range(AKV)])
    wo_r = w_o.rearrange("(k p) n -> p k n", p=P)
    for n in range(2):
        ring.add(("wo", n), ("x1", NT - 1, 1), [(lambda s: s[:, :, :], wo_r[:, :, 512 * n:512 * n + 512])])
    for e in range(NE):
        ring.add(("w13", e), ("heS", e), [
            (lambda s: s[:, :, 0:FF], w1[e].rearrange("(k p) f -> p k f", p=P)),
            (lambda s: s[:, :, FF:2 * FF], w3[e].rearrange("(k p) f -> p k f", p=P))])
        ring.add(("w2", e), ("y", e, NT - 1, 1), [
            (lambda s: s.rearrange("p k n -> p (k n)")[:, 0:2 * D].rearrange("p (k n) -> p k n", k=2),
             w2[e].rearrange("(k p) n -> p k n", p=P))])

    with ExitStack() as ctx:
        def sb(name, shape):
            return ctx.enter_context(nc.sbuf_tensor(name, shape, F32))

        def sem(name):
            return ctx.enter_context(nc.semaphore(name))

        psum = ctx.enter_context(nc.psum_tensor("psum", [P, 8 * 512], F32))

        ident = sb("ident", [P, P])
        ones = sb("ones", [P, P])
        cum_p, cum_s = sb("cum_p", [P, P]), sb("cum_s", [P, P])
        neg_p, neg_s = sb("neg_p", [P, P]), sb("neg_s", [P, P])
        same = sb("same", [P, P])
        stream = sb("stream", [P, SB])
        adm_idx, adm_att = sb("adm_idx", [P, P]), sb("adm_att", [P, P])
        qsel = sb("qsel", [P, SQ])
        rsel = sb("rsel", [P, SB, P])
        prio = sb("prio", [P, ME])
        pc = sb("pc", [P, 2, P])
        a_row, dtb_row, dsk_row = sb("a_row", [P, HEADS]), sb("dtb_row", [P, HEADS]), sb("dsk_row", [P, HEADS])
        dcol = sb("dcol", [P, HEADS // 2])
        brow = sb("brow", [P, MG + NE])
        cw_col = pc[:, 0, 0:CW * CT].rearrange("p (w c) -> p w c", w=CW)
        cb_col = pc[:, 0, CW * CT:CW * CT + CT]
        gmix = pc[:, 0, 120:128]
        gmoe = pc[:, 1, 0:8]
        gssm = pc[:, 1, 8:24]
        ssq = sb("ssq", [P, 6, 8])

        wring = sb("wring", [P, 3, KD, 512])
        hT = sb("hT", [P, KD, T])
        kvtm = sb("kvtm", [P, NT, SW])
        oT = sb("oT", [P, KD, T])
        oTf = oT[:].rearrange("p k t -> p (k t)")
        arena = sb("arena", [P, 26200])

        class Arena:

            def __init__(self, base, at=0):
                self.base, self.at = base, at

            def take(self, *shape):
                n = 1
                for s in shape:
                    n *= s
                v = self.base[:, self.at:self.at + n]
                self.at += n
                assert self.at <= self.base.shape[1], self.at
                if len(shape) == 1:
                    return v
                names = "abcd"[:len(shape)]
                return v.rearrange(f"p ({' '.join(names)}) -> p {' '.join(names)}",
                                   **{names[i]: shape[i] for i in range(len(shape))})

        keep = Arena(arena)
        kT, qs = keep.take(T), keep.take(SB, KD, SQ)
        bias_p = [None] + [keep.take(P * (i + 1)) for i in range(1, 4)]
        bias_s = keep.take(KEYS)
        ssrow = keep.take(T)
        kept = keep.at
        a1 = Arena(arena, kept)
        xtm, par, junk = a1.take(NT, D), a1.take(2, P), a1.take(D)
        a1 = Arena(arena, a1.at)
        qiT, qis, kiT = a1.take(IH, TP), a1.take(SB, IH, SQ), a1.take(T)
        wsel, wl, wcol = a1.take(SB, P), a1.take(P), a1.take(SB)
        rel, kx_in, kxT = a1.take(2, KEYS), a1.take(2, KJ, IDIM), a1.take(2, PAST)
        top8 = a1.take(8)
        a2 = Arena(arena, kept)
        raw, acc = a2.take(2, 667), a2.take(1, 664)
        xsT, bcT, zT = a2.take(4, T), a2.take(2, T), a2.take(4, T)
        yb = oTf.rearrange("p (u j t) -> p u j t", u=2, j=4)
        btm, bms = a2.take(NT, NS), a2.take(SB, NS)
        xdt, xw = a2.take(2, 512), a2.take(2, 512)
        mt, cbs, ebs = a2.take(3, 512), a2.take(2, P), a2.take(2, 512)
        ytmp, stT = a2.take(512), a2.take(512)
        dtv, av, nac, expae, w2v = (a2.take(NT, HEADS) for _ in range(5))
        st0, s0T = a2.take(2, SB, NS), a2.take(SB, P)
        sout, cin, cst = a2.take(512), a2.take(6, P), a2.take(6, 24)
        cgo, crow = a2.take(6, 27), cin
        a3 = Arena(arena, kept)
        sm, pT, otm = a3.take(2, 512), a3.take(2, 512), a3.take(D)
        mx, rsum, rinv = a3.take(2, AH), a3.take(2, AH), a3.take(2, AH)
        kb, vb, kcT = a3.take(2, KJ, P), a3.take(2, KJ, P), a3.take(2, PAST)
        pexp, ptS, ptN = a3.take(2, KEYS), a3.take(2, KJ, P), a3.take(2, P)
        ob, vnew = a3.take(2, P), a3.take(SB, P)
        a4 = Arena(arena, 0)
        mrg = a4.take(KD, T)
        gate = a4.take(2, 4, T)
        rr, rt = a4.take(T), a4.take(T)
        yz = a4.take(16, T)
        a5 = Arena(arena, KD * T)
        xres, x1 = a5.take(2, D), a5.take(NT, D)
        h2T, ysum = a5.take(KD, T), a5.take(NT, D)
        a6 = Arena(arena, 0)
        heT, hsil = a6.take(2, 2, T), a6.take(2, T)
        wr, lg, xn = a5.take(KD, MG + NE), a5.take(NT, MG + NE), oTf.rearrange("p (t d) -> p t d", t=NT)
        rb = [a5.take(NT, ME) for _ in range(6)]
        comb = a5.take(NT, MG, ME)
        rc = [a5.take(NT, MG) for _ in range(3)]
        rs1 = a5.take(8, NT)
        fin_row = hT[:].rearrange("p k t -> p (k t)")[:, 0:D]

        q_spill = nc.dram_tensor("q_spill", (P, KD, TP), F32, kind="Internal").ap()
        y_spill = nc.dram_tensor("y_spill", (P, 16, T), F32, kind="Internal").ap()

        full = [sem(f"full{i}") for i in range(8)]
        free = [sem(f"free{i}") for i in range(8)]
        slot_loaded = [sem(f"slot_loaded{i}") for i in range(3)]
        params_loaded, rows_loaded = sem("params_loaded"), sem("rows_loaded")
        x_loaded = [sem(f"x_loaded{i}") for i in range(NT)]
        consts, out_written = sem("consts"), sem("out_written")
        dve_chain, act_chain, pool_chain = sem("dve_chain"), sem("act_chain"), sem("pool_chain")

        def bank(key, width=1):
            b = banks.job[key][0]
            return psum[:, b * 512:(b + width) * 512]

        def claim(pe, key):
            for b, n in banks.job[key][2]:
                pe.wait_ge(free[b], n)
            return bank(key)

        def filled(ins, key):
            ins.then_inc(full[banks.job[key][0]], 1)

        def wait_full(eng, key):
            b, n, _, _ = banks.job[key]
            eng.wait_ge(full[b], n)

        def release(ins, key):
            ins.then_inc(free[banks.job[key][0]], 1)

        def wait_read(eng, key, short=0):
            b, _, _, n = banks.job[key]
            eng.wait_ge(free[b], n - short)

        def slot(key):
            return wring[:, ring.job[key][0], :, :]

        def wait_chunk(pe, key):
            s, n = ring.job[key]
            pe.wait_ge(slot_loaded[s], n)
            return slot(key)

        S = {name: sem(name) for name in (
            "x_squares", "x_var", "x_std", "x_scaled", "a_row_ready", "wl_ready", "wsel_ready", "rel_used",
            "bias_ready", "dt_exp", "a_exp", "a_ready", "ae_ready", "raw_zeroed", "raw_ready", "conv_done",
            "xs_ready", "gathered", "bms_ready", "mt_exp", "mt_ready", "y_gated", "y_squares", "y_gained",
            "q_spilled", "y_spilled", "crow_written", "sout_written", "q_back", "vnew_loaded", "y_back",
            "router_loaded", "fin_loaded", "at_exp", "ds_nmax", "ss_var", "ss_std", "m_ready", "hx_squares",
            "hx_var", "hx_std", "hx_scaled", "r_exp_in", "r_exp", "ysum_ready", "fx_squares", "fx_var", "fx_std",
            "fin_ready", "y_written")}
        pair = {name: [sem(f"{name}{i}") for i in range(2)] for name in (
            "kx_loaded", "kb_loaded", "vb_loaded", "st0_loaded", "st0_written", "xres_loaded", "cin_loaded")}

        block = ctx.enter_context(nc.Block())
        N_OUT = 3 * NT

        @block.sync
        def _(sp):
            def chunks(upto_key):
                while sent[0] < len(ring.order):
                    key, _, parts = ring.order[sent[0]]
                    if sent[0] >= ring.slots:
                        wait_full(sp, ring.order[sent[0] - ring.slots][1])
                    for part, src in parts:
                        sp.dma_start(part(slot(key)), src).then_inc(slot_loaded[ring.job[key][0]], 16)
                    sent[0] += 1
                    if key == upto_key:
                        return

            sent = [0]
            for tt in range(SMP):
                sp.dma_start(xtm[:, tt, :], x_prompt[0, tt * P:(tt + 1) * P, :]).then_inc(x_loaded[tt], 16)
            sp.dma_start(xtm[:, SMP, :], x_sample.rearrange("b q d -> (b q) d")).then_inc(x_loaded[SMP], 16)
            for lo, hi, i, src in ((0, 96, 0, conv_w.rearrange("w (c p) -> (w c) p", p=P)),
                                   (96, 120, 0, conv_b.rearrange("(c p) -> c p", p=P)),
                                   (120, 128, 0, norm_mix_g.rearrange("(c p) -> c p", p=P)),
                                   (0, 8, 1, norm_moe_g.rearrange("(c p) -> c p", p=P)),
                                   (8, 24, 1, ssm_norm_g.rearrange("(c p) -> c p", p=P))):
                sp.dma_start(par[lo:hi, i, :], src).then_inc(params_loaded, 16)
            for dst, src in ((a_row[:], A_log), (dtb_row[:], dt_bias), (dsk_row[:], D_skip),
                             (brow[:, 0:MG], b_router_group), (brow[:, MG:MG + NE], b_router_expert)):
                sp.dma_start(dst, src.rearrange("(o n) -> o n", o=1).broadcast_to([P, src.shape[0]])) \
                    .then_inc(rows_loaded, 16)
            chunks(("wqi",))
            for s in range(SB):
                if s == 0:
                    wait_read(sp, ("hT", NT - 1, 1))
                if s >= 2:
                    wait_full(sp, ("kx", s - 2, 1))
                sp.dma_start(kx_in[:, s % 2, :, :], cache_kidx[s].rearrange("(p j) d -> p j d", j=KJ)) \
                    .then_inc(pair["kx_loaded"][s % 2], 16)
            sp.wait_ge(S["bias_ready"], 4)
            chunks(("wz", 0))
            for g in range(GROUPS):
                if g:
                    sp.wait_ge(S["crow_written"], 96 * g)
                for at, n, c in ((0, 4, 512 * g), (4, 1, INNER + NS * g), (5, 1, INNER + (GROUPS + g) * NS)):
                    sp.dma_start(cin[0:24, at:at + n, :],
                                 state_conv[:, :, c:c + n * P].rearrange("b r (c p) -> (b r) c p", p=P)) \
                        .then_inc(pair["cin_loaded"][0], 16)
                chunks(("wz", min(g + 1, GROUPS - 1)) if g + 1 < GROUPS else ("wgb", 0))
                for j in range(4):
                    u = 4 * g + j
                    if u >= 2:
                        sp.wait_ge(pair["st0_written"][u % 2], 16 * (u // 2))
                    r = (4 * g + j) * P
                    sp.dma_start(st0[:, u % 2, :, :],
                                 state_ssm.rearrange("b h p n -> (h p) b n")[r:r + P, :, :]) \
                        .then_inc(pair["st0_loaded"][u % 2], 16)
            sp.wait_ge(S["q_spilled"], 16)
            sp.wait_ge(S["y_spilled"], 16 * GROUPS)
            wait_read(sp, ("ss", GROUPS - 1, 1))
            for u in range(2):
                sp.wait_ge(pair["st0_written"][u], 16 * 8)
            sp.wait_ge(S["crow_written"], 16 * 6 * GROUPS)
            sp.wait_ge(S["sout_written"], 16 * GROUPS)
            sp.dma_start(oT[:, :, 0:TP], q_spill[:, :, :]).then_inc(S["q_back"], 16)
            for s in range(SB):
                if s >= 2:
                    wait_full(sp, ("do", s - 2))
                sp.dma_start(kb[:, s % 2, :, :], cache_k[s].rearrange("(p j) g d -> p j (g d)", j=KJ)) \
                    .then_inc(pair["kb_loaded"][s % 2], 16)
                sp.dma_start(vb[:, s % 2, :, :], cache_v[s].rearrange("(p j) g d -> p j (g d)", j=KJ)) \
                    .then_inc(pair["vb_loaded"][s % 2], 16)
            wait_read(sp, ("dT", SB - 1))
            sp.dma_start(yz[:, :, :], y_spill[:, :, :]).then_inc(S["y_back"], 16)
            chunks(("wo", 1))
            sp.wait_ge(S["m_ready"], 2)
            wait_full(sp, ("aS", 1))
            sp.dma_start(wr[:, :, 0:MG], w_router_group.rearrange("(k p) n -> p k n", p=P)).then_inc(S["router_loaded"], 16)
            sp.dma_start(wr[:, :, MG:], w_router_expert.rearrange("(k p) n -> p k n", p=P)).then_inc(S["router_loaded"], 16)
            for tt in range(NT):
                if tt >= 2:
                    wait_read(sp, ("x1", tt - 2, 1))
                src = x_prompt[0, tt * P:(tt + 1) * P, :] if tt < SMP else x_sample.rearrange("b q d -> (b q) d")
                sp.dma_start(xres[:, tt % 2, :], src).then_inc(pair["xres_loaded"][tt % 2], 16)
            wait_full(sp, ("rt", NT - 1))
            sp.dma_start(fin_row, norm_final_g.rearrange("(o n) -> o n", o=1).broadcast_to([P, D])) \
                .then_inc(S["fin_loaded"], 16)
            chunks(None)
            for tt in range(NT):
                sp.wait_ge(S["fin_ready"], tt + 1)
                dst = y_prompt[0, tt * P:(tt + 1) * P, :] if tt < SMP else y_sample.rearrange("b q d -> (b q) d")
                sp.dma_start(dst, ysum[:, tt, :]).then_inc(S["y_written"], 16)
            sp.wait_ge(S["y_written"], 16 * NT)
            sp.wait_ge(out_written, 16 * N_OUT)
            for i in range(2):
                sp.wait_ge(pair["st0_written"][i], 16 * 8)
            sp.wait_ge(S["crow_written"], 16 * 6 * GROUPS)
            sp.wait_ge(S["sout_written"], 16 * GROUPS)

        @block.gpsimd
        def _(pool):
            n = [0]

            def link(ins):
                n[0] += 1
                ins.then_inc(pool_chain, 1)
                pool.wait_ge(pool_chain, n[0])

            def select(out, in_, fill, pattern, base, cm, op=ALU.is_ge):
                link(nc.gpsimd.affine_select(out=out, in_=in_, compare_op=op, fill=fill, base=base,
                                             pattern=pattern, channel_multiplier=cm))

            for t, v in ((ident, 0.0), (ones, 1.0), (cum_p, 1.0), (neg_p, 0.0), (same, 1.0), (stream, 1.0),
                         (adm_idx, 0.0), (adm_att, 0.0)):
                link(nc.gpsimd.memset(t[:], v))
            select(ident[:], ident[:], 1.0, [[-1, P]], 0, 1, ALU.not_equal)
            select(cum_p[:], cum_p[:], 0.0, [[1, P]], 0, -1)
            select(neg_p[:], neg_p[:], NEG, [[1, P]], 0, -1)
            for t, w in ((same, SQ), (stream, 1)):
                v = t[:].rearrange("p (b q) -> p b q", q=w)
                select(v, v, 0.0, [[-SQ, SB], [0, w]], 0, 1)
                select(v, v, 0.0, [[SQ, SB], [0, w]], SQ - 1, -1)
            select(cum_s[:], same[:], 0.0, [[1, P]], 0, -1)
            link(nc.gpsimd.tensor_scalar(neg_s[:], cum_s[:], 1.0, -NEG, ALU.subtract, ALU.mult))
            for t, fill in ((adm_idx, NOTADM), (adm_att, NEG)):
                v = t[:].rearrange("p (a k) -> p a k", k=CHUNK)
                select(v, v, fill, [[-CHUNK, 2], [0, CHUNK]], 0, 1)
            nc.gpsimd.iota(prio[:], [[-1, ME]], base=ME, channel_multiplier=0,
                           allow_small_or_imprecise_dtypes=True).then_inc(consts, 1)
            for tt in range(NT):
                wait_read(pool, ("kv", tt))
                for at, width, dp, ds in ((SK, 128, k_prompt, k_sample), (SV, 128, v_prompt, v_sample),
                                          (SKI, 64, kidx_prompt, kidx_sample)):
                    if tt < SMP:
                        dst = dp[0, tt * P:(tt + 1) * P]
                    else:
                        dst = ds.rearrange("b q g d -> (b q) g d" if width == 128 else "b q d -> (b q) d")
                    if width == 128:
                        dst = dst.rearrange("t g d -> t (g d)")
                    pool.dma_start(dst, kvtm[:, tt, at:at + width]).then_inc(out_written, 16)
            wait_read(pool, ("qS", 1))
            pool.dma_start(q_spill[:, :, :], oT[:, :, 0:TP]).then_inc(S["q_spilled"], 16)
            pool.wait_ge(S["bias_ready"], 4)
            for i in range(2):
                link(nc.gpsimd.memset(raw[:, i, 0:3], 0.0))
            nc.gpsimd.memset(cgo[:, 0, 0:3], 0.0).then_inc(S["raw_zeroed"], 1)
            for g in range(GROUPS):
                for j in range(6):
                    u = 6 * g + j
                    pool.wait_ge(S["raw_ready"], u + 1)
                    if j == 0 and g:
                        wait_full(pool, ("cO", g - 1, 1))
                    nc.gpsimd.tensor_copy(cgo[:, j, 0:3], raw[:, u % 2, 512:515])
                    nc.gpsimd.tensor_copy(cgo[:, j, 3:27].rearrange("p (b r) -> p b r", r=3),
                                          raw[:, u % 2, 515:667].rearrange("p (b q) -> p b q", q=19)[:, :, 16:19]) \
                        .then_inc(S["gathered"], 1)
                wait_read(pool, ("bt", g, 1))
                if g:
                    wait_full(pool, ("sn", g - 1, 3, 1))
                nc.gpsimd.tensor_tensor(bms, btm[:, SMP:SMP + 1, :].broadcast_to([P, SB, NS]),
                                        stream[:].rearrange("p (b o) -> p b o", o=1).broadcast_to([P, SB, NS]),
                                        ALU.mult).then_inc(S["bms_ready"], 1)
                wait_read(pool, ("cO", g, 1))
                for at, n_, c in ((0, 4, 512 * g), (4, 1, INNER + NS * g), (5, 1, INNER + (GROUPS + g) * NS)):
                    pool.dma_start(conv_prompt[0, :, c:c + n_ * P].rearrange("r (c p) -> r c p", p=P),
                                   crow[0:3, at:at + n_, :]).then_inc(S["crow_written"], 16)
                    pool.dma_start(conv_sample[:, :, c:c + n_ * P].rearrange("b r (c p) -> (b r) c p", p=P),
                                   crow[3:27, at:at + n_, :]).then_inc(S["crow_written"], 16)
                wait_read(pool, ("so", g))
                pool.dma_start(ssm_prompt[0].rearrange("h p n -> (h p) n")[g * 512:(g + 1) * 512, :]
                               .rearrange("(j p) n -> p j n", p=P),
                               sout.rearrange("p (j n) -> p j n", n=NS)).then_inc(S["sout_written"], 16)
                for j in range(4):
                    u = 4 * g + j
                    wait_read(pool, ("sn", g, j, 1))
                    pool.dma_start(ssm_sample.rearrange("b h p n -> (h p) b n")[u * P:(u + 1) * P, :, :],
                                   st0[:, u % 2, :, :]).then_inc(pair["st0_written"][u % 2], 16)
                pool.wait_ge(S["y_gained"], g + 1)
                pool.dma_start(y_spill[:, 4 * g:4 * g + 4, :], yb[:, g % 2, :, :]).then_inc(S["y_spilled"], 16)
            wait_read(pool, ("ss", GROUPS - 1, 1))
            for u in range(2):
                pool.wait_ge(pair["st0_written"][u], 16 * 8)
            for s in range(SB):
                pool.dma_start(vnew[0:SQ, s, :], kvtm[SQ * s:SQ * (s + 1), SMP, SV:SV + P]) \
                    .then_inc(S["vnew_loaded"], 16)
        def ssd_pe(pe, g, product, turn, prompt, sample):
            mm = nc.tensor.matmul
            pe.wait_ge(pair["cin_loaded"][0], 16 * 3 * (g + 1))
            o = claim(pe, ("cT", g))
            for j in range(6):
                ins = turn(o[:, 24 * j:24 * (j + 1)], cin[0:24, j, :], 24)
            filled(ins, ("cT", g))
            w = wait_chunk(pe, ("wx", g))
            o = claim(pe, ("xbcS", g, 0))
            for j in range(4):
                ins = product(o[:, j * P:(j + 1) * P], w, j * P, P, sample, P)
            filled(ins, ("xbcS", g, 0))
            for j in range(4):
                o = claim(pe, ("xbc", g, j))
                filled(product(o, w, j * P, P, prompt, TP), ("xbc", g, j))
            w = wait_chunk(pe, ("wbc", g))
            o = claim(pe, ("xbcS", g, 1))
            for j in range(2):
                ins = product(o[:, j * P:(j + 1) * P], w, j * P, P, sample, P)
            filled(ins, ("xbcS", g, 1))
            for j in range(2):
                o = claim(pe, ("xbc", g, 4 + j))
                filled(product(o, w, j * P, P, prompt, TP), ("xbc", g, 4 + j))
            w = wait_chunk(pe, ("wz", g))
            for j in range(4):
                o = claim(pe, ("z", g, j))
                filled(product(o, w, j * P, P, prompt, TP), ("z", g, j))
            o = claim(pe, ("zS", g))
            for j in range(4):
                ins = product(o[:, j * P:(j + 1) * P], w, j * P, P, sample, P)
            filled(ins, ("zS", g))
            pe.wait_ge(S["gathered"], 6 * (g + 1))
            for c, js in ((0, range(4)), (1, range(4, 6))):
                o = claim(pe, ("cO", g, c))
                for j in js:
                    ins = turn(o[0:27, (j - js[0]) * P:(j - js[0] + 1) * P], cgo[:, j, :])
                filled(ins, ("cO", g, c))
            pe.wait_ge(S["xs_ready"], 6 * (g + 1))
            o = claim(pe, ("bt", g, 0))
            for tt in range(SMP):
                ins = turn(o[:, tt * P:(tt + 1) * P], bcT[:, 0, tt * P:(tt + 1) * P])
            filled(ins, ("bt", g, 0))
            o = claim(pe, ("bt", g, 1))
            filled(turn(o[:, 0:P], bcT[:, 0, TP:T]), ("bt", g, 1))
            for tt in range(NT):
                tok = slice(tt * P, (tt + 1) * P)
                cum = (cum_p if tt < SMP else cum_s)[:]
                o = claim(pe, ("xt", g, tt))
                for j in range(4):
                    ins = turn(o[:, j * P:(j + 1) * P], xsT[:, j, tok])
                filled(ins, ("xt", g, tt))
                o = claim(pe, ("cb", g, tt))
                filled(mm(o[:, 0:P], bcT[:, 0, tok], bcT[:, 1, tok], start=True, stop=True), ("cb", g, tt))
                for i in range(2):
                    o = claim(pe, ("sg", g, tt, i))
                    for h in range(4):
                        hd = HG * g + 4 * i + h
                        ins = mm(o[:, h * P:(h + 1) * P], av[:, tt, hd:hd + 1].broadcast_to([P, P]), cum,
                                 start=True, stop=True)
                    filled(ins, ("sg", g, tt, i))
                o = claim(pe, ("eb", g, tt))
                for h in range(HG):
                    hd = HG * g + h
                    ins = mm(o[HP * (h % 2):HP * (h % 2) + HP, (h // 2) * P:(h // 2 + 1) * P],
                             av[:, tt, hd:hd + 1].broadcast_to([P, HP]), cum, start=True, stop=True)
                filled(ins, ("eb", g, tt))
                if 0 < tt < SMP:
                    wait_read(pe, ("st", g, tt - 1))
                    o = claim(pe, ("yi", g, tt))
                    for j in range(4):
                        ins = mm(o[:, j * P:(j + 1) * P], stT[:, j * P:(j + 1) * P], bcT[:, 1, tok], start=True, stop=True)
                    filled(ins, ("yi", g, tt))
                wait_read(pe, ("xt", g, tt))
                if tt < SMP:
                    wait_read(pe, ("bt", g, 1))
                    o = claim(pe, ("st", g, tt))
                    filled(mm(o, btm[:, tt, :], xw[:, tt % 2, :], start=True, stop=True), ("st", g, tt))
                o = claim(pe, ("yo", g, tt))
                for i in range(2):
                    pe.wait_ge(S["mt_ready"], 2 * (NT * g + tt) + i + 1)
                    m = mt[:, (2 * (NT * g + tt) + i) % 3, :]
                    for h in range(4 * i, 4 * i + 4):
                        ins = mm(o[HP * (h % 2):HP * (h % 2) + HP, (h // 2) * P:(h // 2 + 1) * P],
                                 xdt[:, tt % 2, HP * h:HP * (h + 1)], m[:, (h % 4) * P:(h % 4 + 1) * P],
                                 start=True, stop=True)
                filled(ins, ("yo", g, tt))
            wait_read(pe, ("st", g, SMP - 1))
            o = claim(pe, ("so", g))
            for j in range(4):
                ins = turn(o[:, j * P:(j + 1) * P], stT[:, j * P:(j + 1) * P])
            filled(ins, ("so", g))
            pe.wait_ge(S["bms_ready"], g + 1)
            for j in range(4):
                u = 4 * g + j
                pe.wait_ge(pair["st0_loaded"][u % 2], 16 * (u // 2 + 1))
                for i in range(2):
                    o = claim(pe, ("s0", g, j, i))
                    for b in range(4):
                        ins = turn(o[:, b * P:(b + 1) * P], st0[:, u % 2, 4 * i + b, :])
                    filled(ins, ("s0", g, j, i))
                for i in range(2):
                    o = claim(pe, ("sn", g, j, i))
                    filled(mm(o, xw[:, 0, j * P:(j + 1) * P], bms[:, 4 * i:4 * i + 4, :].rearrange("p b n -> p (b n)"),
                              start=True, stop=True), ("sn", g, j, i))
                wait_read(pe, ("s0", g, j, 1))
                o = claim(pe, ("ys", g, j))
                for b in range(SB):
                    ins = mm(o[:, b * SQ:(b + 1) * SQ], s0T[:, b, :], bcT[:, 1, TP + b * SQ:TP + (b + 1) * SQ],
                             start=True, stop=True)
                filled(ins, ("ys", g, j))
            pe.wait_ge(S["y_squares"], g + 1)
            for i, (a, b) in enumerate(((0, TP), (TP, T))):
                o = claim(pe, ("ss", g, i))
                for j in range(4):
                    ins = mm(o[:, 0:b - a], ones[:], zT[:, j, a:b], start=j == 0, stop=j == 3)
                filled(ins, ("ss", g, i))

        def attention_pe(pe, turn):
            mm = nc.tensor.matmul
            pe.wait_ge(S["q_back"], 16)
            pe.wait_ge(S["bias_ready"], 4)
            for i in range(SMP):
                n = P * (i + 1)
                for h in range(AH + 1):
                    if h < AH:
                        t, g = h % AR, h // AR
                        o = claim(pe, ("s", i, h))
                        filled(mm(o[:, 0:n], oT[HD * g:HD * (g + 1), t, i * P:(i + 1) * P], kT[HD * g:HD * (g + 1), 0:n],
                                  start=True, stop=True), ("s", i, h))
                    if h > 0:
                        u = AH * i + h - 1
                        t, g = (h - 1) % AR, (h - 1) // AR
                        pe.wait_ge(S["at_exp"], u + 1)
                        o = claim(pe, ("pT", i, h - 1))
                        for c in range(i + 1):
                            ins = turn(o[:, c * P:(c + 1) * P], sm[:, u % 2, c * P:(c + 1) * P])
                        filled(ins, ("pT", i, h - 1))
                        if t == 0:
                            oo = claim(pe, ("o", i, g))
                        wait_read(pe, ("pT", i, h - 1))
                        for c in range(i + 1):
                            ins = mm(oo[:, t * HD:(t + 1) * HD], pT[:, u % 2, c * P:(c + 1) * P],
                                     kvtm[:, c, SV + g * HD:SV + (g + 1) * HD], start=c == 0, stop=c == i)
                        if t == AR - 1:
                            filled(ins, ("o", i, g))
                wait_read(pe, ("o", i, 1))
                for c in range(2):
                    o = claim(pe, ("oT", i, c))
                    for t in range(4):
                        ins = turn(o[:, t * P:(t + 1) * P], otm[:, (4 * c + t) * P:(4 * c + t + 1) * P])
                    filled(ins, ("oT", i, c))
            for s in range(SB):
                pe.wait_ge(pair["kb_loaded"][s % 2], 16 * (s // 2 + 1))
                for c in range(2):
                    o = claim(pe, ("kc", s, c))
                    for j in range(4):
                        ins = turn(o[:, j * P:(j + 1) * P], kb[:, s % 2, 4 * c + j, :])
                    filled(ins, ("kc", s, c))
                wait_read(pe, ("kc", s, 0))
                wait_read(pe, ("kc", s, 1))
                for g in range(AKV):
                    claim(pe, ("ds", s, g))
                    o = bank(("ds", s, g), 3)[:, 0:KEYS]
                    rows = slice(HD * g, HD * (g + 1))
                    for c in range(3):
                        a, b = c * 512, min((c + 1) * 512, KEYS)
                        rhs = kcT[rows, s % 2, a:b] if c < 2 else kT[rows, TP + s * SQ:TP + (s + 1) * SQ]
                        mm(o[:, a:b], rsel[:, s, :], bias_s[:, a:b], start=True, stop=False)
                        ins = mm(o[:, a:b], qs[rows, s].rearrange("d t q -> d (t q)"), rhs, start=False, stop=True)
                    filled(ins, ("ds", s, g))
                pe.wait_ge(pair["vb_loaded"][s % 2], 16 * (s // 2 + 1))
                for g in range(AKV):
                    u = AKV * s + g
                    wait_read(pe, ("ds", s, g))
                    for c in range(3):
                        o = claim(pe, ("pt", s, g, c))
                        if c < 2:
                            pj = pexp[:, u % 2, 0:PAST].rearrange("p (k j) -> p j k", j=KJ)
                            for j in range(4):
                                ins = turn(o[:, j * P:(j + 1) * P], pj[:, 4 * c + j, :])
                        else:
                            ins = turn(o[0:SQ, 0:P], pexp[:, u % 2, PAST:KEYS])
                        filled(ins, ("pt", s, g, c))
                o = claim(pe, ("do", s))
                for g in range(AKV):
                    u = AKV * s + g
                    for c in (0, 2):
                        wait_read(pe, ("pt", s, g, c))
                    for j in range(KJ):
                        mm(o[:, g * HD:(g + 1) * HD], ptS[:, u % 2, j, :], vb[:, s % 2, j, g * HD:(g + 1) * HD],
                           start=j == 0, stop=False)
                    if s == 0 and g == 0:
                        pe.wait_ge(S["vnew_loaded"], 16 * SB)
                    ins = mm(o[:, g * HD:(g + 1) * HD], ptN[0:SQ, u % 2, :], vnew[0:SQ, s, g * HD:(g + 1) * HD],
                             start=False, stop=True)
                filled(ins, ("do", s))
                wait_read(pe, ("do", s))
                o = claim(pe, ("dT", s))
                filled(turn(o[:, 0:P], ob[:, s % 2, :]), ("dT", s))

        @block.tensor
        def _(pe):
            mm = nc.tensor.matmul

            def product(out, chunk, m0, m, rhs, n, ks=KD, first=True, last=True):
                for k in range(ks):
                    ins = mm(out, chunk[:, k, m0:m0 + m], rhs(k), start=first and k == 0, stop=last and k == ks - 1)
                return ins

            def turn(out, in_, rows=P):
                return nc.tensor.transpose(out, in_, ident[0:rows, 0:rows])

            prompt = lambda k: hT[:, k, 0:TP]
            sample = lambda k: hT[:, k, TP:T]

            pe.wait_ge(consts, 1)
            pe.wait_ge(params_loaded, 16 * 5)
            o = claim(pe, ("par", 0))
            filled(turn(o[:, 0:P], par[:, 0, :]), ("par", 0))
            o = claim(pe, ("par", 1))
            filled(turn(o[:, 0:24], par[0:24, 1, :], 24), ("par", 1))
            for tt in range(NT):
                pe.wait_ge(S["x_scaled"], tt + 1)
                for c in range(2):
                    o = claim(pe, ("hT", tt, c))
                    for k in range(4):
                        ins = turn(o[:, k * P:(k + 1) * P], xtm[:, tt, (4 * c + k) * P:(4 * c + k + 1) * P])
                    filled(ins, ("hT", tt, c))
            wait_read(pe, ("hT", NT - 1, 1))
            w = wait_chunk(pe, ("small",))
            for tt in range(NT):
                o = claim(pe, ("kv", tt))
                for k in range(KD):
                    ins = mm(o[:, 0:SW], hT[:, k, tt * P:(tt + 1) * P], w[:, k, 0:SW], start=k == 0, stop=k == KD - 1)
                filled(ins, ("kv", tt))
            for c in range(2):
                w = wait_chunk(pe, ("wq", c))
                for t in range(4):
                    o = claim(pe, ("q", 4 * c + t))
                    filled(product(o, w, t * P, P, prompt, TP), ("q", 4 * c + t))
                o = claim(pe, ("qS", c))
                for t in range(4):
                    ins = product(o[:, t * P:(t + 1) * P], w, t * P, P, sample, P)
                filled(ins, ("qS", c))
            w = wait_chunk(pe, ("wqi",))
            for t in range(4):
                o = claim(pe, ("qi", t))
                filled(product(o, w, t * P, P, prompt, TP), ("qi", t))
            o = claim(pe, ("qiS",))
            for t in range(4):
                ins = product(o[:, t * P:(t + 1) * P], w, t * P, P, sample, P)
            filled(ins, ("qiS",))
            wait_read(pe, ("kv", NT - 1))
            o = claim(pe, ("kT", 0))
            for tt in range(SMP):
                ins = turn(o[:, tt * P:(tt + 1) * P], kvtm[:, tt, SK:SK + P])
            filled(ins, ("kT", 0))
            o = claim(pe, ("kT", 1))
            filled(turn(o[:, 0:P], kvtm[:, SMP, SK:SK + P]), ("kT", 1))
            o = claim(pe, ("kT", 2))
            for tt in range(SMP):
                ins = turn(o[0:HD, tt * P:(tt + 1) * P], kvtm[:, tt, SKI:SKI + IDIM])
            filled(ins, ("kT", 2))
            o = claim(pe, ("kT", 3))
            filled(turn(o[0:HD, 0:P], kvtm[:, SMP, SKI:SKI + IDIM]), ("kT", 3))
            wait_read(pe, ("kT", 3))
            for i in range(1, 4):
                for h in range(IH):
                    o = claim(pe, ("pd", i, h))
                    filled(mm(o[:, 0:P * (i + 1)], qiT[0:HD, h, i * P:(i + 1) * P], kiT[0:HD, 0:P * (i + 1)],
                              start=True, stop=True), ("pd", i, h))
            pe.wait_ge(S["wl_ready"], 1)
            o = claim(pe, ("wc",))
            filled(mm(o[:, 0:SB], wl, stream[:], start=True, stop=True), ("wc",))
            di = [claim(pe, ("di", i)) for i in range(3)]
            pe.wait_ge(S["wsel_ready"], 1)
            for s in range(SB + 2):
                if s < SB:
                    pe.wait_ge(pair["kx_loaded"][s % 2], 16 * (s // 2 + 1))
                    for c in range(2):
                        o = claim(pe, ("kx", s, c))
                        for j in range(4):
                            ins = turn(o[0:IDIM, j * P:(j + 1) * P], kx_in[:, s % 2, 4 * c + j, :])
                        filled(ins, ("kx", s, c))
                if 1 <= s <= SB:
                    b = s - 1
                    wait_read(pe, ("kx", b, 0))
                    wait_read(pe, ("kx", b, 1))
                    for c in range(3):
                        o = claim(pe, ("dd", b, c))
                        rhs = kxT[0:IDIM, b % 2, c * 512:(c + 1) * 512] if c < 2 else \
                            kiT[0:IDIM, TP + b * SQ:TP + (b + 1) * SQ]
                        filled(mm(o[:, 0:rhs.shape[1]], qis[0:HD, b].rearrange("d h q -> d (h q)"), rhs,
                                  start=True, stop=True), ("dd", b, c))
                if s >= 2:
                    b = s - 2
                    wait_read(pe, ("dd", b, 2))
                    for c in range(3):
                        w_ = 512 if c < 2 else SQ
                        ins = mm(di[c][:, 0:w_], wsel[:, b, :], rel[:, b % 2, c * 512:c * 512 + w_],
                                 start=b == 0, stop=b == SB - 1, skip_group_check=True)
                        if b == SB - 1:
                            filled(ins, ("di", c))
            pe.wait_ge(S["a_ready"], 1)
            for tt in range(NT):
                o = claim(pe, ("ac", tt))
                filled(mm(o[:, 0:HEADS], (cum_p if tt < SMP else cum_s)[:], av[:, tt, :], start=True, stop=True), ("ac", tt))
                o = claim(pe, ("ae", tt))
                filled(mm(o[:, 0:HEADS], (ones if tt < SMP else same)[:], av[:, tt, :], start=True, stop=True), ("ae", tt))
            for g in range(GROUPS):
                ssd_pe(pe, g, product, turn, prompt, sample)
            attention_pe(pe, turn)
            for n in range(2):
                for what in ("ga", "gb", "a", "b"):
                    if what[0] == "g":
                        ws = [wait_chunk(pe, ("w" + what, n))]
                        rp, rs = [prompt], [sample]
                    elif what == "a":
                        ws = [wait_chunk(pe, ("wso", n, c)) for c in range(2)]
                        rp = [lambda k: yz[:, k, 0:TP], lambda k: yz[:, 8 + k, 0:TP]]
                        rs = [lambda k: yz[:, k, TP:T], lambda k: yz[:, 8 + k, TP:T]]
                        pe.wait_ge(S["y_back"], 16)
                    else:
                        ws = [wait_chunk(pe, ("wao", n))]
                        rp, rs = [lambda k: oT[:, k, 0:TP]], [lambda k: oT[:, k, TP:T]]
                        wait_read(pe, ("dT", SB - 1))
                    for j in range(4):
                        o = claim(pe, (what, n, j))
                        for i, w in enumerate(ws):
                            ins = product(o, w, j * P, P, rp[i], TP, first=i == 0, last=i == len(ws) - 1)
                        filled(ins, (what, n, j))
                    o = claim(pe, (what + "S", n))
                    for j in range(4):
                        for i, w in enumerate(ws):
                            ins = product(o[:, j * P:(j + 1) * P], w, j * P, P, rs[i], P, first=i == 0,
                                          last=i == len(ws) - 1)
                    filled(ins, (what + "S", n))
            ws = [wait_chunk(pe, ("wo", n)) for n in range(2)]
            pe.wait_ge(S["m_ready"], 2)
            for tt in range(NT):
                for n in range(2):
                    o = claim(pe, ("x1", tt, n))
                    for k in range(KD):
                        ins = mm(o, mrg[:, k, tt * P:(tt + 1) * P], ws[n][:, k, :], start=k == 0, stop=k == KD - 1)
                    filled(ins, ("x1", tt, n))
            for tt in range(NT):
                pe.wait_ge(S["hx_scaled"], tt + 1)
                for c in range(2):
                    o = claim(pe, ("h2", tt, c))
                    for k in range(4):
                        ins = turn(o[:, k * P:(k + 1) * P], xn[:, tt, (4 * c + k) * P:(4 * c + k + 1) * P])
                    filled(ins, ("h2", tt, c))
            pe.wait_ge(S["router_loaded"], 32)
            for tt in range(NT):
                wait_read(pe, ("h2", tt, 1))
                o = claim(pe, ("rt", tt))
                for k in range(KD):
                    ins = mm(o[:, 0:MG + NE], h2T[:, k, tt * P:(tt + 1) * P], wr[:, k, :], start=k == 0, stop=k == KD - 1)
                filled(ins, ("rt", tt))
            for e in range(NE):
                w = wait_chunk(pe, ("w13", e))
                oS = claim(pe, ("heS", e))
                for j in range(4):
                    o = claim(pe, ("he", e, j))
                    filled(product(o, w, j * P, P, lambda k: h2T[:, k, 0:TP], TP), ("he", e, j))
                for j in range(4):
                    ins = product(oS[:, j * P:(j + 1) * P], w, j * P, P, lambda k: h2T[:, k, TP:T], P)
                filled(ins, ("heS", e))
                w = wait_chunk(pe, ("w2", e)).rearrange("p k n -> p (k n)")[:, 0:2 * D].rearrange("p (k n) -> p k n", k=2)
                wait_read(pe, ("heS", e))
                for tt in range(NT):
                    for n in range(2):
                        o = claim(pe, ("y", e, tt, n))
                        for k in range(2):
                            ins = mm(o, heT[:, e % 2, k, tt * P:(tt + 1) * P], w[:, k, n * 512:(n + 1) * 512],
                                     start=k == 0, stop=k == 1)
                        filled(ins, ("y", e, tt, n))

        def ssd_act(act, g, fn, copy):
            if g:
                act.wait_ge(S["y_gated"], g)
                wait_full(act, ("ss", g - 1, 1))
            copy(("cT", g), cst, bank(("cT", g))[:, 0:144].rearrange("p (j r) -> p j r", r=24))
            for j in range(7):
                if j < 6:
                    u = 6 * g + j
                    r = raw[:, u % 2, :]
                    rsm = r[:, 515:667].rearrange("p (b q) -> p b q", q=19)
                    if u < 2:
                        act.wait_ge(S["raw_zeroed"], 1)
                    else:
                        act.wait_ge(S["conv_done"], u - 1)
                        act.wait_ge(S["gathered"], u - 1)
                    c = j // 4
                    copy(("xbc", g, j), r[:, 3:515], bank(("xbc", g, j)))
                    wait_full(act, ("xbcS", g, c))
                    ins = fn(rsm[:, :, 3:19], bank(("xbcS", g, c))[:, (j - 4 * c) * P:(j - 4 * c + 1) * P]
                             .rearrange("p (b q) -> p b q", q=SQ), ACT.Copy)
                    if j in (3, 5):
                        release(ins, ("xbcS", g, c))
                    wait_read(act, ("cT", g))
                    fn(rsm[:, :, 0:3], cst[:, j, :].rearrange("p (b r) -> p b r", r=3), ACT.Copy) \
                        .then_inc(S["raw_ready"], 1)
                if j > 0:
                    u = 6 * g + j - 1
                    ct = 4 * g + j - 1 if j < 5 else 16 + g if j == 5 else 20 + g
                    dst = xsT[:, j - 1, :] if j < 5 else bcT[:, j - 5, :]
                    act.wait_ge(S["conv_done"], u + 1)
                    fn(dst[:, 0:TP], acc[:, 0, 0:TP], ACT.Silu, bias=cb_col[:, ct:ct + 1])
                    fn(dst[:, TP:T].rearrange("p (b q) -> p b q", q=SQ),
                       acc[:, 0, 512:664].rearrange("p (b q) -> p b q", q=19)[:, :, 3:19], ACT.Silu,
                       bias=cb_col[:, ct:ct + 1]).then_inc(S["xs_ready"], 1)
            for j in range(4):
                wait_full(act, ("z", g, j))
                release(fn(zT[:, j, 0:TP], bank(("z", g, j)), ACT.Silu), ("z", g, j))
            wait_full(act, ("zS", g))
            release(fn(zT[:, :, TP:T], bank(("zS", g)).rearrange("p (j q) -> p j q", j=4), ACT.Silu), ("zS", g))
            if g:
                act.wait_ge(S["crow_written"], 96 * g)
            for c, w in ((0, 4), (1, 2)):
                copy(("cO", g, c), crow[0:27, 4 * c:4 * c + w, :],
                     bank(("cO", g, c))[0:27, 0:w * P].rearrange("p (j n) -> p j n", n=P))
            if g:
                act.wait_ge(S["bms_ready"], g)
            copy(("bt", g, 0), btm[:, 0:4, :], bank(("bt", g, 0)).rearrange("p (t n) -> p t n", n=P))
            copy(("bt", g, 1), btm[:, SMP, :], bank(("bt", g, 1))[:, 0:P])
            for tt in range(NT):
                k = NT * g + tt
                if k >= 2:
                    act.wait_ge(S["mt_ready"], 2 * (k - 1))
                copy(("cb", g, tt), cbs[:, k % 2, :], bank(("cb", g, tt))[:, 0:P])
                for i in range(2):
                    u = 2 * k + i
                    wait_read(act, ("sg", g, tt, i))
                    m = mt[:, u % 3, :]
                    for h in range(4):
                        hd = HG * g + 4 * i + h
                        ins = fn(m[:, h * P:(h + 1) * P], m[:, h * P:(h + 1) * P], ACT.Exp, bias=nac[:, tt, hd:hd + 1])
                    ins.then_inc(S["mt_exp"], 1)
                wait_full(act, ("eb", g, tt))
                if tt >= 2:
                    wait_read(act, ("yo", g, tt - 2))
                elif g:
                    wait_read(act, ("yo", g - 1, tt + 3))
                release(fn(ebs[:, k % 2, :], bank(("eb", g, tt)), ACT.Exp), ("eb", g, tt))
            if g:
                act.wait_ge(S["sout_written"], 16 * g)
            copy(("so", g), sout, bank(("so", g)))
            for j in range(4):
                for i in range(2):
                    if (g or j) and i == 0:
                        wait_full(act, ("ys", g, j - 1) if j else ("ys", g - 1, 3))
                    copy(("s0", g, j, i), s0T[:, 4 * i:4 * i + 4, :],
                         bank(("s0", g, j, i)).rearrange("p (b q) -> p b q", b=4))
            act.wait_ge(S["y_gated"], g + 1)
            fn(zT, yb[:, g % 2, :, :], ACT.Square).then_inc(S["y_squares"], 1)
            act.wait_ge(S["y_squares"], g + 1)
            for j in range(4):
                ins = fn(yb[:, g % 2, j, :], yb[:, g % 2, j, :], ACT.Copy, scale=gssm[:, 4 * g + j:4 * g + j + 1])
            ins.then_inc(S["y_gained"], 1)

        @block.scalar
        def _(act):
            n = [0]

            def link(ins):
                n[0] += 1
                ins.then_inc(act_chain, 1)
                act.wait_ge(act_chain, n[0])

            fn = nc.scalar.activation

            def copy(key, out, in_):
                wait_full(act, key)
                release(fn(out, in_, ACT.Copy), key)

            copy(("par", 0), pc[:, 0, :], bank(("par", 0))[:, 0:P])
            copy(("par", 1), pc[:, 1, 0:24], bank(("par", 1))[:, 0:24])
            act.wait_ge(rows_loaded, 16 * 5)
            fn(a_row[:], a_row[:], ACT.Exp).then_inc(S["a_row_ready"], 1)
            for tt in range(NT):
                act.wait_ge(x_loaded[tt], 16)
                if tt:
                    act.wait_ge(S["x_squares"], tt)
                fn(junk, xtm[:, tt, :], ACT.Square, accum_out=ssq[:, 0, tt:tt + 1]).then_inc(S["x_squares"], 1)
            act.wait_ge(S["x_var"], 1)
            fn(ssq[:, 1, 0:NT], ssq[:, 0, 0:NT], ACT.Sqrt).then_inc(S["x_std"], 1)
            for tt in range(NT):
                copy(("kv", tt), kvtm[:, tt, :], bank(("kv", tt))[:, 0:SW])
            for c in range(2):
                for t in range(4 * c, 4 * c + 4):
                    copy(("q", t), oT[:, t, 0:TP], bank(("q", t)))
                wait_full(act, ("qS", c))
                for t in range(4):
                    ins = fn(qs[:, :, 4 * c + t, :],
                             bank(("qS", c))[:, t * P:(t + 1) * P].rearrange("p (b q) -> p b q", q=SQ), ACT.Copy)
                release(ins, ("qS", c))
            for t in range(4):
                wait_full(act, ("qi", t))
                fn(qiT[0:HD, 2 * t, :], bank(("qi", t))[0:HD, :], ACT.Copy)
                release(fn(qiT[0:HD, 2 * t + 1, :], bank(("qi", t))[HD:P, :], ACT.Copy), ("qi", t))
            wait_full(act, ("qiS",))
            for h in range(IH):
                ins = fn(qis[0:HD, :, h, :],
                         bank(("qiS",))[HD * (h % 2):HD * (h % 2) + HD, (h // 2) * P:(h // 2 + 1) * P]
                         .rearrange("p (b q) -> p b q", q=SQ), ACT.Copy)
            release(ins, ("qiS",))
            copy(("kT", 0), kT[:, 0:TP], bank(("kT", 0)))
            copy(("kT", 1), kT[:, TP:T], bank(("kT", 1))[:, 0:P])
            copy(("kT", 2), kiT[0:HD, 0:TP], bank(("kT", 2))[0:HD, :])
            copy(("kT", 3), kiT[0:HD, TP:T], bank(("kT", 3))[0:HD, 0:P])
            for i in range(1, 4):
                for h in range(IH):
                    u, w = IH * (i - 1) + h, P * (i + 1)
                    wait_full(act, ("pd", i, h))
                    if u >= 2:
                        act.wait_ge(S["rel_used"], u - 1)
                    release(fn(rel[:, u % 2, 0:w], bank(("pd", i, h))[:, 0:w], ACT.Relu), ("pd", i, h))
            copy(("wc",), wcol, bank(("wc",))[:, 0:SB])
            act.wait_ge(S["rel_used"], 3 * IH)
            for s in range(SB + 1):
                if s < SB:
                    for c in range(2):
                        copy(("kx", s, c), kxT[0:IDIM, s % 2, :].rearrange("d (p j) -> d j p", j=KJ)[:, 4 * c:4 * c + 4, :],
                             bank(("kx", s, c))[0:IDIM, :].rearrange("d (j p) -> d j p", j=4))
                if s >= 1:
                    b = s - 1
                    for c in range(3):
                        w = 512 if c < 2 else SQ
                        wait_full(act, ("dd", b, c))
                        release(fn(rel[:, b % 2, 512 * c:512 * c + w], bank(("dd", b, c))[:, 0:w], ACT.Relu), ("dd", b, c))
            act.wait_ge(S["dt_exp"], 1)
            fn(w2v, w2v, ACT.Exp, scale=-1.0).then_inc(S["a_exp"], 1)
            for tt in range(NT):
                wait_read(act, ("ae", tt), 1)
                release(fn(expae[:, tt, :], bank(("ae", tt))[:, 0:HEADS], ACT.Exp), ("ae", tt))
            act.wait_ge(S["ae_ready"], 1)
            fn(w2v, w2v, ACT.Exp).then_inc(S["a_exp"], 1)
            for g in range(GROUPS):
                ssd_act(act, g, fn, copy)
            for i in range(SMP):
                w = P * (i + 1)
                for h in range(AH + 1):
                    if h < AH:
                        u = AH * i + h
                        wait_read(act, ("s", i, h))
                        fn(sm[:, u % 2, 0:w], sm[:, u % 2, 0:w], ACT.Exp, bias=mx[:, i % 2, h:h + 1], scale=-1.0,
                           accum_out=rsum[:, i % 2, h:h + 1]).then_inc(S["at_exp"], 1)
                    if h > 0:
                        u = AH * i + h - 1
                        copy(("pT", i, h - 1), pT[:, u % 2, 0:w], bank(("pT", i, h - 1))[:, 0:w])
                for c in range(2):
                    copy(("oT", i, c), oT[:, 4 * c:4 * c + 4, i * P:(i + 1) * P],
                         bank(("oT", i, c)).rearrange("p (t q) -> p t q", t=4))
            for s in range(SB):
                copy(("kc", s, 1), kcT[:, s % 2, :].rearrange("d (p j) -> d j p", j=KJ)[:, 4:8, :],
                     bank(("kc", s, 1)).rearrange("d (j p) -> d j p", j=4))
                for g in range(AKV):
                    u = AKV * s + g
                    act.wait_ge(S["ds_nmax"], u + 1)
                    release(fn(pexp[:, u % 2, :], bank(("ds", s, g), 3)[:, 0:KEYS], ACT.Exp,
                               bias=mx[:, s % 2, 2 + g:3 + g], scale=ATT_SCALE,
                               accum_out=rsum[:, s % 2, g:g + 1]), ("ds", s, g))
                for g in range(AKV):
                    u = AKV * s + g
                    copy(("pt", s, g, 1), ptS[:, u % 2, 4:8, :], bank(("pt", s, g, 1)).rearrange("p (j q) -> p j q", j=4))
                    copy(("pt", s, g, 2), ptN[0:SQ, u % 2, :], bank(("pt", s, g, 2))[0:SQ, 0:P])
                copy(("dT", s), oT[:, :, TP + s * SQ:TP + (s + 1) * SQ],
                     bank(("dT", s))[:, 0:P].rearrange("p (t q) -> p t q", q=SQ))
            act.wait_ge(S["ss_var"], 1)
            fn(rt, rt, ACT.Sqrt).then_inc(S["ss_std"], 1)
            for m in range(2):
                for i, what in enumerate(("ga", "gb")):
                    if m:
                        wait_read(act, (("aS", "bS")[i], 0))
                    if m:
                        act.wait_ge(S["m_ready"], 1)
                    for j in range(4):
                        wait_full(act, (what, m, j))
                        release(fn(gate[:, i, j, 0:TP], bank((what, m, j)), ACT.Sigmoid), (what, m, j))
                    wait_full(act, (what + "S", m))
                    release(fn(gate[:, i, :, TP:T], bank((what + "S", m)).rearrange("p (j q) -> p j q", j=4),
                               ACT.Sigmoid), (what + "S", m))
            for tt in range(NT):
                wait_read(act, ("x1", tt, 1))
                fn(xn[:, tt, :], x1[:, tt, :], ACT.Square, accum_out=ssq[:, 2, tt:tt + 1]).then_inc(S["hx_squares"], 1)
            act.wait_ge(S["hx_var"], 1)
            fn(ssq[:, 3, 0:NT], ssq[:, 2, 0:NT], ACT.Sqrt).then_inc(S["hx_std"], 1)
            for i in range(2):
                act.wait_ge(S["r_exp_in"], i + 1)
                e = rc[2] if i == 0 else rs1[:, 4, :]
                fn(e, e, ACT.Exp).then_inc(S["r_exp"], 1)
            for e in range(NE):
                if e:
                    wait_read(act, ("heS", e - 1))
                for j in range(2):
                    wait_full(act, ("he", e, j))
                    release(fn(hsil[:, j, 0:TP], bank(("he", e, j)), ACT.Silu), ("he", e, j))
                wait_full(act, ("heS", e))
                release(fn(hsil[:, :, TP:T], bank(("heS", e))[:, 0:2 * P].rearrange("p (j q) -> p j q", j=2), ACT.Silu),
                        ("heS", e))
            for tt in range(NT):
                act.wait_ge(S["ysum_ready"], tt + 1)
                fn(xn[:, tt, :], ysum[:, tt, :], ACT.Square, accum_out=ssq[:, 4, tt:tt + 1]).then_inc(S["fx_squares"], 1)
            act.wait_ge(S["fx_var"], 1)
            fn(ssq[:, 5, 0:NT], ssq[:, 4, 0:NT], ACT.Sqrt).then_inc(S["fx_std"], 1)

        def ssd_dve(dve, g, link, over):
            tt_, ts_, stt = nc.vector.tensor_tensor, nc.vector.tensor_scalar, nc.vector.scalar_tensor_tensor
            heads = slice(HG * g, HG * (g + 1))
            y = yb[:, g % 2, :, :]
            for j in range(6):
                u = 6 * g + j
                ct = 4 * g + j if j < 4 else 16 + g if j == 4 else 20 + g
                dve.wait_ge(S["raw_ready"], u + 1)
                if u:
                    dve.wait_ge(S["xs_ready"], u)
                a, r = acc[:, 0, :], raw[:, u % 2, :]
                link(ts_(a, r[:, 0:664], cw_col[:, 0, ct:ct + 1], None, ALU.mult))
                for w in range(1, CW):
                    ins = stt(out=a, in0=r[:, w:w + 664], scalar=cw_col[:, w, ct:ct + 1], in1=a, op0=ALU.mult, op1=ALU.add)
                    if w < CW - 1:
                        link(ins)
                ins.then_inc(S["conv_done"], 1)
            for tt in range(NT):
                k = NT * g + tt
                wait_full(dve, ("xt", g, tt))
                if tt >= 2:
                    wait_full(dve, ("yo", g, tt - 2))
                elif tt == 0 and g:
                    wait_full(dve, ("ys", g - 1, 3))
                xp = bank(("xt", g, tt)).rearrange("p (h d) -> p h d", d=HP)
                tt_(xdt[:, tt % 2, :].rearrange("p (h d) -> p h d", d=HP), xp, over(dtv[:, tt, heads], HP), ALU.mult)
                release(tt_(xw[:, tt % 2, :].rearrange("p (h d) -> p h d", d=HP), xp, over(w2v[:, tt, heads], HP),
                            ALU.mult), ("xt", g, tt))
                neg = (neg_p if tt < SMP else neg_s)[:].rearrange("p (o l) -> p o l", o=1).broadcast_to([P, 4, P])
                for i in range(2):
                    u = 2 * k + i
                    wait_full(dve, ("sg", g, tt, i))
                    if u >= 3:
                        kk = (u - 3) // 2
                        wait_full(dve, ("yo", kk // NT, kk % NT))
                    release(tt_(mt[:, u % 3, :].rearrange("p (h l) -> p h l", h=4),
                                bank(("sg", g, tt, i)).rearrange("p (h l) -> p h l", h=4), neg, ALU.add), ("sg", g, tt, i))
                wait_read(dve, ("cb", g, tt))
                for i in range(2):
                    u = 2 * k + i
                    dve.wait_ge(S["mt_exp"], u + 1)
                    m = mt[:, u % 3, :].rearrange("p (h l) -> p h l", h=4)
                    tt_(m, m, cbs[:, k % 2, :].rearrange("p (o l) -> p o l", o=1).broadcast_to([P, 4, P]), ALU.mult) \
                        .then_inc(S["mt_ready"], 1)
                tok = slice(tt * P, (tt + 1) * P)
                if tt == 0:
                    if g == 0:
                        dve.wait_ge(S["q_spilled"], 16)
                    elif g >= 2:
                        dve.wait_ge(S["y_spilled"], 16 * (g - 1))
                yv = y[:, :, tok]
                if 0 < tt < SMP:
                    wait_full(dve, ("yi", g, tt))
                    wait_read(dve, ("eb", g, tt))
                    release(tt_(ytmp, bank(("yi", g, tt)), ebs[:, k % 2, :], ALU.mult), ("yi", g, tt))
                if tt < SMP:
                    wait_full(dve, ("st", g, tt))
                    if tt == 0:
                        ins = nc.vector.tensor_copy(stT, bank(("st", g, tt)))
                    else:
                        sv = stT.rearrange("p (h d) -> p h d", d=HP)
                        link(tt_(sv, sv, over(expae[:, tt, heads], HP), ALU.mult))
                        ins = tt_(stT, stT, bank(("st", g, tt)), ALU.add)
                    release(ins, ("st", g, tt))
                    wait_read(dve, ("st", g, tt))
                wait_full(dve, ("yo", g, tt))
                yo = bank(("yo", g, tt)).rearrange("p (j l) -> p j l", j=4)
                if 0 < tt < SMP:
                    wait_read(dve, ("yi", g, tt))
                    ins = tt_(yv, yo, ytmp.rearrange("p (j l) -> p j l", j=4), ALU.add)
                else:
                    ins = nc.vector.tensor_copy(yv, yo)
                release(ins, ("yo", g, tt))
            k = NT * g + SMP
            wait_read(dve, ("eb", g, SMP))
            wait_read(dve, ("yo", g, SMP))
            for j in range(4):
                u = 4 * g + j
                dec = ebs[:, k % 2, j * P:(j + 1) * P].rearrange("p (b q) -> p b q", q=SQ)[:, :, SQ - 1:SQ]
                for i in range(2):
                    wait_full(dve, ("sn", g, j, i))
                    sv = st0[:, u % 2, 4 * i:4 * i + 4, :]
                    link(tt_(sv, sv, dec[:, 4 * i:4 * i + 4, :].broadcast_to([P, 4, NS]), ALU.mult))
                    release(tt_(sv, sv, bank(("sn", g, j, i)).rearrange("p (b n) -> p b n", n=NS), ALU.add),
                            ("sn", g, j, i))
                wait_full(dve, ("ys", g, j))
                release(tt_(ytmp[:, 0:P], bank(("ys", g, j))[:, 0:P], ebs[:, k % 2, j * P:(j + 1) * P], ALU.mult),
                        ("ys", g, j))
                wait_read(dve, ("ys", g, j))
                link(tt_(y[:, j, TP:T], y[:, j, TP:T], ytmp[:, 0:P], ALU.add))
            for j in range(4):
                link(stt(out=y[:, j, :], in0=xsT[:, j, :], scalar=dcol[:, 4 * g + j:4 * g + j + 1], in1=y[:, j, :],
                         op0=ALU.mult, op1=ALU.add))
            wait_read(dve, ("zS", g))
            tt_(y, y, zT, ALU.mult).then_inc(S["y_gated"], 1)
            for i, (a, b) in enumerate(((0, TP), (TP, T))):
                wait_full(dve, ("ss", g, i))
                src = bank(("ss", g, i))[:, 0:b - a]
                if g == 0:
                    ins = nc.vector.tensor_copy(ssrow[:, a:b], src)
                else:
                    ins = tt_(ssrow[:, a:b], ssrow[:, a:b], src, ALU.add)
                release(ins, ("ss", g, i))
                wait_read(dve, ("ss", g, i))

        def attention_dve(dve, link, over):
            tt_, ts_ = nc.vector.tensor_tensor, nc.vector.tensor_scalar
            wait_full(dve, ("s", 0, 0))
            for i in range(SMP):
                w = P * (i + 1)
                bias = adm_att[:] if i == 0 else bias_p[i]
                for h in range(AH + 2):
                    if h < AH:
                        u = AH * i + h
                        wait_full(dve, ("s", i, h))
                        release(nc.vector.tensor_tensor_reduce(
                            out=sm[:, u % 2, 0:w], in0=bank(("s", i, h))[:, 0:w], in1=bias, scale=-ATT_SCALE, scalar=3.0e38,
                            op0=ALU.add, op1=ALU.min, accum_out=mx[:, i % 2, h:h + 1]), ("s", i, h))
                    if h in (AR + 1, AH + 1):
                        g = (h - 2) // AR
                        dve.wait_ge(S["at_exp"], AH * i + AR * (g + 1))
                        hs = slice(AR * g, AR * (g + 1))
                        link(nc.vector.reciprocal(rinv[:, i % 2, hs], rsum[:, i % 2, hs]))
                        wait_full(dve, ("o", i, g))
                        release(tt_(otm.rearrange("p (t g d) -> p g t d", g=AKV, d=HD)[:, g, :, :],
                                    bank(("o", i, g)).rearrange("p (t d) -> p t d", d=HD), over(rinv[:, i % 2, hs], HD),
                                    ALU.mult), ("o", i, g))
            for s in range(SB):
                wait_full(dve, ("kc", s, 0))
                release(nc.vector.tensor_copy(kcT[:, s % 2, :].rearrange("d (p j) -> d j p", j=KJ)[:, 0:4, :],
                                              bank(("kc", s, 0)).rearrange("d (j p) -> d j p", j=4)), ("kc", s, 0))
                for g in range(AKV):
                    wait_full(dve, ("ds", s, g))
                    link(nc.vector.tensor_reduce(mx[:, s % 2, g:g + 1], bank(("ds", s, g), 3)[:, 0:KEYS], AX.X, ALU.max))
                    ts_(mx[:, s % 2, 2 + g:3 + g], mx[:, s % 2, g:g + 1], -ATT_SCALE, None, ALU.mult) \
                        .then_inc(S["ds_nmax"], 1)
                for g in range(AKV):
                    u = AKV * s + g
                    key = ("pt", s, g, 0)
                    wait_full(dve, key)
                    release(nc.vector.tensor_copy(ptS[:, u % 2, 0:4, :], bank(key).rearrange("p (j q) -> p j q", j=4)), key)
                wait_read(dve, ("ds", s, 1))
                link(nc.vector.reciprocal(rinv[:, s % 2, 0:2], rsum[:, s % 2, 0:2]))
                wait_full(dve, ("do", s))
                release(tt_(ob[:, s % 2, :].rearrange("p (g d) -> p g d", g=AKV),
                            bank(("do", s))[:, 0:P].rearrange("p (g d) -> p g d", g=AKV), over(rinv[:, s % 2, 0:2], HD),
                            ALU.mult), ("do", s))

        def route(dve, link, over):
            tt_, ts_, stt, red = (nc.vector.tensor_tensor, nc.vector.tensor_scalar, nc.vector.scalar_tensor_tensor,
                                  nc.vector.tensor_reduce)
            gl = lg[:, :, 0:MG]
            el = lg[:, :, MG:].rearrange("p t (g e) -> p t g e", g=MG)
            gmax, gsum, m1, m2, ex, den, top_ = (rs1[:, i, :] for i in range(7))

            def first(mask, vals, best, pr, k):
                link(tt_(mask, vals, over(best, k), ALU.is_equal))
                link(tt_(mask, mask, pr.rearrange("p (o e) -> p o e", o=1).broadcast_to([P, NT, k]), ALU.mult))
                link(red(top_, mask, AX.X, ALU.max))
                link(tt_(mask, mask, over(top_, k), ALU.is_equal))

            link(red(gmax, gl, AX.X, ALU.max))
            tt_(rc[2], gl, over(gmax, MG), ALU.subtract).then_inc(S["r_exp_in"], 1)
            first(rc[0], gl, gmax, prio[:, ME - MG:ME], MG)
            for gi in range(MG):
                sel = rc[0][:, :, gi:gi + 1].broadcast_to([P, NT, ME])
                link(tt_(rb[1], el[:, :, gi, :], sel, ALU.mult))
                link(nc.vector.tensor_copy(rb[0], rb[1]) if gi == 0 else tt_(rb[0], rb[0], rb[1], ALU.add))
            link(red(m1, rb[0], AX.X, ALU.max))
            first(rb[2], rb[0], m1, prio[:], ME)
            link(stt(out=rb[3], in0=rb[2], scalar=NEG, in1=rb[0], op0=ALU.mult, op1=ALU.add))
            link(red(m2, rb[3], AX.X, ALU.max))
            first(rb[4], rb[3], m2, prio[:], ME)
            tt_(ex, m2, m1, ALU.subtract).then_inc(S["r_exp_in"], 1)
            dve.wait_ge(S["r_exp"], 2)
            link(red(gsum, rc[2], AX.X, ALU.add))
            link(ts_(den, ex, 1.0, None, ALU.add))
            link(tt_(den, den, gsum, ALU.mult))
            link(nc.vector.reciprocal(den, den))
            link(tt_(ex, ex, den, ALU.mult))
            link(tt_(rb[2], rb[2], over(den, ME), ALU.mult))
            link(tt_(rb[4], rb[4], over(ex, ME), ALU.mult))
            link(tt_(rb[2], rb[2], rb[4], ALU.add))
            for gi in range(MG):
                link(tt_(comb[:, :, gi, :], rb[2], rc[0][:, :, gi:gi + 1].broadcast_to([P, NT, ME]), ALU.mult))

        @block.vector
        def _(dve):
            n = [0]
            tt_ = nc.vector.tensor_tensor
            ts_ = nc.vector.tensor_scalar
            stt = nc.vector.scalar_tensor_tensor

            def link(ins):
                n[0] += 1
                ins.then_inc(dve_chain, 1)
                dve.wait_ge(dve_chain, n[0])

            def newton(r, v, tmp):
                link(tt_(tmp, r, r, ALU.mult))
                link(tt_(tmp, tmp, v, ALU.mult))
                link(ts_(tmp, tmp, -0.5, 1.5, ALU.mult, ALU.add))
                link(tt_(r, r, tmp, ALU.mult))

            def over(ap, k):
                return ap.rearrange("p (n o) -> p n o", o=1).broadcast_to([P, ap.shape[1], k])

            dve.wait_ge(consts, 1)
            link(nc.vector.tensor_reduce(qsel[:], ident[:].rearrange("p (b q) -> p q b", q=SQ), AX.X, ALU.add))
            for b in range(SB):
                link(ts_(rsel[:, b, :].rearrange("p (r q) -> p r q", q=SQ),
                         qsel[:].rearrange("p (o q) -> p o q", o=1).broadcast_to([P, KD, SQ]),
                         stream[:, b:b + 1], None, ALU.mult))
            dve.wait_ge(S["a_row_ready"], 1)
            link(ts_(a_row[:], a_row[:], -1.0, None, ALU.mult))
            pairs = dsk_row[:].rearrange("p (j i) -> p i j", i=2)
            link(nc.vector.tensor_copy(dcol[0:HP, :], pairs[0:HP, 0, :]))
            link(nc.vector.tensor_copy(dcol[HP:P, :], pairs[HP:P, 1, :]))
            dve.wait_ge(S["x_squares"], NT)
            ts_(ssq[:, 0, 0:NT], ssq[:, 0, 0:NT], 1.0 / D, EPS, ALU.mult, ALU.add).then_inc(S["x_var"], 1)
            dve.wait_ge(S["x_std"], 1)
            link(nc.vector.reciprocal(ssq[:, 1, 0:NT], ssq[:, 1, 0:NT]))
            newton(ssq[:, 1, 0:NT], ssq[:, 0, 0:NT], ssq[:, 2, 0:NT])
            wait_read(dve, ("par", 1))
            for tt in range(NT + 1):
                if tt < NT:
                    ts_(xtm[:, tt, :], xtm[:, tt, :], ssq[:, 1, tt:tt + 1], None, ALU.mult).then_inc(S["x_scaled"], 1)
                if tt > 0:
                    for c in range(2):
                        key = ("hT", tt - 1, c)
                        wait_full(dve, key)
                        release(tt_(hT[:, 4 * c:4 * c + 4, (tt - 1) * P:tt * P],
                                    bank(key).rearrange("p (k q) -> p k q", k=4), over(gmix[:, 4 * c:4 * c + 4], P),
                                    ALU.mult), key)
            wait_read(dve, ("kv", NT - 1))
            link(ts_(kvtm[:, :, SWI:SDT], kvtm[:, :, SWI:SDT], IDX_SCALE, None, ALU.mult))
            tt_(wl.rearrange("p (h q) -> p h q", q=SQ), over(kvtm[:, SMP, SWI:SDT], SQ),
                qsel[:].rearrange("p (o q) -> p o q", o=1).broadcast_to([P, IH, SQ]), ALU.mult).then_inc(S["wl_ready"], 1)
            for i in range(1, 4):
                w = P * (i + 1)
                for h in range(IH):
                    u = IH * (i - 1) + h
                    wait_read(dve, ("pd", i, h))
                    wt = kvtm[:, i, SWI + h:SWI + h + 1]
                    if h == 0:
                        ins = ts_(bias_p[i], rel[:, u % 2, 0:w], wt, None, ALU.mult)
                    else:
                        ins = stt(out=bias_p[i], in0=rel[:, u % 2, 0:w], scalar=wt, in1=bias_p[i], op0=ALU.mult,
                                  op1=ALU.add)
                    ins.then_inc(S["rel_used"], 1)
                    dve.wait_ge(S["rel_used"], u + 1)
                link(tt_(bias_p[i][:, w - P:w], bias_p[i][:, w - P:w], adm_idx[:], ALU.add))
            link(nc.vector.memset(wsel, 0.0))
            wait_read(dve, ("wc",))
            for b in range(SB):
                ins = ts_(wsel[:, b, b * SQ:(b + 1) * SQ], qsel[:], wcol[:, b:b + 1], None, ALU.mult)
            ins.then_inc(S["wsel_ready"], 1)

            def top(scores, count):
                for _ in range(count // 8):
                    link(nc.vector.max(top8, scores))
                    link(nc.vector.match_replace(scores, top8, scores, TAKEN))
                ts_(scores, scores, CUT, NEG, ALU.is_gt, ALU.mult).then_inc(S["bias_ready"], 1)

            for i in range(1, 4):
                top(bias_p[i], TOPK_P)
            for c in range(3):
                w = 512 if c < 2 else SQ
                wait_full(dve, ("di", c))
                release(nc.vector.tensor_copy(bias_s[:, 512 * c:512 * c + w], bank(("di", c))[:, 0:w]), ("di", c))
            wait_read(dve, ("di", 2))
            top(bias_s, TOPK_S)
            tmp = st0[:, 0, :, :].rearrange("p b n -> p (b n)")
            tm = [tmp[:, i * NT * HEADS:(i + 1) * NT * HEADS].rearrange("p (t h) -> p t h", h=HEADS) for i in range(4)]
            link(tt_(dtv, kvtm[:, :, SDT:SW], dtb_row[:].rearrange("p (o h) -> p o h", o=1).broadcast_to([P, NT, HEADS]),
                     ALU.add))
            link(ts_(w2v, dtv, -1.0, None, ALU.mult))
            tt_(w2v, w2v, dtv, ALU.max).then_inc(S["dt_exp"], 1)
            dve.wait_ge(S["a_exp"], 1)
            link(ts_(tm[0], w2v, 2.0, None, ALU.add))
            link(nc.vector.reciprocal(tm[0], tm[0]))
            link(tt_(tm[0], w2v, tm[0], ALU.mult))
            link(tt_(tm[1], tm[0], tm[0], ALU.mult))
            link(ts_(tm[2], tm[1], 2.0 / 17, 2.0 / 15, ALU.mult, ALU.add))
            for m in (13, 11, 9, 7, 5, 3, 1):
                link(tt_(tm[2], tm[2], tm[1], ALU.mult))
                link(ts_(tm[2], tm[2], 2.0 / m, None, ALU.add))
            link(tt_(tm[2], tm[2], tm[0], ALU.mult))
            link(stt(out=dtv, in0=dtv, scalar=0.0, in1=tm[2], op0=ALU.max, op1=ALU.add))
            tt_(av, dtv, a_row[:].rearrange("p (o h) -> p o h", o=1).broadcast_to([P, NT, HEADS]), ALU.mult) \
                .then_inc(S["a_ready"], 1)
            for tt in range(NT):
                wait_full(dve, ("ac", tt))
                release(ts_(nac[:, tt, :], bank(("ac", tt))[:, 0:HEADS], -1.0, None, ALU.mult), ("ac", tt))
                wait_full(dve, ("ae", tt))
                wait_read(dve, ("ac", tt))
                release(tt_(w2v[:, tt, :], bank(("ae", tt))[:, 0:HEADS], nac[:, tt, :], ALU.add), ("ae", tt))
            ins_ready = ts_(ssq[:, 2, 0:1], ssq[:, 2, 0:1], 0.0, None, ALU.add)
            ins_ready.then_inc(S["ae_ready"], 1)
            dve.wait_ge(S["a_exp"], 2)
            link(tt_(w2v, w2v, dtv, ALU.mult))
            for g in range(GROUPS):
                ssd_dve(dve, g, link, over)
            attention_dve(dve, link, over)
            wait_full(dve, ("dT", SB - 1))
            wait_read(dve, ("dT", SB - 1))
            link(ts_(rr, ssrow, 1.0 / INNER, EPS, ALU.mult, ALU.add))
            nc.vector.tensor_copy(rt, rr).then_inc(S["ss_var"], 1)
            dve.wait_ge(S["ss_std"], 1)
            link(nc.vector.reciprocal(rt, rt))
            newton(rt, rr, mrg[:, 0, :])
            for m in range(2):
                wait_read(dve, ("gaS", m))
                link(tt_(gate[:, 0], gate[:, 0], rt.rearrange("p (o t) -> p o t", o=1).broadcast_to([P, 4, T]), ALU.mult))
                for j in range(4):
                    wait_full(dve, ("a", m, j))
                    release(tt_(mrg[:, 4 * m + j, 0:TP], bank(("a", m, j)), gate[:, 0, j, 0:TP], ALU.mult), ("a", m, j))
                wait_full(dve, ("aS", m))
                release(tt_(mrg[:, 4 * m:4 * m + 4, TP:T], bank(("aS", m)).rearrange("p (j q) -> p j q", j=4),
                            gate[:, 0, :, TP:T], ALU.mult), ("aS", m))
                wait_read(dve, ("gbS", m))
                for j in range(4):
                    wait_full(dve, ("b", m, j))
                    release(tt_(gate[:, 1, j, 0:TP], bank(("b", m, j)), gate[:, 1, j, 0:TP], ALU.mult), ("b", m, j))
                wait_full(dve, ("bS", m))
                release(tt_(gate[:, 1, :, TP:T], bank(("bS", m)).rearrange("p (j q) -> p j q", j=4),
                            gate[:, 1, :, TP:T], ALU.mult), ("bS", m))
                wait_read(dve, ("bS", m))
                tt_(mrg[:, 4 * m:4 * m + 4, :], mrg[:, 4 * m:4 * m + 4, :], gate[:, 1], ALU.add).then_inc(S["m_ready"], 1)
            for tt in range(NT):
                dve.wait_ge(pair["xres_loaded"][tt % 2], 16 * (tt // 2 + 1))
                for m in range(2):
                    wait_full(dve, ("x1", tt, m))
                    release(tt_(x1[:, tt, 512 * m:512 * m + 512], bank(("x1", tt, m)),
                                xres[:, tt % 2, 512 * m:512 * m + 512], ALU.add), ("x1", tt, m))
            dve.wait_ge(S["hx_squares"], NT)
            ts_(ssq[:, 2, 0:NT], ssq[:, 2, 0:NT], 1.0 / D, EPS, ALU.mult, ALU.add).then_inc(S["hx_var"], 1)
            dve.wait_ge(S["hx_std"], 1)
            link(nc.vector.reciprocal(ssq[:, 3, 0:NT], ssq[:, 3, 0:NT]))
            newton(ssq[:, 3, 0:NT], ssq[:, 2, 0:NT], ssq[:, 4, 0:NT])
            for tt in range(NT + 1):
                if tt < NT:
                    ts_(xn[:, tt, :], x1[:, tt, :], ssq[:, 3, tt:tt + 1], None, ALU.mult).then_inc(S["hx_scaled"], 1)
                if tt > 0:
                    for c in range(2):
                        key = ("h2", tt - 1, c)
                        wait_full(dve, key)
                        release(tt_(h2T[:, 4 * c:4 * c + 4, (tt - 1) * P:tt * P],
                                    bank(key).rearrange("p (k q) -> p k q", k=4), over(gmoe[:, 4 * c:4 * c + 4], P),
                                    ALU.mult), key)
            for tt in range(NT):
                wait_full(dve, ("rt", tt))
                release(tt_(lg[:, tt, :], bank(("rt", tt))[:, 0:MG + NE], brow[:], ALU.add), ("rt", tt))
            wait_read(dve, ("rt", NT - 1))
            route(dve, link, over)
            for e in range(NE):
                for m in range(2):
                    wait_full(dve, ("he", e, 2 + m))
                    wait_read(dve, ("he", e, m))
                    release(tt_(heT[:, e % 2, m, 0:TP], bank(("he", e, 2 + m)), hsil[:, m, 0:TP], ALU.mult),
                            ("he", e, 2 + m))
                wait_read(dve, ("heS", e), 1)
                release(tt_(heT[:, e % 2, :, TP:T], bank(("heS", e))[:, 2 * P:4 * P].rearrange("p (j q) -> p j q", j=2),
                            hsil[:, :, TP:T], ALU.mult), ("heS", e))
                for tt in range(NT):
                    for m in range(2):
                        key = ("y", e, tt, m)
                        c = comb[:, tt, e // ME, e % ME:e % ME + 1]
                        out = ysum[:, tt, 512 * m:512 * m + 512]
                        wait_full(dve, key)
                        if e == 0:
                            ins = ts_(out, bank(key), c, None, ALU.mult)
                        else:
                            wait_read(dve, ("y", e - 1, tt, m))
                            ins = stt(out=out, in0=bank(key), scalar=c, in1=out, op0=ALU.mult, op1=ALU.add)
                        release(ins, key)
            wait_read(dve, ("y", NE - 1, NT - 1, 1))
            for tt in range(NT):
                tt_(ysum[:, tt, :], ysum[:, tt, :], x1[:, tt, :], ALU.add).then_inc(S["ysum_ready"], 1)
            dve.wait_ge(S["fx_squares"], NT)
            ts_(ssq[:, 4, 0:NT], ssq[:, 4, 0:NT], 1.0 / D, EPS, ALU.mult, ALU.add).then_inc(S["fx_var"], 1)
            dve.wait_ge(S["fx_std"], 1)
            link(nc.vector.reciprocal(ssq[:, 5, 0:NT], ssq[:, 5, 0:NT]))
            newton(ssq[:, 5, 0:NT], ssq[:, 4, 0:NT], ssq[:, 2, 0:NT])
            dve.wait_ge(S["fin_loaded"], 16)
            for tt in range(NT):
                stt(out=ysum[:, tt, :], in0=ysum[:, tt, :], scalar=ssq[:, 5, tt:tt + 1], in1=fin_row, op0=ALU.mult,
                    op1=ALU.mult).then_inc(S["fin_ready"], 1)


_INS = ['x_prompt', 'x_sample', 'cache_k', 'cache_v', 'cache_kidx', 'state_conv', 'state_ssm', 'norm_mix_g', 'w_in',
        'conv_w', 'conv_b', 'dt_bias', 'A_log', 'D_skip', 'ssm_norm_g', 'w_ssm_out', 'w_attn_out', 'w_o', 'norm_moe_g',
        'w_router_group', 'b_router_group', 'w_router_expert', 'b_router_expert', 'w1', 'w3', 'w2', 'norm_final_g']
_OUTS = [(1, TP, D), (SB, SQ, D), (1, TP, AKV, HD), (1, TP, AKV, HD), (1, TP, IDIM), (1, CW - 1, CD),
         (1, HEADS, HP, NS), (SB, SQ, AKV, HD), (SB, SQ, AKV, HD), (SB, SQ, IDIM), (SB, CW - 1, CD),
         (SB, HEADS, HP, NS)]


def kernel(**inputs):
    import numpy as _np
    import concourse.bacc as _bacc
    from concourse import mybir as _mybir
    from concourse.bass_utils import run_bass_kernel_spmd as _run

    nc = _bacc.Bacc("TRN2", target_bir_lowering=False, num_devices=1)
    arrays, args = {}, []
    for name in _INS:
        a = _np.ascontiguousarray(inputs[name])
        arrays[f"in_{name}"] = a
        args.append(nc.dram_tensor(f"in_{name}", a.shape, _mybir.dt.from_np(a.dtype), kind="ExternalInput").ap())
    for i, shape in enumerate(_OUTS):
        args.append(nc.dram_tensor(f"out_{i}", shape, _mybir.dt.float32, kind="ExternalOutput").ap())
    hybrid_layer(nc, *args)
    r = _run(nc, [arrays], core_ids=[0])
    return tuple(r.results[0][f"out_{i}"] for i in range(len(_OUTS)))
```

```python
from contextlib import ExitStack

import concourse.bass as bass
from concourse import mybir

F32 = mybir.dt.float32
I32 = mybir.dt.int32
ALU = mybir.AluOpType
ACT = mybir.ActivationFunctionType
AX = mybir.AxisListType

P = 128
D = 1024
KD = D // P
TP = 512
SB, SQ = 8, 16
T = TP + SB * SQ
NT = T // P
SMP = NT - 1
PAST = 1024
KEYS = PAST + SQ
KJ = PAST // P
EPS = 1e-6
INNER, HEADS, HP, GROUPS, NS = 2048, 32, 64, 4, 128
HG = HEADS // GROUPS
CD = INNER + 2 * GROUPS * NS
CT = CD // P
CW = 4
AH, AKV, HD = 16, 2, 64
AR = AH // AKV
IH, IDIM = 8, 64
IDX_SCALE = (IH * IDIM) ** -0.5
TOPK_P, TOPK_S = 128, 256
ROUNDS_P = TOPK_P // 8
ROUNDS = 3 * ROUNDS_P + TOPK_S // 8
CHUNK = 64
ATT_SCALE = HD ** -0.5
MG, ME = 4, 8
NE = MG * ME
FF = 256
SLOTS = 64
TAIL = (2 * T - 1) // SLOTS
NB = NE + TAIL
NOWHERE = 1 << 20
Z0 = 0
X0 = INNER
B0 = X0 + INNER
C0 = B0 + GROUPS * NS
DT0 = X0 + CD
Q0 = DT0 + HEADS
K0 = Q0 + AH * HD
V0 = K0 + AKV * HD
QI0 = V0 + AKV * HD
KI0 = QI0 + IH * IDIM
WI0 = KI0 + IDIM
G0 = WI0 + IH
SK, SV, SKI, SWI, SDT, SW = 0, 128, 256, 320, 328, 360
NEG = -1.0e30
NOTADM = -1.0e38
TAKEN = -3.0e38
CUT = -2.0e38


class Banks:

    def __init__(self):
        self.job, self.turn = {}, {}
        self.full, self.free = [0] * 8, [0] * 8
        self.last = [None] * 8

    def add(self, key, pool, readers=1, width=1):
        assert key not in self.job, key
        i = self.turn.get(pool, 0)
        self.turn[pool] = i + 1
        b = pool[i % len(pool)]
        before = sorted({self.last[c] for c in range(b, b + width) if self.last[c]})
        self.full[b] += 1
        self.free[b] += readers
        for c in range(b, b + width):
            self.last[c] = (b, self.free[b])
        self.job[key] = (b, self.full[b], before, self.free[b])


class Ring:

    def __init__(self, slots):
        self.slots, self.job, self.order, self.loads = slots, {}, [], [0] * slots

    def add(self, key, used, parts):
        s = len(self.order) % self.slots
        self.loads[s] += 16 * len(parts)
        self.job[key] = (s, self.loads[s])
        self.order.append((key, used, parts))


def plan_banks():
    b = Banks()
    any8 = tuple(range(8))
    for i in range(2):
        b.add(("par", i), any8)
    for tt in range(NT):
        for c in range(2):
            b.add(("hT", tt, c), any8)
    for tt in range(NT):
        b.add(("kv", tt), any8)
    for c in range(2):
        for t in range(4 * c, 4 * c + 4):
            b.add(("q", t), any8)
        b.add(("qS", c), any8)
    for t in range(4):
        b.add(("qi", t), any8)
    b.add(("qiS",), any8)
    for i in range(4):
        b.add(("kT", i), any8)
    for i in range(1, 4):
        for h in range(IH):
            b.add(("pd", i, h), any8)
    b.add(("wc",), (3,))
    for i in range(3):
        b.add(("di", i), (0, 1, 2))
    work = (3, 4, 5, 6, 7)
    for s in range(SB + 2):
        if s < SB:
            b.add(("kx", s, 0), work)
            b.add(("kx", s, 1), work)
        if 1 <= s <= SB:
            for c in range(3):
                b.add(("dd", s - 1, c), work)
    for tt in range(NT):
        b.add(("ac", tt), any8)
        b.add(("ae", tt), any8, readers=2)
    for g in range(GROUPS):
        plan_group(b, g)
    for i in range(SMP):
        for k in range(AH + 3):
            if k < AH:
                b.add(("s", i, k), (0, 1, 2))
            if 2 <= k < AH + 2:
                b.add(("pT", i, k - 2), (3, 4, 5))
            if k >= 3 and (k - 3) % AR == 0:
                b.add(("o", i, (k - 3) // AR), (6, 7))
    for s in range(SB + 1):
        if s < SB:
            for c in range(2):
                b.add(("kc", s, c), (6, 7))
            for g in range(AKV):
                b.add(("ds", s, g), (0, 3), width=3)
        if s >= 1:
            for g in range(AKV):
                for c in range(3):
                    b.add(("pt", s - 1, g, c), (6, 7))
            b.add(("do", s - 1), (6, 7))
    for n in range(2):
        for what in ("ga", "gb", "a", "b"):
            for c in range(4):
                b.add((what, n, c), (0, 1, 2, 3))
            b.add((what + "S", n), (4, 5, 6, 7))
    for tt in range(NT):
        for n in range(2):
            b.add(("x1", tt, n), any8)
    for tt in range(NT):
        for c in range(2):
            b.add(("h2", tt, c), any8)
    for tt in range(NT):
        b.add(("rt", tt), any8)
    b.add(("rank",), any8)
    b.add(("slots",), any8)
    return b


def plan_group(b, g):
    lo, hi = (0, 1, 2, 3), (4, 5, 6, 7)
    b.add(("cT", g), hi)
    b.add(("xbcS", g, 0), hi)
    for j in range(4):
        b.add(("xbc", g, j), lo)
    if g:
        for i in range(2):
            b.add(("ss", g - 1, i), hi)
    b.add(("xbcS", g, 1), hi)
    for j in range(4, 6):
        b.add(("xbc", g, j), lo)
    for j in range(4):
        b.add(("z", g, j), lo)
    b.add(("zS", g), hi)
    b.add(("cO", g, 0), hi)
    b.add(("cO", g, 1), hi)
    b.add(("bt", g, 0), hi)
    b.add(("bt", g, 1), hi)
    for tt in range(NT):
        b.add(("xt", g, tt), lo)
        b.add(("cb", g, tt), hi)
        for i in range(2):
            b.add(("sg", g, tt, i), lo)
        b.add(("eb", g, tt), hi)
        if 0 < tt < SMP:
            b.add(("yi", g, tt), lo)
        if tt < SMP:
            b.add(("st", g, tt), hi)
        b.add(("yo", g, tt), lo)
    b.add(("so", g), hi)
    for j in range(4):
        for i in range(2):
            b.add(("s0", g, j, i), lo)
        for i in range(2):
            b.add(("sn", g, j, i), hi)
        b.add(("ys", g, j), lo)
    if g == GROUPS - 1:
        for i in range(2):
            b.add(("ss", g, i), hi)


def hybrid_layer(nc, x_prompt, x_sample, cache_k, cache_v, cache_kidx, state_conv, state_ssm,
                 norm_mix_g, w_in, conv_w, conv_b, dt_bias, A_log, D_skip, ssm_norm_g,
                 w_ssm_out, w_attn_out, w_o, norm_moe_g, w_router_group, b_router_group,
                 w_router_expert, b_router_expert, w1, w3, w2, norm_final_g,
                 y_prompt, y_sample, k_prompt, v_prompt, kidx_prompt, conv_prompt, ssm_prompt,
                 k_sample, v_sample, kidx_sample, conv_sample, ssm_sample):
    banks = plan_banks()
    w_in_r = w_in.rearrange("(k p) n -> p k n", p=P)

    ring = Ring(3)

    def cols(a, n, at=0):
        return (lambda s: s[:, :, at:at + n], w_in_r[:, :, a:a + n])

    ring.add(("small",), ("kv", NT - 1), [cols(K0, 256), cols(KI0, 72, SKI), cols(DT0, 32, SDT)])
    for c in range(2):
        ring.add(("wq", c), ("qS", c), [
            (lambda s, k=k, g=g: s[:, k, :].rearrange("p (t g d) -> p g t d", g=AKV, d=HD)[:, g, :, :],
             w_in[k * P:(k + 1) * P, Q0 + g * AR * HD + c * 256:Q0 + g * AR * HD + c * 256 + 256]
             .rearrange("p (t d) -> p t d", d=HD))
            for k in range(KD) for g in range(AKV)])
    ring.add(("wqi",), ("qiS",), [cols(QI0, 512)])
    for g in range(GROUPS):
        ring.add(("wx", g), ("xbc", g, 3), [cols(X0 + 512 * g, 512)])
        ring.add(("wbc", g), ("xbc", g, 5), [cols(B0 + NS * g, NS), cols(C0 + NS * g, NS, NS)])
        ring.add(("wz", g), ("zS", g), [cols(Z0 + 512 * g, 512)])
    wso_r = w_ssm_out.rearrange("(k p) n -> p k n", p=P)
    for n in range(2):
        ring.add(("wga", n), ("gaS", n), [cols(G0 + 512 * n, 512)])
        ring.add(("wgb", n), ("gbS", n), [cols(G0 + D + 512 * n, 512)])
        for c in range(2):
            ring.add(("wso", n, c), ("aS", n), [(lambda s: s[:, :, :], wso_r[:, 8 * c:8 * c + 8, 512 * n:512 * n + 512])])
        ring.add(("wao", n), ("bS", n), [
            (lambda s, g=g: s[g * HD:(g + 1) * HD, :, :],
             w_attn_out[g * AR * HD:(g + 1) * AR * HD, 512 * n:512 * n + 512].rearrange("(t d) n -> d t n", d=HD))
            for g in range(AKV)])
    wo_r = w_o.rearrange("(k p) n -> p k n", p=P)
    for n in range(2):
        ring.add(("wo", n), ("x1", NT - 1, 1), [(lambda s: s[:, :, :], wo_r[:, :, 512 * n:512 * n + 512])])
    with ExitStack() as ctx:
        def sb(name, shape, dtype=F32):
            return ctx.enter_context(nc.sbuf_tensor(name, shape, dtype))

        def sem(name):
            return ctx.enter_context(nc.semaphore(name))

        psum = ctx.enter_context(nc.psum_tensor("psum", [P, 8 * 512], F32))

        ident = sb("ident", [P, P])
        ones = sb("ones", [P, P])
        cum_p, cum_s = sb("cum_p", [P, P]), sb("cum_s", [P, P])
        neg_p, neg_s = sb("neg_p", [P, P]), sb("neg_s", [P, P])
        same = sb("same", [P, P])
        stream = sb("stream", [P, SB])
        adm_idx, adm_att = sb("adm_idx", [P, P]), sb("adm_att", [P, P])
        qsel = sb("qsel", [P, SQ])
        prio = sb("prio", [P, ME])
        count = sb("count", [P, SLOTS])
        entry = sb("entry", [P, 2, NT])
        slot_row = sb("slot_row", [P, NB], I32)
        tail_expert = sb("tail_expert", [P, TAIL], I32)
        beyond = sb("beyond", [P, 1], I32)
        cur_row = sb("cur_row", [P, 1], I32)
        wk = sb("wk", [P, 2, NT])
        pc = sb("pc", [P, 2, P])
        a_row, dtb_row, dsk_row = sb("a_row", [P, HEADS]), sb("dtb_row", [P, HEADS]), sb("dsk_row", [P, HEADS])
        dcol = sb("dcol", [P, HEADS // 2])
        brow = sb("brow", [P, MG + NE])
        cw_col = pc[:, 0, 0:CW * CT].rearrange("p (w c) -> p w c", w=CW)
        cb_col = pc[:, 0, CW * CT:CW * CT + CT]
        gmix = pc[:, 0, 120:128]
        gmoe = pc[:, 1, 0:8]
        gssm = pc[:, 1, 8:24]
        ssq = sb("ssq", [P, 6, 8])

        wring = sb("wring", [P, 3, KD, 512])
        hT = sb("hT", [P, KD, T])
        kvtm = sb("kvtm", [P, NT, SW])
        oT = sb("oT", [P, KD, T])
        hTf = hT[:].rearrange("p k t -> p (k t)")
        oTf = oT[:].rearrange("p k t -> p (k t)")
        arena = sb("arena", [P, 27044])

        class Arena:

            def __init__(self, base, at=0):
                self.base, self.at = base, at

            def take(self, *shape):
                n = 1
                for s in shape:
                    n *= s
                v = self.base[:, self.at:self.at + n]
                self.at += n
                assert self.at <= self.base.shape[1], self.at
                if len(shape) == 1:
                    return v
                names = "abcd"[:len(shape)]
                return v.rearrange(f"p ({' '.join(names)}) -> p {' '.join(names)}",
                                   **{names[i]: shape[i] for i in range(len(shape))})

        keep = Arena(arena)
        kT, qs = keep.take(T), keep.take(SB, KD, SQ)
        bias_p = [None] + [keep.take(P * (i + 1)) for i in range(1, 4)]
        bias_s = keep.take(KEYS)
        ssrow = keep.take(T)
        kept = keep.at
        a1 = Arena(arena, kept)
        xtm, par, junk = a1.take(NT, D), a1.take(2, P), a1.take(D)
        a1 = Arena(arena, a1.at)
        qiT, qis, kiT = a1.take(IH, TP), a1.take(SB, IH, SQ), a1.take(T)
        wsel, wl, wcol = a1.take(SB, P), a1.take(P), a1.take(SB)
        rel, kx_in, kxT = a1.take(2, KEYS), a1.take(2, KJ, IDIM), a1.take(2, PAST)
        top8 = ssq[:, 5, :]
        a2 = Arena(arena, kept)
        raw, acc = a2.take(2, 667), a2.take(1, 664)
        xsT, bcT, zT = a2.take(4, T), a2.take(2, T), a2.take(4, T)
        yb = oTf.rearrange("p (u j t) -> p u j t", u=2, j=4)
        btm, bms = a2.take(NT, NS), a2.take(SB, NS)
        xdt, xw = a2.take(2, 512), a2.take(2, 512)
        mt, cbs, ebs = a2.take(3, 512), a2.take(2, P), a2.take(2, 512)
        ytmp, stT = a2.take(512), a2.take(512)
        dtv, av, nac, expae, w2v = (a2.take(NT, HEADS) for _ in range(5))
        st0, s0T = a2.take(3, SB, NS), a2.take(SB, P)
        sout, cin, cst = a2.take(512), a2.take(6, P), a2.take(6, 24)
        cgo, crow = a2.take(6, 27), cin
        a3 = Arena(arena, kept)
        sm, pT = a3.take(3, 512), a3.take(2, 512)
        kz, qz, bexp = a3.take(AKV, TP), a3.take(SB, AKV, P), a3.take(2, KEYS)
        mx, rsum, rinv = a3.take(8), a3.take(8), a3.take(8)
        kb, vb, kcT = a3.take(2, KJ, P), a3.take(2, KJ, P), a3.take(2, PAST)
        pexp, ptS, ptN = a3.take(2, KEYS), a3.take(2, KJ, P), a3.take(2, P)
        vnew = a3.take(SB, P)
        a4 = Arena(arena, 0)
        mrg = a4.take(KD, T)
        gate = a4.take(2, 4, T)
        rr, rt = a4.take(T), a4.take(T)
        yz = a4.take(16, T)
        a5 = Arena(arena, KD * T)
        xres, x1 = a5.take(2, D), a5.take(NT, D)
        h2T, xn = a5.take(KD, T), oTf.rearrange("p (t d) -> p t d", t=NT)
        hg, hgT, ysl = a5.take(2, D), a5.take(2, KD, SLOTS), a5.take(2, D)
        hsil, hetm, heT = a5.take(2, FF), a5.take(2, FF), a5.take(2, 2, SLOTS)
        lg = a5.take(NT, MG + NE)
        rb = [a5.take(NT, ME) for _ in range(5)]
        rc = [a5.take(NT, MG) for _ in range(3)]
        rs1 = a5.take(8, NT)
        hot = a5.take(2, NT, NE)
        cnt = a5.take(NT, NE)
        rank_, tmp_e = a5.take(NT, NE), a5.take(2, NT, NE)
        need, first_x, scan = a5.take(NE), a5.take(NE), a5.take(2, NE)
        rk, ek, xk, qk, bk = (a5.take(2, NT) for _ in range(5))
        a6 = Arena(arena, a5.at)
        wr = a6.take(KD, MG + NE)
        at_pos, at_blk = a6.take(2, SLOTS), a6.take(2, NB)
        tail_sum = ysl.rearrange("p u d -> p (u d)")[:, 0:2 * TAIL * NE].rearrange("p (i x e) -> p i x e", i=2, e=NE)
        w13 = [hTf[:, 0:KD * 512].rearrange("p (k n) -> p k n", k=KD)] + [wring[:, s] for s in (1, 2, 0)]
        h2f = h2T.rearrange("p k t -> p (k t)")
        w2s = [v.rearrange("p (k n) -> p k n", k=2) for v in
               (arena[:, 0:2 * D], arena[:, 2 * D:4 * D], arena[:, 4 * D:6 * D], h2f[:, 0:2 * D])]
        nothing = ssq[:, 5, 7:8]
        fin_row = h2f[:, 2 * D:3 * D]
        rows_in = [hg[:, 0], hg[:, 1], h2f[:, 3 * D:4 * D], h2f[:, 4 * D:5 * D]]
        ypart = arena[:, 0:4 * D].rearrange("p (u c d) -> p u c d", u=2, c=2)

        x_rows = nc.dram_tensor("x_rows", (2 * T, D), F32, kind="Internal").ap()
        y_rows = nc.dram_tensor("y_rows", (2 * T, D), F32, kind="Internal").ap()
        q_spill = nc.dram_tensor("q_spill", (P, KD, TP), F32, kind="Internal").ap()
        y_spill = nc.dram_tensor("y_spill", (P, 16, T), F32, kind="Internal").ap()

        full = [sem(f"full{i}") for i in range(8)]
        free = [sem(f"free{i}") for i in range(8)]
        slot_loaded = [sem(f"slot_loaded{i}") for i in range(3)]
        params_loaded, rows_loaded = sem("params_loaded"), sem("rows_loaded")
        x_loaded = [sem(f"x_loaded{i}") for i in range(NT)]
        consts, out_written = sem("consts"), sem("out_written")
        dve_chain, act_chain, pool_chain = sem("dve_chain"), sem("act_chain"), sem("pool_chain")

        def bank(key, width=1):
            b = banks.job[key][0]
            return psum[:, b * 512:(b + width) * 512]

        def pbank(i):
            return psum[:, i * 512:(i + 1) * 512]

        def claim(pe, key):
            for b, n in banks.job[key][2]:
                pe.wait_ge(free[b], n)
            return bank(key)

        def filled(ins, key):
            ins.then_inc(full[banks.job[key][0]], 1)

        def wait_full(eng, key):
            b, n, _, _ = banks.job[key]
            eng.wait_ge(full[b], n)

        def release(ins, key):
            ins.then_inc(free[banks.job[key][0]], 1)

        def wait_read(eng, key, short=0):
            b, _, _, n = banks.job[key]
            eng.wait_ge(free[b], n - short)

        def slot(key):
            return wring[:, ring.job[key][0], :, :]

        def wait_chunk(pe, key):
            s, n = ring.job[key]
            pe.wait_ge(slot_loaded[s], n)
            return slot(key)

        S = {name: sem(name) for name in (
            "x_squares", "x_var", "x_std", "x_scaled", "a_row_ready", "wl_ready", "wsel_ready", "rel_used",
            "bias_ready", "dt_exp", "a_exp", "a_ready", "ae_ready", "raw_zeroed", "raw_ready", "conv_done",
            "xs_ready", "gathered", "bms_ready", "mt_exp", "mt_ready", "y_gated", "y_squares", "y_gained",
            "q_spilled", "y_spilled", "crow_written", "sout_written", "q_back", "vnew_loaded", "y_back",
            "router_loaded", "fin_loaded", "at_exp", "kz_ready", "p_scaled", "ss_var", "ss_std", "m_ready", "hx_squares",
            "hx_var", "hx_std", "hx_scaled", "r_exp_in", "r_exp", "ysum_ready", "hot_ready", "at_ready", "at_used", "t_full", "t_read", "up_full", "silu_ready", "he_ready",
            "heT_full", "heT_ready",
            "dn0_full", "dn1_full", "dn0_read", "dn1_read", "xn_stored", "fx_squares", "fx_var", "fx_std",
            "fin_ready", "y_written", "parts_added", "last_chain")}
        w13_loaded = [sem(f"w13_loaded{i}") for i in range(4)]
        st0_loaded = [sem(f"st0_loaded{i}") for i in range(3)]
        st0_written = [sem(f"st0_written{i}") for i in range(3)]
        w2_loaded = [sem(f"w2_loaded{i}") for i in range(4)]
        gathered_rows = [sem(f"gathered_rows{i}") for i in range(4)]
        pair = {name: [sem(f"{name}{i}") for i in range(2)] for name in (
            "kx_loaded", "kb_loaded", "bexp_loaded", "vb_loaded", "xres_loaded", "cin_loaded", "scattered", "ypart_loaded")}

        main = ExitStack()
        block = main.enter_context(nc.Block())
        ST0_USES = [len(range(i, 4 * GROUPS, 3)) for i in range(3)]
        N_OUT = 3 * NT

        @block.sync
        def _(sp):
            def chunks(upto_key):
                while sent[0] < len(ring.order):
                    key, _, parts = ring.order[sent[0]]
                    if sent[0] >= ring.slots:
                        wait_full(sp, ring.order[sent[0] - ring.slots][1])
                    for part, src in parts:
                        sp.dma_start(part(slot(key)), src).then_inc(slot_loaded[ring.job[key][0]], 16)
                    sent[0] += 1
                    if key == upto_key:
                        return

            sent = [0]
            for tt in range(SMP):
                sp.dma_start(xtm[:, tt, :], x_prompt[0, tt * P:(tt + 1) * P, :]).then_inc(x_loaded[tt], 16)
            sp.dma_start(xtm[:, SMP, :], x_sample.rearrange("b q d -> (b q) d")).then_inc(x_loaded[SMP], 16)
            for lo, hi, i, src in ((0, 96, 0, conv_w.rearrange("w (c p) -> (w c) p", p=P)),
                                   (96, 120, 0, conv_b.rearrange("(c p) -> c p", p=P)),
                                   (120, 128, 0, norm_mix_g.rearrange("(c p) -> c p", p=P)),
                                   (0, 8, 1, norm_moe_g.rearrange("(c p) -> c p", p=P)),
                                   (8, 24, 1, ssm_norm_g.rearrange("(c p) -> c p", p=P))):
                sp.dma_start(par[lo:hi, i, :], src).then_inc(params_loaded, 16)
            for dst, src in ((a_row[:], A_log), (dtb_row[:], dt_bias), (dsk_row[:], D_skip),
                             (brow[:, 0:MG], b_router_group), (brow[:, MG:MG + NE], b_router_expert)):
                sp.dma_start(dst, src.rearrange("(o n) -> o n", o=1).broadcast_to([P, src.shape[0]])) \
                    .then_inc(rows_loaded, 16)
            chunks(("wqi",))
            for s in range(SB):
                if s == 0:
                    wait_read(sp, ("hT", NT - 1, 1))
                if s >= 2:
                    wait_full(sp, ("kx", s - 2, 1))
                sp.dma_start(kx_in[:, s % 2, :, :], cache_kidx[s].rearrange("(p j) d -> p j d", j=KJ)) \
                    .then_inc(pair["kx_loaded"][s % 2], 16)
            for c in range(3):
                wait_read(sp, ("di", c))
            chunks(("wz", 0))
            for g in range(GROUPS):
                if g:
                    sp.wait_ge(S["crow_written"], 96 * g)
                for at, n, c in ((0, 4, 512 * g), (4, 1, INNER + NS * g), (5, 1, INNER + (GROUPS + g) * NS)):
                    sp.dma_start(cin[0:24, at:at + n, :],
                                 state_conv[:, :, c:c + n * P].rearrange("b r (c p) -> (b r) c p", p=P)) \
                        .then_inc(pair["cin_loaded"][0], 16)
                chunks(("wz", min(g + 1, GROUPS - 1)) if g + 1 < GROUPS else ("wgb", 0))
                for j in range(4):
                    u = 4 * g + j
                    if u >= 3:
                        sp.wait_ge(st0_written[u % 3], 16 * (u // 3))
                    r = (4 * g + j) * P
                    sp.dma_start(st0[:, u % 3, :, :],
                                 state_ssm.rearrange("b h p n -> (h p) b n")[r:r + P, :, :]) \
                        .then_inc(st0_loaded[u % 3], 16)
            sp.wait_ge(S["q_spilled"], 16)
            sp.wait_ge(S["y_spilled"], 16 * GROUPS)
            wait_read(sp, ("ss", GROUPS - 1, 1))
            for i in range(3):
                sp.wait_ge(st0_written[i], 16 * ST0_USES[i])
            sp.wait_ge(S["crow_written"], 16 * 6 * GROUPS)
            sp.wait_ge(S["sout_written"], 16 * GROUPS)
            sp.dma_start(oT[:, :, 0:TP], q_spill[:, :, :]).then_inc(S["q_back"], 16)
            sp.wait_ge(S["bias_ready"], 4)
            for s in range(SB + 1):
                if s < SB:
                    if s >= 2:
                        wait_full(sp, ("kc", s - 2, 1))
                    sp.dma_start(kb[:, s % 2, :, :], cache_k[s].rearrange("(p j) g d -> p j (g d)", j=KJ)) \
                        .then_inc(pair["kb_loaded"][s % 2], 16)
                    if s >= 2:
                        wait_read(sp, ("ds", s - 2, 1))
                    for t in range(AR):
                        sp.dma_start(bexp[t * SQ:(t + 1) * SQ, s % 2, :], bias_s[s * SQ:(s + 1) * SQ, :]) \
                            .then_inc(pair["bexp_loaded"][s % 2], 16)
                if s >= 1:
                    b = s - 1
                    if b >= 2:
                        wait_full(sp, ("do", b - 2))
                    sp.dma_start(vb[:, b % 2, :, :], cache_v[b].rearrange("(p j) g d -> p j (g d)", j=KJ)) \
                        .then_inc(pair["vb_loaded"][b % 2], 16)
            wait_read(sp, ("do", SB - 1))
            sp.dma_start(yz[:, :, :], y_spill[:, :, :]).then_inc(S["y_back"], 16)
            chunks(("wo", 1))

            def load13(e):
                sp.dma_start(w13[e % 4][:, :, 0:FF], w1[e].rearrange("(k p) f -> p k f", p=P)) \
                    .then_inc(w13_loaded[e % 4], 16)
                sp.dma_start(w13[e % 4][:, :, FF:], w3[e].rearrange("(k p) f -> p k f", p=P)) \
                    .then_inc(w13_loaded[e % 4], 16)

            def load2(e):
                sp.dma_start(w2s[e % 4], w2[e].rearrange("(k p) n -> p k n", p=P)).then_inc(w2_loaded[e % 4], 16)

            sp.wait_ge(S["m_ready"], 2)
            wait_full(sp, ("bS", 1))
            sp.dma_start(wr[:, :, 0:MG], w_router_group.rearrange("(k p) n -> p k n", p=P)).then_inc(S["router_loaded"], 16)
            sp.dma_start(wr[:, :, MG:], w_router_expert.rearrange("(k p) n -> p k n", p=P)).then_inc(S["router_loaded"], 16)
            for tt in range(NT):
                if tt >= 2:
                    wait_read(sp, ("x1", tt - 2, 1))
                src = x_prompt[0, tt * P:(tt + 1) * P, :] if tt < SMP else x_sample.rearrange("b q d -> (b q) d")
                sp.dma_start(xres[:, tt % 2, :], src).then_inc(pair["xres_loaded"][tt % 2], 16)
                if tt == 1:
                    load13(0)
                    load13(1)
            wait_read(sp, ("x1", NT - 1, 1))
            load2(0)
            load13(2)
            load2(1)
            load13(3)
            load2(2)
            wait_full(sp, ("rt", NT - 1))
            load2(3)
            sp.dma_start(fin_row, norm_final_g.rearrange("(o n) -> o n", o=1).broadcast_to([P, D])) \
                .then_inc(S["fin_loaded"], 16)
            for e in range(4, NE):
                sp.wait_ge(S["up_full"], e - 3)
                load13(e)
                sp.wait_ge(S["dn1_full"], e - 3)
                load2(e)
            sp.wait_ge(out_written, 16 * N_OUT)
            for i in range(3):
                sp.wait_ge(st0_written[i], 16 * ST0_USES[i])
            sp.wait_ge(S["crow_written"], 16 * 6 * GROUPS)
            sp.wait_ge(S["sout_written"], 16 * GROUPS)

        @block.gpsimd
        def _(pool):
            n = [0]

            def link(ins):
                n[0] += 1
                ins.then_inc(pool_chain, 1)
                pool.wait_ge(pool_chain, n[0])

            def select(out, in_, fill, pattern, base, cm, op=ALU.is_ge):
                link(nc.gpsimd.affine_select(out=out, in_=in_, compare_op=op, fill=fill, base=base,
                                             pattern=pattern, channel_multiplier=cm))

            for t, v in ((ident, 0.0), (ones, 1.0), (cum_p, 1.0), (neg_p, 0.0), (same, 1.0), (stream, 1.0),
                         (adm_idx, 0.0), (adm_att, 0.0)):
                link(nc.gpsimd.memset(t[:], v))
            select(ident[:], ident[:], 1.0, [[-1, P]], 0, 1, ALU.not_equal)
            select(cum_p[:], cum_p[:], 0.0, [[1, P]], 0, -1)
            select(neg_p[:], neg_p[:], NEG, [[1, P]], 0, -1)
            for t, w in ((same, SQ), (stream, 1)):
                v = t[:].rearrange("p (b q) -> p b q", q=w)
                select(v, v, 0.0, [[-SQ, SB], [0, w]], 0, 1)
                select(v, v, 0.0, [[SQ, SB], [0, w]], SQ - 1, -1)
            select(cum_s[:], same[:], 0.0, [[1, P]], 0, -1)
            link(nc.gpsimd.tensor_scalar(neg_s[:], cum_s[:], 1.0, -NEG, ALU.subtract, ALU.mult))
            for t, fill in ((adm_idx, NOTADM), (adm_att, NEG)):
                v = t[:].rearrange("p (a k) -> p a k", k=CHUNK)
                select(v, v, fill, [[-CHUNK, 2], [0, CHUNK]], 0, 1)
            nc.gpsimd.iota(prio[:], [[-1, ME]], base=ME, channel_multiplier=0,
                           allow_small_or_imprecise_dtypes=True).then_inc(consts, 1)
            nc.gpsimd.iota(count[:], [[1, SLOTS]], base=0, channel_multiplier=0,
                           allow_small_or_imprecise_dtypes=True).then_inc(consts, 1)
            nc.gpsimd.iota(entry[:], [[T, 2], [P, NT]], base=1, channel_multiplier=1,
                           allow_small_or_imprecise_dtypes=True).then_inc(consts, 1)
            for tt in range(NT):
                wait_read(pool, ("kv", tt))
                for at, width, dp, ds in ((SK, 128, k_prompt, k_sample), (SV, 128, v_prompt, v_sample),
                                          (SKI, 64, kidx_prompt, kidx_sample)):
                    if tt < SMP:
                        dst = dp[0, tt * P:(tt + 1) * P]
                    else:
                        dst = ds.rearrange("b q g d -> (b q) g d" if width == 128 else "b q d -> (b q) d")
                    if width == 128:
                        dst = dst.rearrange("t g d -> t (g d)")
                    pool.dma_start(dst, kvtm[:, tt, at:at + width]).then_inc(out_written, 16)
            wait_read(pool, ("qS", 1))
            pool.dma_start(q_spill[:, :, :], oT[:, :, 0:TP]).then_inc(S["q_spilled"], 16)
            for c in range(3):
                wait_read(pool, ("di", c))
            for i in range(2):
                link(nc.gpsimd.memset(raw[:, i, 0:3], 0.0))
            nc.gpsimd.memset(cgo[:, 0, 0:3], 0.0).then_inc(S["raw_zeroed"], 1)
            for g in range(GROUPS):
                for j in range(6):
                    u = 6 * g + j
                    pool.wait_ge(S["raw_ready"], u + 1)
                    if j == 0 and g:
                        wait_full(pool, ("cO", g - 1, 1))
                    nc.gpsimd.tensor_copy(cgo[:, j, 0:3], raw[:, u % 2, 512:515])
                    nc.gpsimd.tensor_copy(cgo[:, j, 3:27].rearrange("p (b r) -> p b r", r=3),
                                          raw[:, u % 2, 515:667].rearrange("p (b q) -> p b q", q=19)[:, :, 16:19]) \
                        .then_inc(S["gathered"], 1)
                wait_read(pool, ("bt", g, 1))
                if g:
                    wait_full(pool, ("sn", g - 1, 3, 1))
                nc.gpsimd.tensor_tensor(bms, btm[:, SMP:SMP + 1, :].broadcast_to([P, SB, NS]),
                                        stream[:].rearrange("p (b o) -> p b o", o=1).broadcast_to([P, SB, NS]),
                                        ALU.mult).then_inc(S["bms_ready"], 1)
                wait_read(pool, ("cO", g, 1))
                for at, n_, c in ((0, 4, 512 * g), (4, 1, INNER + NS * g), (5, 1, INNER + (GROUPS + g) * NS)):
                    pool.dma_start(conv_prompt[0, :, c:c + n_ * P].rearrange("r (c p) -> r c p", p=P),
                                   crow[0:3, at:at + n_, :]).then_inc(S["crow_written"], 16)
                    pool.dma_start(conv_sample[:, :, c:c + n_ * P].rearrange("b r (c p) -> (b r) c p", p=P),
                                   crow[3:27, at:at + n_, :]).then_inc(S["crow_written"], 16)
                wait_read(pool, ("so", g))
                pool.dma_start(ssm_prompt[0].rearrange("h p n -> (h p) n")[g * 512:(g + 1) * 512, :]
                               .rearrange("(j p) n -> p j n", p=P),
                               sout.rearrange("p (j n) -> p j n", n=NS)).then_inc(S["sout_written"], 16)
                for j in range(4):
                    u = 4 * g + j
                    wait_read(pool, ("sn", g, j, 1))
                    pool.dma_start(ssm_sample.rearrange("b h p n -> (h p) b n")[u * P:(u + 1) * P, :, :],
                                   st0[:, u % 3, :, :]).then_inc(st0_written[u % 3], 16)
                pool.wait_ge(S["y_gained"], g + 1)
                pool.dma_start(y_spill[:, 4 * g:4 * g + 4, :], yb[:, g % 2, :, :]).then_inc(S["y_spilled"], 16)
            wait_read(pool, ("ss", GROUPS - 1, 1))
            for i in range(3):
                pool.wait_ge(st0_written[i], 16 * ST0_USES[i])
            for s in range(SB):
                pool.dma_start(vnew[0:SQ, s, :], kvtm[SQ * s:SQ * (s + 1), SMP, SV:SV + P]) \
                    .then_inc(S["vnew_loaded"], 16)
            wait_read(pool, ("x1", NT - 1, 1))
            link(nc.gpsimd.memset(hg, 0.0))
            for tt in range(NT):
                pool.wait_ge(S["hx_scaled"], tt + 1)
                for c in range(2):
                    pool.dma_start(x_rows[c * T + tt * P:c * T + (tt + 1) * P, :], xn[:, tt, :]) \
                        .then_inc(S["xn_stored"], 16)
            pool.wait_ge(S["xn_stored"], 16 * 2 * NT)
            wait_full(pool, ("rt", NT - 1))
            for i in (2, 3):
                link(nc.gpsimd.memset(rows_in[i], 0.0))
            wait_read(pool, ("slots",))

            def gather(e):
                pool.indirect_dma_start(rows_in[e % 4][0:SLOTS, :], None, x_rows[:, :],
                                        bass.IndirectOffsetOnAxis(ap=slot_row[0:SLOTS, e:e + 1], axis=0),
                                        bounds_check=2 * T - 1, oob_is_err=False) \
                    .then_inc(gathered_rows[e % 4], 16)

            for e in range(4):
                gather(e)
            for e in range(NE):
                if e + 4 < NE:
                    pool.wait_ge(S["t_full"], e + 1)
                    gather(e + 4)
                pool.wait_ge(S["dn0_read"], e + 1)
                pool.wait_ge(S["dn1_read"], e + 1)
                pool.indirect_dma_start(y_rows[:, :],
                                        bass.IndirectOffsetOnAxis(ap=slot_row[0:SLOTS, e:e + 1], axis=0),
                                        ysl[0:SLOTS, e % 2, :], None, bounds_check=2 * T - 1, oob_is_err=False) \
                    .then_inc(pair["scattered"][e % 2], 16)
            for i in range(2):
                pool.wait_ge(pair["scattered"][i], 16 * NE // 2)
        def ssd_pe(pe, g, product, turn, prompt, sample):
            mm = nc.tensor.matmul
            pe.wait_ge(pair["cin_loaded"][0], 16 * 3 * (g + 1))
            o = claim(pe, ("cT", g))
            for j in range(6):
                ins = turn(o[:, 24 * j:24 * (j + 1)], cin[0:24, j, :], 24)
            filled(ins, ("cT", g))
            w = wait_chunk(pe, ("wx", g))
            o = claim(pe, ("xbcS", g, 0))
            for j in range(4):
                ins = product(o[:, j * P:(j + 1) * P], w, j * P, P, sample, P)
            filled(ins, ("xbcS", g, 0))
            for j in range(4):
                o = claim(pe, ("xbc", g, j))
                filled(product(o, w, j * P, P, prompt, TP), ("xbc", g, j))
            if g:
                squares_pe(pe, g - 1)
            w = wait_chunk(pe, ("wbc", g))
            o = claim(pe, ("xbcS", g, 1))
            for j in range(2):
                ins = product(o[:, j * P:(j + 1) * P], w, j * P, P, sample, P)
            filled(ins, ("xbcS", g, 1))
            for j in range(2):
                o = claim(pe, ("xbc", g, 4 + j))
                filled(product(o, w, j * P, P, prompt, TP), ("xbc", g, 4 + j))
            w = wait_chunk(pe, ("wz", g))
            for j in range(4):
                o = claim(pe, ("z", g, j))
                filled(product(o, w, j * P, P, prompt, TP), ("z", g, j))
            o = claim(pe, ("zS", g))
            for j in range(4):
                ins = product(o[:, j * P:(j + 1) * P], w, j * P, P, sample, P)
            filled(ins, ("zS", g))
            pe.wait_ge(S["gathered"], 6 * (g + 1))
            for c, js in ((0, range(4)), (1, range(4, 6))):
                o = claim(pe, ("cO", g, c))
                for j in js:
                    ins = turn(o[0:27, (j - js[0]) * P:(j - js[0] + 1) * P], cgo[:, j, :])
                filled(ins, ("cO", g, c))
            pe.wait_ge(S["xs_ready"], 6 * (g + 1))
            o = claim(pe, ("bt", g, 0))
            for tt in range(SMP):
                ins = turn(o[:, tt * P:(tt + 1) * P], bcT[:, 0, tt * P:(tt + 1) * P])
            filled(ins, ("bt", g, 0))
            o = claim(pe, ("bt", g, 1))
            filled(turn(o[:, 0:P], bcT[:, 0, TP:T]), ("bt", g, 1))
            for tt in range(NT):
                tok = slice(tt * P, (tt + 1) * P)
                cum = (cum_p if tt < SMP else cum_s)[:]
                o = claim(pe, ("xt", g, tt))
                for j in range(4):
                    ins = turn(o[:, j * P:(j + 1) * P], xsT[:, j, tok])
                filled(ins, ("xt", g, tt))
                o = claim(pe, ("cb", g, tt))
                filled(mm(o[:, 0:P], bcT[:, 0, tok], bcT[:, 1, tok], start=True, stop=True), ("cb", g, tt))
                for i in range(2):
                    o = claim(pe, ("sg", g, tt, i))
                    for h in range(4):
                        hd = HG * g + 4 * i + h
                        ins = mm(o[:, h * P:(h + 1) * P], av[:, tt, hd:hd + 1].broadcast_to([P, P]), cum,
                                 start=True, stop=True)
                    filled(ins, ("sg", g, tt, i))
                o = claim(pe, ("eb", g, tt))
                for h in range(HG):
                    hd = HG * g + h
                    ins = mm(o[HP * (h % 2):HP * (h % 2) + HP, (h // 2) * P:(h // 2 + 1) * P],
                             av[:, tt, hd:hd + 1].broadcast_to([P, HP]), cum, start=True, stop=True)
                filled(ins, ("eb", g, tt))
                if 0 < tt < SMP:
                    wait_read(pe, ("st", g, tt - 1))
                    o = claim(pe, ("yi", g, tt))
                    for j in range(4):
                        ins = mm(o[:, j * P:(j + 1) * P], stT[:, j * P:(j + 1) * P], bcT[:, 1, tok], start=True, stop=True)
                    filled(ins, ("yi", g, tt))
                wait_read(pe, ("xt", g, tt))
                if tt < SMP:
                    wait_read(pe, ("bt", g, 1))
                    o = claim(pe, ("st", g, tt))
                    filled(mm(o, btm[:, tt, :], xw[:, tt % 2, :], start=True, stop=True), ("st", g, tt))
                o = claim(pe, ("yo", g, tt))
                for i in range(2):
                    pe.wait_ge(S["mt_ready"], 2 * (NT * g + tt) + i + 1)
                    m = mt[:, (2 * (NT * g + tt) + i) % 3, :]
                    for h in range(4 * i, 4 * i + 4):
                        ins = mm(o[HP * (h % 2):HP * (h % 2) + HP, (h // 2) * P:(h // 2 + 1) * P],
                                 xdt[:, tt % 2, HP * h:HP * (h + 1)], m[:, (h % 4) * P:(h % 4 + 1) * P],
                                 start=True, stop=True)
                filled(ins, ("yo", g, tt))
            wait_read(pe, ("st", g, SMP - 1))
            o = claim(pe, ("so", g))
            for j in range(4):
                ins = turn(o[:, j * P:(j + 1) * P], stT[:, j * P:(j + 1) * P])
            filled(ins, ("so", g))
            pe.wait_ge(S["bms_ready"], g + 1)
            for j in range(4):
                u = 4 * g + j
                pe.wait_ge(st0_loaded[u % 3], 16 * (u // 3 + 1))
                for i in range(2):
                    o = claim(pe, ("s0", g, j, i))
                    for b in range(4):
                        ins = turn(o[:, b * P:(b + 1) * P], st0[:, u % 3, 4 * i + b, :])
                    filled(ins, ("s0", g, j, i))
                for i in range(2):
                    o = claim(pe, ("sn", g, j, i))
                    filled(mm(o, xw[:, 0, j * P:(j + 1) * P], bms[:, 4 * i:4 * i + 4, :].rearrange("p b n -> p (b n)"),
                              start=True, stop=True), ("sn", g, j, i))
                wait_read(pe, ("s0", g, j, 1))
                o = claim(pe, ("ys", g, j))
                for b in range(SB):
                    ins = mm(o[:, b * SQ:(b + 1) * SQ], s0T[:, b, :], bcT[:, 1, TP + b * SQ:TP + (b + 1) * SQ],
                             start=True, stop=True)
                filled(ins, ("ys", g, j))
            if g == GROUPS - 1:
                squares_pe(pe, g)

        def squares_pe(pe, g):
            mm = nc.tensor.matmul
            pe.wait_ge(S["y_squares"], g + 1)
            for i, (a, b) in enumerate(((0, TP), (TP, T))):
                o = claim(pe, ("ss", g, i))
                for j in range(4):
                    ins = mm(o[:, 0:b - a], ones[:], zT[:, j, a:b], start=j == 0, stop=j == 3)
                filled(ins, ("ss", g, i))

        def attention_pe(pe, turn):
            mm = nc.tensor.matmul
            pe.wait_ge(S["kz_ready"], 1)
            for i in range(SMP):
                n = P * (i + 1)
                for k in range(AH + 3):
                    if k < AH:
                        t, g = k // AKV, k % AKV
                        o = claim(pe, ("s", i, k))
                        filled(mm(o[:, 0:n], oT[:, t, i * P:(i + 1) * P], kz[:, g, 0:n], start=True, stop=True),
                               ("s", i, k))
                    if 2 <= k < AH + 2:
                        u = AH * i + k - 2
                        pe.wait_ge(S["p_scaled"], u + 1)
                        o = claim(pe, ("pT", i, k - 2))
                        for c in range(i + 1):
                            ins = turn(o[:, c * P:(c + 1) * P], sm[:, u % 3, c * P:(c + 1) * P])
                        filled(ins, ("pT", i, k - 2))
                    if k >= 3:
                        u = AH * i + k - 3
                        t, g = (k - 3) // AKV, (k - 3) % AKV
                        half = (k - 3) // AR
                        if (k - 3) % AR == 0:
                            oo = claim(pe, ("o", i, half))
                        wait_read(pe, ("pT", i, k - 3))
                        for c in range(i + 1):
                            ins = mm(oo[HD * g:HD * (g + 1), (t % 4) * P:(t % 4 + 1) * P],
                                     kvtm[:, c, SV + g * HD:SV + (g + 1) * HD], pT[:, u % 2, c * P:(c + 1) * P],
                                     start=c == 0, stop=c == i)
                        if (k - 3) % AR == AR - 1:
                            filled(ins, ("o", i, half))
            pe.wait_ge(S["kz_ready"], 2)
            for s in range(SB + 1):
                if s < SB:
                    pe.wait_ge(pair["kb_loaded"][s % 2], 16 * (s // 2 + 1))
                    for c in range(2):
                        o = claim(pe, ("kc", s, c))
                        for j in range(4):
                            ins = turn(o[:, j * P:(j + 1) * P], kb[:, s % 2, 4 * c + j, :])
                        filled(ins, ("kc", s, c))
                    wait_read(pe, ("kc", s, 0))
                    wait_read(pe, ("kc", s, 1))
                    for g in range(AKV):
                        claim(pe, ("ds", s, g))
                        o = bank(("ds", s, g), 3)[:, 0:KEYS]
                        for c in range(3):
                            a, b = c * 512, min((c + 1) * 512, KEYS)
                            rhs = kcT[:, s % 2, a:b] if c < 2 else kT[:, TP + s * SQ:TP + (s + 1) * SQ]
                            ins = mm(o[:, a:b], qz[:, s, g, :], rhs, start=True, stop=True)
                        filled(ins, ("ds", s, g))
                if s < 1:
                    continue
                b = s - 1
                for g in range(AKV):
                    u = AKV * b + g
                    pe.wait_ge(S["p_scaled"], AH * SMP + u + 1)
                    for c in range(3):
                        o = claim(pe, ("pt", b, g, c))
                        if c < 2:
                            pj = pexp[:, u % 2, 0:PAST].rearrange("p (k j) -> p j k", j=KJ)
                            for j in range(4):
                                ins = turn(o[:, j * P:(j + 1) * P], pj[:, 4 * c + j, :])
                        else:
                            ins = turn(o[0:SQ, 0:P], pexp[:, u % 2, PAST:KEYS])
                        filled(ins, ("pt", b, g, c))
                pe.wait_ge(pair["vb_loaded"][b % 2], 16 * (b // 2 + 1))
                if b == 0:
                    pe.wait_ge(S["vnew_loaded"], 16 * SB)
                o = claim(pe, ("do", b))
                for g in range(AKV):
                    u = AKV * b + g
                    for c in range(3):
                        wait_read(pe, ("pt", b, g, c))
                    cols_ = slice(g * HD, (g + 1) * HD)
                    for j in range(KJ):
                        mm(o[cols_, 0:P], vb[:, b % 2, j, cols_], ptS[:, u % 2, j, :], start=j == 0, stop=False)
                    ins = mm(o[cols_, 0:P], vnew[0:SQ, b, cols_], ptN[0:SQ, u % 2, :], start=False, stop=True)
                filled(ins, ("do", b))

        @block.tensor
        def _(pe):
            mm = nc.tensor.matmul

            def product(out, chunk, m0, m, rhs, n, ks=KD, first=True, last=True):
                for k in range(ks):
                    ins = mm(out, chunk[:, k, m0:m0 + m], rhs(k), start=first and k == 0, stop=last and k == ks - 1)
                return ins

            def turn(out, in_, rows=P):
                return nc.tensor.transpose(out, in_, ident[0:rows, 0:rows])

            prompt = lambda k: hT[:, k, 0:TP]
            sample = lambda k: hT[:, k, TP:T]

            pe.wait_ge(consts, 3)
            pe.wait_ge(params_loaded, 16 * 5)
            o = claim(pe, ("par", 0))
            filled(turn(o[:, 0:P], par[:, 0, :]), ("par", 0))
            o = claim(pe, ("par", 1))
            filled(turn(o[:, 0:24], par[0:24, 1, :], 24), ("par", 1))
            for tt in range(NT):
                pe.wait_ge(S["x_scaled"], tt + 1)
                for c in range(2):
                    o = claim(pe, ("hT", tt, c))
                    for k in range(4):
                        ins = turn(o[:, k * P:(k + 1) * P], xtm[:, tt, (4 * c + k) * P:(4 * c + k + 1) * P])
                    filled(ins, ("hT", tt, c))
            wait_read(pe, ("hT", NT - 1, 1))
            w = wait_chunk(pe, ("small",))
            for tt in range(NT):
                o = claim(pe, ("kv", tt))
                for k in range(KD):
                    ins = mm(o[:, 0:SW], hT[:, k, tt * P:(tt + 1) * P], w[:, k, 0:SW], start=k == 0, stop=k == KD - 1)
                filled(ins, ("kv", tt))
            ins.then_inc if False else None
            for c in range(2):
                w = wait_chunk(pe, ("wq", c))
                for t in range(4):
                    o = claim(pe, ("q", 4 * c + t))
                    filled(product(o, w, t * P, P, prompt, TP), ("q", 4 * c + t))
                o = claim(pe, ("qS", c))
                for t in range(4):
                    ins = product(o[:, t * P:(t + 1) * P], w, t * P, P, sample, P)
                filled(ins, ("qS", c))
            w = wait_chunk(pe, ("wqi",))
            for t in range(4):
                o = claim(pe, ("qi", t))
                filled(product(o, w, t * P, P, prompt, TP), ("qi", t))
            o = claim(pe, ("qiS",))
            for t in range(4):
                ins = product(o[:, t * P:(t + 1) * P], w, t * P, P, sample, P)
            filled(ins, ("qiS",))
            wait_read(pe, ("kv", NT - 1))
            o = claim(pe, ("kT", 0))
            for tt in range(SMP):
                ins = turn(o[:, tt * P:(tt + 1) * P], kvtm[:, tt, SK:SK + P])
            filled(ins, ("kT", 0))
            o = claim(pe, ("kT", 1))
            filled(turn(o[:, 0:P], kvtm[:, SMP, SK:SK + P]), ("kT", 1))
            o = claim(pe, ("kT", 2))
            for tt in range(SMP):
                ins = turn(o[0:HD, tt * P:(tt + 1) * P], kvtm[:, tt, SKI:SKI + IDIM])
            filled(ins, ("kT", 2))
            o = claim(pe, ("kT", 3))
            filled(turn(o[0:HD, 0:P], kvtm[:, SMP, SKI:SKI + IDIM]), ("kT", 3))
            wait_read(pe, ("kT", 3))
            for i in range(1, 4):
                for h in range(IH):
                    o = claim(pe, ("pd", i, h))
                    filled(mm(o[:, 0:P * (i + 1)], qiT[0:HD, h, i * P:(i + 1) * P], kiT[0:HD, 0:P * (i + 1)],
                              start=True, stop=True), ("pd", i, h))
            pe.wait_ge(S["wl_ready"], 1)
            o = claim(pe, ("wc",))
            filled(mm(o[:, 0:SB], wl, stream[:], start=True, stop=True), ("wc",))
            di = [claim(pe, ("di", i)) for i in range(3)]
            pe.wait_ge(S["wsel_ready"], 1)
            for s in range(SB + 2):
                if s < SB:
                    pe.wait_ge(pair["kx_loaded"][s % 2], 16 * (s // 2 + 1))
                    for c in range(2):
                        o = claim(pe, ("kx", s, c))
                        for j in range(4):
                            ins = turn(o[0:IDIM, j * P:(j + 1) * P], kx_in[:, s % 2, 4 * c + j, :])
                        filled(ins, ("kx", s, c))
                if 1 <= s <= SB:
                    b = s - 1
                    wait_read(pe, ("kx", b, 0))
                    wait_read(pe, ("kx", b, 1))
                    for c in range(3):
                        o = claim(pe, ("dd", b, c))
                        rhs = kxT[0:IDIM, b % 2, c * 512:(c + 1) * 512] if c < 2 else \
                            kiT[0:IDIM, TP + b * SQ:TP + (b + 1) * SQ]
                        filled(mm(o[:, 0:rhs.shape[1]], qis[0:HD, b].rearrange("d h q -> d (h q)"), rhs,
                                  start=True, stop=True), ("dd", b, c))
                if s >= 2:
                    b = s - 2
                    wait_read(pe, ("dd", b, 2))
                    for c in range(3):
                        w_ = 512 if c < 2 else SQ
                        ins = mm(di[c][:, 0:w_], wsel[:, b, :], rel[:, b % 2, c * 512:c * 512 + w_],
                                 start=b == 0, stop=b == SB - 1, skip_group_check=True)
                        if b == SB - 1:
                            filled(ins, ("di", c))
            pe.wait_ge(S["a_ready"], 1)
            for tt in range(NT):
                o = claim(pe, ("ac", tt))
                filled(mm(o[:, 0:HEADS], (cum_p if tt < SMP else cum_s)[:], av[:, tt, :], start=True, stop=True), ("ac", tt))
                o = claim(pe, ("ae", tt))
                filled(mm(o[:, 0:HEADS], (ones if tt < SMP else same)[:], av[:, tt, :], start=True, stop=True), ("ae", tt))
            for g in range(GROUPS):
                ssd_pe(pe, g, product, turn, prompt, sample)
            attention_pe(pe, turn)
            for n in range(2):
                for what in ("ga", "gb", "a", "b"):
                    if what[0] == "g":
                        ws = [wait_chunk(pe, ("w" + what, n))]
                        rp, rs = [prompt], [sample]
                    elif what == "a":
                        ws = [wait_chunk(pe, ("wso", n, c)) for c in range(2)]
                        rp = [lambda k: yz[:, k, 0:TP], lambda k: yz[:, 8 + k, 0:TP]]
                        rs = [lambda k: yz[:, k, TP:T], lambda k: yz[:, 8 + k, TP:T]]
                        pe.wait_ge(S["y_back"], 16)
                    else:
                        ws = [wait_chunk(pe, ("wao", n))]
                        rp, rs = [lambda k: oT[:, k, 0:TP]], [lambda k: oT[:, k, TP:T]]
                        wait_read(pe, ("do", SB - 1))
                    for j in range(4):
                        o = claim(pe, (what, n, j))
                        for i, w in enumerate(ws):
                            ins = product(o, w, j * P, P, rp[i], TP, first=i == 0, last=i == len(ws) - 1)
                        filled(ins, (what, n, j))
                    o = claim(pe, (what + "S", n))
                    for j in range(4):
                        for i, w in enumerate(ws):
                            ins = product(o[:, j * P:(j + 1) * P], w, j * P, P, rs[i], P, first=i == 0,
                                          last=i == len(ws) - 1)
                    filled(ins, (what + "S", n))
            ws = [wait_chunk(pe, ("wo", n)) for n in range(2)]
            pe.wait_ge(S["m_ready"], 2)
            for tt in range(NT):
                for n in range(2):
                    o = claim(pe, ("x1", tt, n))
                    for k in range(KD):
                        ins = mm(o, mrg[:, k, tt * P:(tt + 1) * P], ws[n][:, k, :], start=k == 0, stop=k == KD - 1)
                    filled(ins, ("x1", tt, n))
            for tt in range(NT):
                pe.wait_ge(S["hx_scaled"], tt + 1)
                for c in range(2):
                    o = claim(pe, ("h2", tt, c))
                    for k in range(4):
                        ins = turn(o[:, k * P:(k + 1) * P], xn[:, tt, (4 * c + k) * P:(4 * c + k + 1) * P])
                    filled(ins, ("h2", tt, c))
            pe.wait_ge(S["router_loaded"], 32)
            for tt in range(NT):
                wait_read(pe, ("h2", tt, 1))
                o = claim(pe, ("rt", tt))
                for k in range(KD):
                    ins = mm(o[:, 0:MG + NE], h2T[:, k, tt * P:(tt + 1) * P], wr[:, k, :], start=k == 0, stop=k == KD - 1)
                filled(ins, ("rt", tt))
            pe.wait_ge(S["hot_ready"], 1)
            o = claim(pe, ("rank",))
            for tt in range(NT):
                for t in range(tt):
                    mm(o[:, tt * NE:(tt + 1) * NE], ones[:], cnt[:, t, :], start=t == 0, stop=False)
                mm(o[:, tt * NE:(tt + 1) * NE], cum_p[:], cnt[:, tt, :], start=tt == 0, stop=True)
            for t in range(NT):
                ins = mm(o[:, NT * NE:(NT + 1) * NE], ones[:], cnt[:, t, :], start=t == 0, stop=t == NT - 1)
            filled(ins, ("rank",))
            o = claim(pe, ("slots",))
            for i in range(2 * NT):
                pe.wait_ge(S["at_ready"], i + 1)
                ins = mm(o[0:SLOTS, 0:NB], at_pos[:, i % 2, :], at_blk[:, i % 2, :], start=i == 0, stop=i == 2 * NT - 1)
                if i < 2 * NT - 1:
                    ins.then_inc(S["at_used"], 1)
            filled(ins, ("slots",))
            for b in range(8):
                pe.wait_ge(free[b], banks.free[b])

            def turned(e):
                pe.wait_ge(gathered_rows[e % 4], 16 * (e // 4 + 1))
                if e >= 2:
                    pe.wait_ge(S["t_read"], e - 1)
                o = pbank(e % 2)
                for k in range(KD):
                    ins = nc.tensor.transpose(o[:, k * SLOTS:(k + 1) * SLOTS], rows_in[e % 4][0:SLOTS, k * P:(k + 1) * P],
                                              ident[0:SLOTS, 0:SLOTS])
                ins.then_inc(S["t_full"], 1)

            def up(e):
                pe.wait_ge(S["t_read"], e + 1)
                pe.wait_ge(w13_loaded[e % 4], 32 * (e // 4 + 1))
                if e >= 2:
                    pe.wait_ge(S["heT_ready"], e - 1)
                for k in range(KD):
                    ins = mm(pbank(2 + e % 2)[0:SLOTS, :], hgT[:, e % 2, k, :], w13[e % 4][:, k, :], start=k == 0,
                             stop=k == KD - 1)
                ins.then_inc(S["up_full"], 1)

            def hidden_turned(e):
                pe.wait_ge(S["he_ready"], e + 1)
                for k in range(2):
                    ins = nc.tensor.transpose(pbank(2 + e % 2)[:, k * SLOTS:(k + 1) * SLOTS],
                                              hetm[0:SLOTS, e % 2, k * P:(k + 1) * P], ident[0:SLOTS, 0:SLOTS])
                ins.then_inc(S["heT_full"], 1)

            def down(e):
                pe.wait_ge(S["heT_ready"], e + 1)
                pe.wait_ge(w2_loaded[e % 4], 16 * (e // 4 + 1))
                if e >= 2:
                    pe.wait_ge(S["dn0_read"], e - 1)
                    pe.wait_ge(S["dn1_read"], e - 1)
                for m in range(2):
                    for k in range(2):
                        ins = mm(pbank(4 + 2 * (e % 2) + m)[0:SLOTS, :], heT[:, e % 2, k, :],
                                 w2s[e % 4][:, k, 512 * m:512 * m + 512], start=k == 0, stop=k == 1)
                    ins.then_inc(S["dn0_full" if m == 0 else "dn1_full"], 1)

            turned(0)
            turned(1)
            up(0)
            hidden_turned(0)
            for e in range(NE):
                if e + 2 < NE:
                    turned(e + 2)
                if e + 1 < NE:
                    up(e + 1)
                down(e)
                if e + 1 < NE:
                    hidden_turned(e + 1)

        def ssd_act(act, g, fn, copy):
            if g:
                act.wait_ge(S["y_gated"], g)
            copy(("cT", g), cst, bank(("cT", g))[:, 0:144].rearrange("p (j r) -> p j r", r=24))
            for j in range(7):
                if j < 6:
                    u = 6 * g + j
                    r = raw[:, u % 2, :]
                    rsm = r[:, 515:667].rearrange("p (b q) -> p b q", q=19)
                    if u < 2:
                        act.wait_ge(S["raw_zeroed"], 1)
                    else:
                        act.wait_ge(S["conv_done"], u - 1)
                        act.wait_ge(S["gathered"], u - 1)
                    c = j // 4
                    copy(("xbc", g, j), r[:, 3:515], bank(("xbc", g, j)))
                    wait_full(act, ("xbcS", g, c))
                    ins = fn(rsm[:, :, 3:19], bank(("xbcS", g, c))[:, (j - 4 * c) * P:(j - 4 * c + 1) * P]
                             .rearrange("p (b q) -> p b q", q=SQ), ACT.Copy)
                    if j in (3, 5):
                        release(ins, ("xbcS", g, c))
                    wait_read(act, ("cT", g))
                    fn(rsm[:, :, 0:3], cst[:, j, :].rearrange("p (b r) -> p b r", r=3), ACT.Copy) \
                        .then_inc(S["raw_ready"], 1)
                if j > 0:
                    u = 6 * g + j - 1
                    ct = 4 * g + j - 1 if j < 5 else 16 + g if j == 5 else 20 + g
                    dst = xsT[:, j - 1, :] if j < 5 else bcT[:, j - 5, :]
                    act.wait_ge(S["conv_done"], u + 1)
                    fn(dst[:, 0:TP], acc[:, 0, 0:TP], ACT.Silu, bias=cb_col[:, ct:ct + 1])
                    fn(dst[:, TP:T].rearrange("p (b q) -> p b q", q=SQ),
                       acc[:, 0, 512:664].rearrange("p (b q) -> p b q", q=19)[:, :, 3:19], ACT.Silu,
                       bias=cb_col[:, ct:ct + 1]).then_inc(S["xs_ready"], 1)
            if g:
                wait_full(act, ("ss", g - 1, 1))
            for j in range(4):
                wait_full(act, ("z", g, j))
                release(fn(zT[:, j, 0:TP], bank(("z", g, j)), ACT.Silu), ("z", g, j))
            wait_full(act, ("zS", g))
            release(fn(zT[:, :, TP:T], bank(("zS", g)).rearrange("p (j q) -> p j q", j=4), ACT.Silu), ("zS", g))
            if g:
                act.wait_ge(S["crow_written"], 96 * g)
            for c, w in ((0, 4), (1, 2)):
                copy(("cO", g, c), crow[0:27, 4 * c:4 * c + w, :],
                     bank(("cO", g, c))[0:27, 0:w * P].rearrange("p (j n) -> p j n", n=P))
            if g:
                act.wait_ge(S["bms_ready"], g)
            copy(("bt", g, 0), btm[:, 0:4, :], bank(("bt", g, 0)).rearrange("p (t n) -> p t n", n=P))
            copy(("bt", g, 1), btm[:, SMP, :], bank(("bt", g, 1))[:, 0:P])
            for tt in range(NT):
                k = NT * g + tt
                if k >= 2:
                    act.wait_ge(S["mt_ready"], 2 * (k - 1))
                copy(("cb", g, tt), cbs[:, k % 2, :], bank(("cb", g, tt))[:, 0:P])
                for i in range(2):
                    u = 2 * k + i
                    wait_read(act, ("sg", g, tt, i))
                    m = mt[:, u % 3, :]
                    for h in range(4):
                        hd = HG * g + 4 * i + h
                        ins = fn(m[:, h * P:(h + 1) * P], m[:, h * P:(h + 1) * P], ACT.Exp, bias=nac[:, tt, hd:hd + 1])
                    ins.then_inc(S["mt_exp"], 1)
                wait_full(act, ("eb", g, tt))
                if tt >= 2:
                    wait_read(act, ("yo", g, tt - 2))
                elif g:
                    wait_read(act, ("yo", g - 1, tt + 3))
                release(fn(ebs[:, k % 2, :], bank(("eb", g, tt)), ACT.Exp), ("eb", g, tt))
            if g:
                act.wait_ge(S["sout_written"], 16 * g)
            copy(("so", g), sout, bank(("so", g)))
            for j in range(4):
                for i in range(2):
                    if (g or j) and i == 0:
                        wait_full(act, ("ys", g, j - 1) if j else ("ys", g - 1, 3))
                    copy(("s0", g, j, i), s0T[:, 4 * i:4 * i + 4, :],
                         bank(("s0", g, j, i)).rearrange("p (b q) -> p b q", b=4))
            act.wait_ge(S["y_gated"], g + 1)
            fn(zT, yb[:, g % 2, :, :], ACT.Square).then_inc(S["y_squares"], 1)
            act.wait_ge(S["y_squares"], g + 1)
            for j in range(4):
                ins = fn(yb[:, g % 2, j, :], yb[:, g % 2, j, :], ACT.Copy, scale=gssm[:, 4 * g + j:4 * g + j + 1])
            ins.then_inc(S["y_gained"], 1)

        @block.scalar
        def _(act):
            n = [0]

            def link(ins):
                n[0] += 1
                ins.then_inc(act_chain, 1)
                act.wait_ge(act_chain, n[0])

            fn = nc.scalar.activation

            def copy(key, out, in_):
                wait_full(act, key)
                release(fn(out, in_, ACT.Copy), key)

            copy(("par", 0), pc[:, 0, :], bank(("par", 0))[:, 0:P])
            copy(("par", 1), pc[:, 1, 0:24], bank(("par", 1))[:, 0:24])
            act.wait_ge(rows_loaded, 16 * 5)
            fn(a_row[:], a_row[:], ACT.Exp).then_inc(S["a_row_ready"], 1)
            for tt in range(NT):
                act.wait_ge(x_loaded[tt], 16)
                if tt:
                    act.wait_ge(S["x_squares"], tt)
                fn(junk, xtm[:, tt, :], ACT.Square, accum_out=ssq[:, 0, tt:tt + 1]).then_inc(S["x_squares"], 1)
            act.wait_ge(S["x_var"], 1)
            fn(ssq[:, 1, 0:NT], ssq[:, 0, 0:NT], ACT.Sqrt).then_inc(S["x_std"], 1)
            for tt in range(NT):
                copy(("kv", tt), kvtm[:, tt, :], bank(("kv", tt))[:, 0:SW])
            for c in range(2):
                for t in range(4 * c, 4 * c + 4):
                    copy(("q", t), oT[:, t, 0:TP], bank(("q", t)))
                wait_full(act, ("qS", c))
                for t in range(4):
                    ins = fn(qs[:, :, 4 * c + t, :],
                             bank(("qS", c))[:, t * P:(t + 1) * P].rearrange("p (b q) -> p b q", q=SQ), ACT.Copy)
                release(ins, ("qS", c))
            for t in range(4):
                wait_full(act, ("qi", t))
                fn(qiT[0:HD, 2 * t, :], bank(("qi", t))[0:HD, :], ACT.Copy)
                release(fn(qiT[0:HD, 2 * t + 1, :], bank(("qi", t))[HD:P, :], ACT.Copy), ("qi", t))
            wait_full(act, ("qiS",))
            for h in range(IH):
                ins = fn(qis[0:HD, :, h, :],
                         bank(("qiS",))[HD * (h % 2):HD * (h % 2) + HD, (h // 2) * P:(h // 2 + 1) * P]
                         .rearrange("p (b q) -> p b q", q=SQ), ACT.Copy)
            release(ins, ("qiS",))
            copy(("kT", 0), kT[:, 0:TP], bank(("kT", 0)))
            copy(("kT", 1), kT[:, TP:T], bank(("kT", 1))[:, 0:P])
            copy(("kT", 2), kiT[0:HD, 0:TP], bank(("kT", 2))[0:HD, :])
            copy(("kT", 3), kiT[0:HD, TP:T], bank(("kT", 3))[0:HD, 0:P])
            for i in range(1, 4):
                for h in range(IH):
                    u, w = IH * (i - 1) + h, P * (i + 1)
                    wait_full(act, ("pd", i, h))
                    if u >= 2:
                        act.wait_ge(S["rel_used"], u - 1)
                    release(fn(rel[:, u % 2, 0:w], bank(("pd", i, h))[:, 0:w], ACT.Relu), ("pd", i, h))
            copy(("wc",), wcol, bank(("wc",))[:, 0:SB])
            act.wait_ge(S["rel_used"], 3 * IH)
            for s in range(SB + 1):
                if s < SB:
                    for c in range(2):
                        copy(("kx", s, c), kxT[0:IDIM, s % 2, :].rearrange("d (p j) -> d j p", j=KJ)[:, 4 * c:4 * c + 4, :],
                             bank(("kx", s, c))[0:IDIM, :].rearrange("d (j p) -> d j p", j=4))
                if s >= 1:
                    b = s - 1
                    for c in range(3):
                        w = 512 if c < 2 else SQ
                        wait_full(act, ("dd", b, c))
                        release(fn(rel[:, b % 2, 512 * c:512 * c + w], bank(("dd", b, c))[:, 0:w], ACT.Relu), ("dd", b, c))
            act.wait_ge(S["dt_exp"], 1)
            fn(w2v, w2v, ACT.Exp, scale=-1.0).then_inc(S["a_exp"], 1)
            for tt in range(NT):
                wait_read(act, ("ae", tt), 1)
                release(fn(expae[:, tt, :], bank(("ae", tt))[:, 0:HEADS], ACT.Exp), ("ae", tt))
            act.wait_ge(S["ae_ready"], 1)
            fn(w2v, w2v, ACT.Exp).then_inc(S["a_exp"], 1)
            for g in range(GROUPS):
                ssd_act(act, g, fn, copy)
            for i in range(SMP):
                w = P * (i + 1)
                for k in range(AH + 3):
                    if k < AH:
                        u = AH * i + k
                        wait_read(act, ("s", i, k))
                        fn(sm[:, u % 3, 0:w], sm[:, u % 3, 0:w], ACT.Exp, bias=mx[:, u % 8:u % 8 + 1], scale=-1.0,
                           accum_out=rsum[:, u % 8:u % 8 + 1]).then_inc(S["at_exp"], 1)
                    if 2 <= k < AH + 2:
                        u = AH * i + k - 2
                        copy(("pT", i, k - 2), pT[:, u % 2, 0:w], bank(("pT", i, k - 2))[:, 0:w])
                    if k >= 3 and (k - 3) % AR == AR - 1:
                        c = (k - 3) // AR
                        copy(("o", i, c), oT[:, 4 * c:4 * c + 4, i * P:(i + 1) * P],
                             bank(("o", i, c)).rearrange("p (t q) -> p t q", t=4))
            for s in range(SB + 1):
                if s < SB:
                    copy(("kc", s, 1), kcT[:, s % 2, :].rearrange("d (p j) -> d j p", j=KJ)[:, 4:8, :],
                         bank(("kc", s, 1)).rearrange("d (j p) -> d j p", j=4))
                for g in range(AKV):
                    u = AKV * s + g
                    if s >= 1:
                        copy(("pt", s - 1, g, 1), ptS[:, u % 2, 4:8, :],
                             bank(("pt", s - 1, g, 1)).rearrange("p (j q) -> p j q", j=4))
                        copy(("pt", s - 1, g, 2), ptN[0:SQ, u % 2, :], bank(("pt", s - 1, g, 2))[0:SQ, 0:P])
                    if s < SB:
                        v = AH * SMP + u
                        wait_read(act, ("ds", s, g))
                        fn(pexp[:, u % 2, :], pexp[:, u % 2, :], ACT.Exp, bias=mx[:, v % 8:v % 8 + 1], scale=-1.0,
                           accum_out=rsum[:, v % 8:v % 8 + 1]).then_inc(S["at_exp"], 1)
                if s >= 1:
                    copy(("do", s - 1), oT[:, :, TP + (s - 1) * SQ:TP + s * SQ],
                         bank(("do", s - 1))[:, 0:P].rearrange("p (t q) -> p t q", q=SQ))
            act.wait_ge(S["ss_var"], 1)
            fn(rt, rt, ACT.Sqrt).then_inc(S["ss_std"], 1)
            for m in range(2):
                for i, what in enumerate(("ga", "gb")):
                    if m:
                        wait_read(act, (("aS", "bS")[i], 0))
                    if m:
                        act.wait_ge(S["m_ready"], 1)
                    for j in range(4):
                        wait_full(act, (what, m, j))
                        release(fn(gate[:, i, j, 0:TP], bank((what, m, j)), ACT.Sigmoid), (what, m, j))
                    wait_full(act, (what + "S", m))
                    release(fn(gate[:, i, :, TP:T], bank((what + "S", m)).rearrange("p (j q) -> p j q", j=4),
                               ACT.Sigmoid), (what + "S", m))
            for tt in range(NT):
                wait_read(act, ("x1", tt, 1))
                fn(xn[:, tt, :], x1[:, tt, :], ACT.Square, accum_out=ssq[:, 2, tt:tt + 1]).then_inc(S["hx_squares"], 1)
            act.wait_ge(S["hx_var"], 1)
            fn(ssq[:, 3, 0:NT], ssq[:, 2, 0:NT], ACT.Sqrt).then_inc(S["hx_std"], 1)
            for i in range(2):
                act.wait_ge(S["r_exp_in"], i + 1)
                e = rc[2] if i == 0 else rs1[:, 4, :]
                fn(e, e, ACT.Exp).then_inc(S["r_exp"], 1)
            for e in range(-1, NE):
                if e + 1 < NE:
                    u = e + 1
                    act.wait_ge(S["up_full"], u + 1)
                    fn(hsil[0:SLOTS, u % 2], pbank(2 + u % 2)[0:SLOTS, 0:FF], ACT.Silu) \
                        .then_inc(S["silu_ready"], 1)
                    act.wait_ge(S["heT_full"], u + 1)
                    fn(heT[:, u % 2], pbank(2 + u % 2)[:, 0:2 * SLOTS].rearrange("p (j q) -> p j q", j=2), ACT.Copy) \
                        .then_inc(S["heT_ready"], 1)
                if e >= 0:
                    act.wait_ge(S["dn0_full"], e + 1)
                    if e >= 2:
                        act.wait_ge(pair["scattered"][e % 2], 16 * (e // 2))
                    fn(ysl[0:SLOTS, e % 2, 0:512], pbank(4 + 2 * (e % 2))[0:SLOTS, :], ACT.Copy).then_inc(S["dn0_read"], 1)

        def ssd_dve(dve, g, link, over, top):
            tt_, ts_, stt = nc.vector.tensor_tensor, nc.vector.tensor_scalar, nc.vector.scalar_tensor_tensor
            heads = slice(HG * g, HG * (g + 1))
            y = yb[:, g % 2, :, :]
            for j in range(6):
                u = 6 * g + j
                ct = 4 * g + j if j < 4 else 16 + g if j == 4 else 20 + g
                dve.wait_ge(S["raw_ready"], u + 1)
                if u:
                    dve.wait_ge(S["xs_ready"], u)
                a, r = acc[:, 0, :], raw[:, u % 2, :]
                link(ts_(a, r[:, 0:664], cw_col[:, 0, ct:ct + 1], None, ALU.mult))
                for w in range(1, CW):
                    ins = stt(out=a, in0=r[:, w:w + 664], scalar=cw_col[:, w, ct:ct + 1], in1=a, op0=ALU.mult, op1=ALU.add)
                    if w < CW - 1:
                        link(ins)
                ins.then_inc(S["conv_done"], 1)
                if j == 3 and g:
                    squares_dve(dve, g - 1)
                top(24 * g + 4 * j, 24 * g + 4 * j + 4)
            for tt in range(NT):
                k = NT * g + tt
                wait_full(dve, ("xt", g, tt))
                if tt >= 2:
                    wait_full(dve, ("yo", g, tt - 2))
                elif tt == 0 and g:
                    wait_full(dve, ("ys", g - 1, 3))
                xp = bank(("xt", g, tt)).rearrange("p (h d) -> p h d", d=HP)
                tt_(xdt[:, tt % 2, :].rearrange("p (h d) -> p h d", d=HP), xp, over(dtv[:, tt, heads], HP), ALU.mult)
                release(tt_(xw[:, tt % 2, :].rearrange("p (h d) -> p h d", d=HP), xp, over(w2v[:, tt, heads], HP),
                            ALU.mult), ("xt", g, tt))
                neg = (neg_p if tt < SMP else neg_s)[:].rearrange("p (o l) -> p o l", o=1).broadcast_to([P, 4, P])
                for i in range(2):
                    u = 2 * k + i
                    wait_full(dve, ("sg", g, tt, i))
                    if u >= 3:
                        kk = (u - 3) // 2
                        wait_full(dve, ("yo", kk // NT, kk % NT))
                    release(tt_(mt[:, u % 3, :].rearrange("p (h l) -> p h l", h=4),
                                bank(("sg", g, tt, i)).rearrange("p (h l) -> p h l", h=4), neg, ALU.add), ("sg", g, tt, i))
                wait_read(dve, ("cb", g, tt))
                for i in range(2):
                    u = 2 * k + i
                    dve.wait_ge(S["mt_exp"], u + 1)
                    m = mt[:, u % 3, :].rearrange("p (h l) -> p h l", h=4)
                    tt_(m, m, cbs[:, k % 2, :].rearrange("p (o l) -> p o l", o=1).broadcast_to([P, 4, P]), ALU.mult) \
                        .then_inc(S["mt_ready"], 1)
                tok = slice(tt * P, (tt + 1) * P)
                if tt == 0:
                    if g == 0:
                        dve.wait_ge(S["q_spilled"], 16)
                    elif g >= 2:
                        dve.wait_ge(S["y_spilled"], 16 * (g - 1))
                yv = y[:, :, tok]
                if 0 < tt < SMP:
                    wait_full(dve, ("yi", g, tt))
                    wait_read(dve, ("eb", g, tt))
                    release(tt_(ytmp, bank(("yi", g, tt)), ebs[:, k % 2, :], ALU.mult), ("yi", g, tt))
                if tt < SMP:
                    wait_full(dve, ("st", g, tt))
                    if tt == 0:
                        ins = nc.vector.tensor_copy(stT, bank(("st", g, tt)))
                    else:
                        sv = stT.rearrange("p (h d) -> p h d", d=HP)
                        link(tt_(sv, sv, over(expae[:, tt, heads], HP), ALU.mult))
                        ins = tt_(stT, stT, bank(("st", g, tt)), ALU.add)
                    release(ins, ("st", g, tt))
                    wait_read(dve, ("st", g, tt))
                wait_full(dve, ("yo", g, tt))
                yo = bank(("yo", g, tt)).rearrange("p (j l) -> p j l", j=4)
                if 0 < tt < SMP:
                    wait_read(dve, ("yi", g, tt))
                    ins = tt_(yv, yo, ytmp.rearrange("p (j l) -> p j l", j=4), ALU.add)
                else:
                    ins = nc.vector.tensor_copy(yv, yo)
                release(ins, ("yo", g, tt))
            k = NT * g + SMP
            wait_read(dve, ("eb", g, SMP))
            wait_read(dve, ("yo", g, SMP))
            for j in range(4):
                u = 4 * g + j
                dec = ebs[:, k % 2, j * P:(j + 1) * P].rearrange("p (b q) -> p b q", q=SQ)[:, :, SQ - 1:SQ]
                for i in range(2):
                    wait_full(dve, ("sn", g, j, i))
                    sv = st0[:, u % 3, 4 * i:4 * i + 4, :]
                    link(tt_(sv, sv, dec[:, 4 * i:4 * i + 4, :].broadcast_to([P, 4, NS]), ALU.mult))
                    release(tt_(sv, sv, bank(("sn", g, j, i)).rearrange("p (b n) -> p b n", n=NS), ALU.add),
                            ("sn", g, j, i))
                wait_full(dve, ("ys", g, j))
                release(tt_(ytmp[:, 0:P], bank(("ys", g, j))[:, 0:P], ebs[:, k % 2, j * P:(j + 1) * P], ALU.mult),
                        ("ys", g, j))
                wait_read(dve, ("ys", g, j))
                link(tt_(y[:, j, TP:T], y[:, j, TP:T], ytmp[:, 0:P], ALU.add))
            for j in range(4):
                link(stt(out=y[:, j, :], in0=xsT[:, j, :], scalar=dcol[:, 4 * g + j:4 * g + j + 1], in1=y[:, j, :],
                         op0=ALU.mult, op1=ALU.add))
            wait_read(dve, ("zS", g))
            tt_(y, y, zT, ALU.mult).then_inc(S["y_gated"], 1)
            if g == GROUPS - 1:
                squares_dve(dve, g)

        def squares_dve(dve, g):
            tt_ = nc.vector.tensor_tensor
            for i, (a, b) in enumerate(((0, TP), (TP, T))):
                wait_full(dve, ("ss", g, i))
                src = bank(("ss", g, i))[:, 0:b - a]
                if g == 0:
                    ins = nc.vector.tensor_copy(ssrow[:, a:b], src)
                else:
                    ins = tt_(ssrow[:, a:b], ssrow[:, a:b], src, ALU.add)
                release(ins, ("ss", g, i))
                wait_read(dve, ("ss", g, i))

        def attention_dve(dve, link, over):
            tt_, ts_, copy = nc.vector.tensor_tensor, nc.vector.tensor_scalar, nc.vector.tensor_copy
            dve.wait_ge(S["q_back"], 16)
            link(nc.vector.memset(kz, 0.0))
            for g in range(AKV):
                rows = slice(HD * g, HD * (g + 1))
                ins = copy(kz[rows, g, :], kT[rows, 0:TP])
                if g == 0:
                    link(ins)
            ins.then_inc(S["kz_ready"], 1)
            link(nc.vector.memset(qz, 0.0))
            for g in range(AKV):
                rows = slice(HD * g, HD * (g + 1))
                ins = copy(qz[rows, :, g, :], qs[rows].rearrange("d s t q -> d s (t q)"))
                if g == 0:
                    link(ins)
            ins.then_inc(S["kz_ready"], 1)

            def least(key, out, scores, bias, u):
                release(nc.vector.tensor_tensor_reduce(out=out, in0=scores, in1=bias, scale=-ATT_SCALE, scalar=3.0e38,
                                                       op0=ALU.add, op1=ALU.min, accum_out=mx[:, u % 8:u % 8 + 1]), key)

            def scaled(p, u):
                dve.wait_ge(S["at_exp"], u + 1)
                r = rinv[:, u % 8:u % 8 + 1]
                link(nc.vector.reciprocal(r, rsum[:, u % 8:u % 8 + 1]))
                ts_(p, p, r, None, ALU.mult).then_inc(S["p_scaled"], 1)

            for i in range(SMP):
                w = P * (i + 1)
                bias = adm_att[:] if i == 0 else bias_p[i]
                for k in range(AH + 1):
                    u = AH * i + k
                    if k < AH:
                        wait_full(dve, ("s", i, k))
                        least(("s", i, k), sm[:, u % 3, 0:w], bank(("s", i, k))[:, 0:w], bias, u)
                    if k >= 1:
                        scaled(sm[:, (u - 1) % 3, 0:w], u - 1)
            for s in range(SB + 1):
                if s < SB:
                    wait_full(dve, ("kc", s, 0))
                    release(copy(kcT[:, s % 2, :].rearrange("d (p j) -> d j p", j=KJ)[:, 0:4, :],
                                 bank(("kc", s, 0)).rearrange("d (j p) -> d j p", j=4)), ("kc", s, 0))
                for g in range(AKV):
                    u = AKV * s + g
                    if s >= 1:
                        key = ("pt", s - 1, g, 0)
                        wait_full(dve, key)
                        release(copy(ptS[:, u % 2, 0:4, :], bank(key).rearrange("p (j q) -> p j q", j=4)), key)
                    if s < SB:
                        wait_full(dve, ("ds", s, g))
                        if s == 0:
                            wait_full(dve, ("s", SMP - 1, AH - 1))
                        else:
                            wait_full(dve, ("pt", s - 1, g, 2))
                        if g == 0:
                            dve.wait_ge(pair["bexp_loaded"][s % 2], 16 * AR * (s // 2 + 1))
                        least(("ds", s, g), pexp[:, u % 2, :], bank(("ds", s, g), 3)[:, 0:KEYS], bexp[:, s % 2, :],
                              AH * SMP + u)
                if s < SB:
                    for g in range(AKV):
                        u = AKV * s + g
                        scaled(pexp[:, u % 2, :], AH * SMP + u)

        def route(dve, link, over):
            tt_, ts_, stt, red = (nc.vector.tensor_tensor, nc.vector.tensor_scalar, nc.vector.scalar_tensor_tensor,
                                  nc.vector.tensor_reduce)
            gl = lg[:, :, 0:MG]
            el = lg[:, :, MG:].rearrange("p t (g e) -> p t g e", g=MG)
            gmax, gsum, m1, m2, ex, den, top_ = (rs1[:, i, :] for i in range(7))

            def first(mask, vals, best, pr, k):
                link(tt_(mask, vals, over(best, k), ALU.is_equal))
                link(tt_(mask, mask, pr.rearrange("p (o e) -> p o e", o=1).broadcast_to([P, NT, k]), ALU.mult))
                link(red(top_, mask, AX.X, ALU.max))
                link(tt_(mask, mask, over(top_, k), ALU.is_equal))

            link(red(gmax, gl, AX.X, ALU.max))
            tt_(rc[2], gl, over(gmax, MG), ALU.subtract).then_inc(S["r_exp_in"], 1)
            first(rc[0], gl, gmax, prio[:, ME - MG:ME], MG)
            for gi in range(MG):
                sel = rc[0][:, :, gi:gi + 1].broadcast_to([P, NT, ME])
                link(tt_(rb[1], el[:, :, gi, :], sel, ALU.mult))
                link(nc.vector.tensor_copy(rb[0], rb[1]) if gi == 0 else tt_(rb[0], rb[0], rb[1], ALU.add))
            link(red(m1, rb[0], AX.X, ALU.max))
            first(rb[2], rb[0], m1, prio[:], ME)
            link(stt(out=rb[3], in0=rb[2], scalar=NEG, in1=rb[0], op0=ALU.mult, op1=ALU.add))
            link(red(m2, rb[3], AX.X, ALU.max))
            first(rb[4], rb[3], m2, prio[:], ME)
            tt_(ex, m2, m1, ALU.subtract).then_inc(S["r_exp_in"], 1)
            for c, m in ((0, rb[2]), (1, rb[4])):
                for gi in range(MG):
                    link(tt_(hot[:, c, :, gi * ME:(gi + 1) * ME], m, rc[0][:, :, gi:gi + 1].broadcast_to([P, NT, ME]),
                             ALU.mult))
            tt_(cnt, hot[:, 0], hot[:, 1], ALU.add).then_inc(S["hot_ready"], 1)
            dve.wait_ge(S["r_exp"], 2)
            link(red(gsum, rc[2], AX.X, ALU.add))
            link(ts_(den, ex, 1.0, None, ALU.add))
            link(tt_(den, den, gsum, ALU.mult))
            link(nc.vector.reciprocal(den, den))
            link(tt_(ex, ex, den, ALU.mult))
            link(nc.vector.tensor_copy(wk[:, 0, :], den))
            link(nc.vector.tensor_copy(wk[:, 1, :], ex))
            wait_full(dve, ("rank",))
            link(nc.vector.tensor_copy(rank_, bank(("rank",))[:, 0:NT * NE].rearrange("p (t e) -> p t e", e=NE)))
            tot = bank(("rank",))[:, NT * NE:(NT + 1) * NE]
            link(nc.vector.memset(need, 0.0))
            steps = range(1, (T - 1) // SLOTS + 1)
            for m in steps:
                ins = stt(out=need, in0=tot, scalar=float(SLOTS * m), in1=need, op0=ALU.is_gt, op1=ALU.add)
                if m < steps[-1]:
                    link(ins)
            release(ins, ("rank",))
            wait_read(dve, ("rank",))
            link(nc.vector.tensor_copy(scan[:, 0], need))
            for i, d in enumerate((1, 2, 4, 8, 16)):
                s, t = scan[:, i % 2], scan[:, (i + 1) % 2]
                link(nc.vector.tensor_copy(t[:, 0:d], s[:, 0:d]))
                link(tt_(t[:, d:NE], s[:, d:NE], s[:, 0:NE - d], ALU.add))
            upto = scan[:, 1]
            link(tt_(first_x, upto, need, ALU.subtract))
            link(nc.vector.tensor_copy(beyond[:], upto[:, NE - 1:NE]))

            def per_choice(out, table):
                link(tt_(tmp_e.rearrange("p c t e -> p (c t) e"), hot.rearrange("p c t e -> p (c t) e"), table, ALU.mult))
                link(red(out, tmp_e, AX.X, ALU.add))

            def rows(ap):
                return ap.rearrange("p (o e) -> p o e", o=1).broadcast_to([P, 2 * NT, NE])

            for c in range(2):
                link(tt_(tmp_e[:, c], hot[:, c], rank_, ALU.mult))
            link(red(rk, tmp_e, AX.X, ALU.add))
            per_choice(ek, rows(count[:, 0:NE]))
            per_choice(xk, rows(first_x))
            link(nc.vector.memset(qk, 0.0))
            for m in steps:
                link(stt(out=qk, in0=rk, scalar=float(SLOTS * m), in1=qk, op0=ALU.is_gt, op1=ALU.add))
            link(stt(out=rk, in0=qk, scalar=-float(SLOTS), in1=rk, op0=ALU.mult, op1=ALU.add))
            link(ts_(rk, rk, 1.0, None, ALU.subtract))
            link(tt_(xk, xk, qk, ALU.add))
            link(tt_(xk, xk, ek, ALU.subtract))
            link(ts_(xk, xk, float(NE - 1), None, ALU.add))
            link(ts_(qk, qk, 1.0, None, ALU.min))
            link(tt_(xk, xk, qk, ALU.mult))
            link(tt_(bk, ek, xk, ALU.add))
            for i in range(2 * NT):
                c, tt = i // NT, i % NT
                if i >= 2:
                    dve.wait_ge(S["at_used"], i - 1)
                ts_(at_pos[:, i % 2, :], count[:], rk[:, c, tt:tt + 1], None, ALU.is_equal)
                ts_(at_blk[:, i % 2, :], count[:, 0:NB], bk[:, c, tt:tt + 1], entry[:, c, tt:tt + 1], ALU.is_equal,
                    ALU.mult).then_inc(S["at_ready"], 1)
            wait_full(dve, ("slots",))
            o = bank(("slots",))[0:SLOTS, 0:NB]
            nowhere = tmp_e.rearrange("p c t e -> p (c t e)")[0:SLOTS, 0:NB]
            link(ts_(nowhere, o, 0.0, float(NOWHERE), ALU.is_equal, ALU.mult))
            release(stt(out=slot_row[0:SLOTS, :], in0=o, scalar=-1.0, in1=nowhere, op0=ALU.add, op1=ALU.add), ("slots",))
            xs = count[:, 0:TAIL].rearrange("p (x o) -> p x o", o=1).broadcast_to([P, TAIL, NE])

            def per_block(ap):
                return ap.rearrange("p (o e) -> p o e", o=1).broadcast_to([P, TAIL, NE])

            link(tt_(tail_sum[:, 0], per_block(first_x), xs, ALU.is_le))
            link(tt_(tail_sum[:, 1], per_block(upto), xs, ALU.is_gt))
            link(tt_(tail_sum[:, 0], tail_sum[:, 0], tail_sum[:, 1], ALU.mult))
            link(tt_(tail_sum[:, 0], tail_sum[:, 0], per_block(count[:, 0:NE]), ALU.mult))
            rs_tail = tail_sum[:, 1, 0, 0:TAIL]
            link(red(rs_tail, tail_sum[:, 0], AX.X, ALU.add))
            link(nc.vector.tensor_copy(tail_expert[:], rs_tail))

        @block.vector
        def _(dve):
            n = [0]
            tt_ = nc.vector.tensor_tensor
            ts_ = nc.vector.tensor_scalar
            stt = nc.vector.scalar_tensor_tensor

            def link(ins):
                n[0] += 1
                ins.then_inc(dve_chain, 1)
                dve.wait_ge(dve_chain, n[0])

            def newton(r, v, tmp):
                link(tt_(tmp, r, r, ALU.mult))
                link(tt_(tmp, tmp, v, ALU.mult))
                link(ts_(tmp, tmp, -0.5, 1.5, ALU.mult, ALU.add))
                link(tt_(r, r, tmp, ALU.mult))

            def over(ap, k):
                return ap.rearrange("p (n o) -> p n o", o=1).broadcast_to([P, ap.shape[1], k])

            dve.wait_ge(consts, 3)
            link(nc.vector.tensor_reduce(qsel[:], ident[:].rearrange("p (b q) -> p q b", q=SQ), AX.X, ALU.add))
            dve.wait_ge(S["a_row_ready"], 1)
            link(ts_(a_row[:], a_row[:], -1.0, None, ALU.mult))
            pairs = dsk_row[:].rearrange("p (j i) -> p i j", i=2)
            link(nc.vector.tensor_copy(dcol[0:HP, :], pairs[0:HP, 0, :]))
            link(nc.vector.tensor_copy(dcol[HP:P, :], pairs[HP:P, 1, :]))
            dve.wait_ge(S["x_squares"], NT)
            ts_(ssq[:, 0, 0:NT], ssq[:, 0, 0:NT], 1.0 / D, EPS, ALU.mult, ALU.add).then_inc(S["x_var"], 1)
            dve.wait_ge(S["x_std"], 1)
            link(nc.vector.reciprocal(ssq[:, 1, 0:NT], ssq[:, 1, 0:NT]))
            newton(ssq[:, 1, 0:NT], ssq[:, 0, 0:NT], ssq[:, 2, 0:NT])
            wait_read(dve, ("par", 1))
            for tt in range(NT + 1):
                if tt < NT:
                    ts_(xtm[:, tt, :], xtm[:, tt, :], ssq[:, 1, tt:tt + 1], None, ALU.mult).then_inc(S["x_scaled"], 1)
                if tt > 0:
                    for c in range(2):
                        key = ("hT", tt - 1, c)
                        wait_full(dve, key)
                        release(tt_(hT[:, 4 * c:4 * c + 4, (tt - 1) * P:tt * P],
                                    bank(key).rearrange("p (k q) -> p k q", k=4), over(gmix[:, 4 * c:4 * c + 4], P),
                                    ALU.mult), key)
            wait_read(dve, ("kv", NT - 1))
            link(ts_(kvtm[:, :, SWI:SDT], kvtm[:, :, SWI:SDT], IDX_SCALE, None, ALU.mult))
            tt_(wl.rearrange("p (h q) -> p h q", q=SQ), over(kvtm[:, SMP, SWI:SDT], SQ),
                qsel[:].rearrange("p (o q) -> p o q", o=1).broadcast_to([P, IH, SQ]), ALU.mult).then_inc(S["wl_ready"], 1)
            for i in range(1, 4):
                w = P * (i + 1)
                for h in range(IH):
                    u = IH * (i - 1) + h
                    wait_read(dve, ("pd", i, h))
                    wt = kvtm[:, i, SWI + h:SWI + h + 1]
                    if h == 0:
                        ins = ts_(bias_p[i], rel[:, u % 2, 0:w], wt, None, ALU.mult)
                    else:
                        ins = stt(out=bias_p[i], in0=rel[:, u % 2, 0:w], scalar=wt, in1=bias_p[i], op0=ALU.mult,
                                  op1=ALU.add)
                    ins.then_inc(S["rel_used"], 1)
                    dve.wait_ge(S["rel_used"], u + 1)
                link(tt_(bias_p[i][:, w - P:w], bias_p[i][:, w - P:w], adm_idx[:], ALU.add))
            link(nc.vector.memset(wsel, 0.0))
            wait_read(dve, ("wc",))
            for b in range(SB):
                ins = ts_(wsel[:, b, b * SQ:(b + 1) * SQ], qsel[:], wcol[:, b:b + 1], None, ALU.mult)
            ins.then_inc(S["wsel_ready"], 1)

            def top(a, b):
                for k in range(a, min(b, ROUNDS)):
                    i = min(k // ROUNDS_P, 3)
                    scores = bias_p[i + 1] if i < 3 else bias_s
                    link(nc.vector.max(top8, scores))
                    link(nc.vector.match_replace(scores, top8, scores, TAKEN))
                    if k in (ROUNDS_P - 1, 2 * ROUNDS_P - 1, 3 * ROUNDS_P - 1, ROUNDS - 1):
                        ts_(scores, scores, CUT, NEG, ALU.is_gt, ALU.mult).then_inc(S["bias_ready"], 1)

            for c in range(3):
                w = 512 if c < 2 else SQ
                wait_full(dve, ("di", c))
                release(nc.vector.tensor_copy(bias_s[:, 512 * c:512 * c + w], bank(("di", c))[:, 0:w]), ("di", c))
            wait_read(dve, ("di", 2))
            tmp = st0[:, 0, :, :].rearrange("p b n -> p (b n)")
            tm = [tmp[:, i * NT * HEADS:(i + 1) * NT * HEADS].rearrange("p (t h) -> p t h", h=HEADS) for i in range(4)]
            link(tt_(dtv, kvtm[:, :, SDT:SW], dtb_row[:].rearrange("p (o h) -> p o h", o=1).broadcast_to([P, NT, HEADS]),
                     ALU.add))
            link(ts_(w2v, dtv, -1.0, None, ALU.mult))
            tt_(w2v, w2v, dtv, ALU.max).then_inc(S["dt_exp"], 1)
            dve.wait_ge(S["a_exp"], 1)
            link(ts_(tm[0], w2v, 2.0, None, ALU.add))
            link(nc.vector.reciprocal(tm[0], tm[0]))
            link(tt_(tm[0], w2v, tm[0], ALU.mult))
            link(tt_(tm[1], tm[0], tm[0], ALU.mult))
            link(ts_(tm[2], tm[1], 2.0 / 17, 2.0 / 15, ALU.mult, ALU.add))
            for m in (13, 11, 9, 7, 5, 3, 1):
                link(tt_(tm[2], tm[2], tm[1], ALU.mult))
                link(ts_(tm[2], tm[2], 2.0 / m, None, ALU.add))
            link(tt_(tm[2], tm[2], tm[0], ALU.mult))
            link(stt(out=dtv, in0=dtv, scalar=0.0, in1=tm[2], op0=ALU.max, op1=ALU.add))
            tt_(av, dtv, a_row[:].rearrange("p (o h) -> p o h", o=1).broadcast_to([P, NT, HEADS]), ALU.mult) \
                .then_inc(S["a_ready"], 1)
            for tt in range(NT):
                wait_full(dve, ("ac", tt))
                release(ts_(nac[:, tt, :], bank(("ac", tt))[:, 0:HEADS], -1.0, None, ALU.mult), ("ac", tt))
                wait_full(dve, ("ae", tt))
                wait_read(dve, ("ac", tt))
                release(tt_(w2v[:, tt, :], bank(("ae", tt))[:, 0:HEADS], nac[:, tt, :], ALU.add), ("ae", tt))
            ins_ready = ts_(ssq[:, 2, 0:1], ssq[:, 2, 0:1], 0.0, None, ALU.add)
            ins_ready.then_inc(S["ae_ready"], 1)
            dve.wait_ge(S["a_exp"], 2)
            link(tt_(w2v, w2v, dtv, ALU.mult))
            for g in range(GROUPS):
                ssd_dve(dve, g, link, over, top)
            attention_dve(dve, link, over)
            wait_full(dve, ("do", SB - 1))
            wait_read(dve, ("do", SB - 1))
            link(ts_(rr, ssrow, 1.0 / INNER, EPS, ALU.mult, ALU.add))
            nc.vector.tensor_copy(rt, rr).then_inc(S["ss_var"], 1)
            dve.wait_ge(S["ss_std"], 1)
            link(nc.vector.reciprocal(rt, rt))
            newton(rt, rr, mrg[:, 0, :])
            for m in range(2):
                wait_read(dve, ("gaS", m))
                link(tt_(gate[:, 0], gate[:, 0], rt.rearrange("p (o t) -> p o t", o=1).broadcast_to([P, 4, T]), ALU.mult))
                for j in range(4):
                    wait_full(dve, ("a", m, j))
                    release(tt_(mrg[:, 4 * m + j, 0:TP], bank(("a", m, j)), gate[:, 0, j, 0:TP], ALU.mult), ("a", m, j))
                wait_full(dve, ("aS", m))
                release(tt_(mrg[:, 4 * m:4 * m + 4, TP:T], bank(("aS", m)).rearrange("p (j q) -> p j q", j=4),
                            gate[:, 0, :, TP:T], ALU.mult), ("aS", m))
                wait_read(dve, ("gbS", m))
                for j in range(4):
                    wait_full(dve, ("b", m, j))
                    release(tt_(gate[:, 1, j, 0:TP], bank(("b", m, j)), gate[:, 1, j, 0:TP], ALU.mult), ("b", m, j))
                wait_full(dve, ("bS", m))
                release(tt_(gate[:, 1, :, TP:T], bank(("bS", m)).rearrange("p (j q) -> p j q", j=4),
                            gate[:, 1, :, TP:T], ALU.mult), ("bS", m))
                wait_read(dve, ("bS", m))
                tt_(mrg[:, 4 * m:4 * m + 4, :], mrg[:, 4 * m:4 * m + 4, :], gate[:, 1], ALU.add).then_inc(S["m_ready"], 1)
            for tt in range(NT):
                dve.wait_ge(pair["xres_loaded"][tt % 2], 16 * (tt // 2 + 1))
                for m in range(2):
                    wait_full(dve, ("x1", tt, m))
                    release(tt_(x1[:, tt, 512 * m:512 * m + 512], bank(("x1", tt, m)),
                                xres[:, tt % 2, 512 * m:512 * m + 512], ALU.add), ("x1", tt, m))
            dve.wait_ge(S["hx_squares"], NT)
            ts_(ssq[:, 2, 0:NT], ssq[:, 2, 0:NT], 1.0 / D, EPS, ALU.mult, ALU.add).then_inc(S["hx_var"], 1)
            dve.wait_ge(S["hx_std"], 1)
            link(nc.vector.reciprocal(ssq[:, 3, 0:NT], ssq[:, 3, 0:NT]))
            newton(ssq[:, 3, 0:NT], ssq[:, 2, 0:NT], ssq[:, 4, 0:NT])
            for tt in range(NT + 1):
                if tt < NT:
                    ts_(xn[:, tt, :], x1[:, tt, :], ssq[:, 3, tt:tt + 1], None, ALU.mult).then_inc(S["hx_scaled"], 1)
                if tt > 0:
                    for c in range(2):
                        key = ("h2", tt - 1, c)
                        wait_full(dve, key)
                        release(tt_(h2T[:, 4 * c:4 * c + 4, (tt - 1) * P:tt * P],
                                    bank(key).rearrange("p (k q) -> p k q", k=4), over(gmoe[:, 4 * c:4 * c + 4], P),
                                    ALU.mult), key)
            for tt in range(NT):
                wait_full(dve, ("rt", tt))
                release(tt_(lg[:, tt, :], bank(("rt", tt))[:, 0:MG + NE], brow[:], ALU.add), ("rt", tt))
            wait_read(dve, ("rt", NT - 1))
            route(dve, link, over)
            for e in range(-2, NE):
                if e + 2 < NE:
                    u = e + 2
                    dve.wait_ge(S["t_full"], u + 1)
                    tt_(hgT[:, u % 2], pbank(u % 2).rearrange("p (k q) -> p k q", k=KD), over(gmoe, SLOTS), ALU.mult) \
                        .then_inc(S["t_read"], 1)
                if 0 <= e + 1 < NE:
                    u = e + 1
                    dve.wait_ge(S["silu_ready"], u + 1)
                    tt_(hetm[0:SLOTS, u % 2], pbank(2 + u % 2)[0:SLOTS, FF:2 * FF], hsil[0:SLOTS, u % 2], ALU.mult).then_inc(S["he_ready"], 1)
                if e >= 0:
                    dve.wait_ge(S["dn1_full"], e + 1)
                    if e >= 2:
                        dve.wait_ge(pair["scattered"][e % 2], 16 * (e // 2))
                    nc.vector.tensor_copy(ysl[0:SLOTS, e % 2, 512:1024], pbank(5 + 2 * (e % 2))[0:SLOTS, :]) \
                        .then_inc(S["dn1_read"], 1)

        main.close()

        needed = nc.values_load(beyond[0:1, 0:1], min_val=0, max_val=TAIL)
        V = {name: sem(name) for name in ("ov_step", "ov_passed", "ov_idx", "ov_gathered", "ov_weights", "ov_turned", "ov_hT", "ov_up",
                                          "ov_silu", "ov_he", "ov_down", "ov_y", "ov_scattered")}
        with nc.If(needed > 0):
            with nc.Block() as block:
                @block.sync
                def _(sp):
                    with sp.Fori(0, TAIL) as x:
                        sp.wait_ge(V["ov_step"], x + 1)
                        e = sp.value_load(tail_expert[0:1, bass.ds(x, 1)], min_val=0, max_val=NE - 1)
                        for out, src in ((w13[0][:, :, 0:FF], w1), (w13[0][:, :, FF:], w3), (w2s[0], w2)):
                            sp.dma_start(out, src[bass.ds(e, 1)].rearrange("e (k p) f -> p (e k) f", p=P)) \
                                .then_inc(V["ov_weights"], 16)

                @block.gpsimd
                def _(pool):
                    def pass_on():
                        return nc.gpsimd.tensor_tensor(nothing[0:1, :], count[0:1, 0:1], count[0:1, 0:1], ALU.add)

                    pass_on().then_inc(V["ov_step"], 1)
                    with pool.Fori(0, TAIL) as x:
                        pool.wait_ge(V["ov_idx"], x + 1)
                        pass_on().then_inc(V["ov_passed"], 1)
                        pool.indirect_dma_start(hg[0:SLOTS, 0, :], None, x_rows[:, :],
                                                bass.IndirectOffsetOnAxis(ap=cur_row[0:SLOTS, 0:1], axis=0),
                                                bounds_check=2 * T - 1, oob_is_err=False).then_inc(V["ov_gathered"], 16)
                        pool.wait_ge(V["ov_y"], x + 1)
                        pool.wait_ge(V["ov_passed"], 2 * x + 1)
                        pass_on().then_inc(V["ov_passed"], 1)
                        pool.indirect_dma_start(y_rows[:, :], bass.IndirectOffsetOnAxis(ap=cur_row[0:SLOTS, 0:1], axis=0),
                                                ysl[0:SLOTS, 0, :], None, bounds_check=2 * T - 1, oob_is_err=False) \
                            .then_inc(V["ov_scattered"], 16)
                        pool.wait_ge(V["ov_scattered"], 16 * x + 16)
                        pool.wait_ge(V["ov_passed"], 2 * x + 2)
                        pass_on().then_inc(V["ov_step"], 1)

                @block.tensor
                def _(pe):
                    with pe.Fori(0, TAIL) as x:
                        pe.wait_ge(V["ov_gathered"], 16 * x + 16)
                        pe.wait_ge(consts, 3)
                        for k in range(KD):
                            ins = nc.tensor.transpose(psum[:, k * P:(k + 1) * P], hg[:, 0, k * P:(k + 1) * P], ident[:])
                        ins.then_inc(V["ov_turned"], 1)
                        pe.wait_ge(V["ov_hT"], x + 1)
                        pe.wait_ge(V["ov_weights"], 48 * x + 48)
                        for j in range(4):
                            for k in range(KD):
                                ins = nc.tensor.matmul(pbank(2)[:, j * SLOTS:(j + 1) * SLOTS],
                                                       w13[0][:, k, j * P:(j + 1) * P], hgT[:, 0, k, :],
                                                       start=k == 0, stop=k == KD - 1)
                        ins.then_inc(V["ov_up"], 1)
                        pe.wait_ge(V["ov_he"], x + 1)
                        for m in range(2):
                            for k in range(2):
                                ins = nc.tensor.matmul(pbank(4 + m)[0:SLOTS, :], heT[:, 0, k, :],
                                                       w2s[0][:, k, 512 * m:512 * m + 512], start=k == 0, stop=k == 1)
                        ins.then_inc(V["ov_down"], 1)

                @block.scalar
                def _(act):
                    with act.Fori(0, TAIL) as x:
                        act.wait_ge(V["ov_up"], x + 1)
                        nc.scalar.activation(hsil[:, 1, 0:2 * SLOTS], pbank(2)[:, 0:2 * SLOTS], ACT.Silu).then_inc(V["ov_silu"], 1)

                @block.vector
                def _(dve):
                    with dve.Fori(0, TAIL) as x:
                        dve.wait_ge(V["ov_step"], x + 1)
                        nc.vector.tensor_copy(cur_row[0:SLOTS, :], slot_row[0:SLOTS, bass.ds(x + NE, 1)]) \
                            .then_inc(V["ov_idx"], 1)
                        dve.wait_ge(V["ov_turned"], x + 1)
                        nc.vector.tensor_tensor(hgT[:, 0], psum[:, 0:KD * P].rearrange("p (k q) -> p k q", k=KD)[:, :, 0:SLOTS],
                                                gmoe.rearrange("p (k o) -> p k o", o=1).broadcast_to([P, KD, SLOTS]),
                                                ALU.mult).then_inc(V["ov_hT"], 1)
                        dve.wait_ge(V["ov_silu"], x + 1)
                        nc.vector.tensor_tensor(heT[:, 0].rearrange("p j q -> p (j q)"), pbank(2)[:, 2 * SLOTS:4 * SLOTS],
                                                hsil[:, 1, 0:2 * SLOTS], ALU.mult) \
                            .then_inc(V["ov_he"], 1)
                        dve.wait_ge(V["ov_down"], x + 1)
                        nc.vector.tensor_copy(ysl[0:SLOTS, 0, :], psum[0:SLOTS, 4 * 512:6 * 512]).then_inc(V["ov_y"], 1)

        with nc.Block() as block:
            @block.sync
            def _(sp):
                for tt in range(NT):
                    if tt >= 2:
                        sp.wait_ge(S["parts_added"], tt - 1)
                    for c in range(2):
                        sp.dma_start(ypart[:, tt % 2, c, :], y_rows[c * T + tt * P:c * T + (tt + 1) * P, :]) \
                            .then_inc(pair["ypart_loaded"][tt % 2], 16)
                for tt in range(NT):
                    sp.wait_ge(S["fin_ready"], tt + 1)
                    dst = y_prompt[0, tt * P:(tt + 1) * P, :] if tt < SMP else y_sample.rearrange("b q d -> (b q) d")
                    sp.dma_start(dst, x1[:, tt, :]).then_inc(S["y_written"], 16)
                sp.wait_ge(S["y_written"], 16 * NT)

            @block.scalar
            def _(act):
                for tt in range(NT):
                    act.wait_ge(S["parts_added"], tt + 1)
                    nc.scalar.activation(xn[:, tt, :], x1[:, tt, :], ACT.Square, accum_out=ssq[:, 4, tt:tt + 1]) \
                        .then_inc(S["fx_squares"], 1)
                    act.wait_ge(S["fx_var"], tt + 1)
                    nc.scalar.activation(ssq[:, 5, tt:tt + 1], ssq[:, 4, tt:tt + 1], ACT.Sqrt).then_inc(S["fx_std"], 1)

            @block.vector
            def _(dve):
                n = [0]
                stt, tt_, ts_ = nc.vector.scalar_tensor_tensor, nc.vector.tensor_tensor, nc.vector.tensor_scalar

                def link(ins):
                    n[0] += 1
                    ins.then_inc(S["last_chain"], 1)
                    dve.wait_ge(S["last_chain"], n[0])

                def scaled(tt):
                    v, r, t = ssq[:, 4, tt:tt + 1], ssq[:, 5, tt:tt + 1], ssq[:, 2, tt:tt + 1]
                    dve.wait_ge(S["fx_std"], tt + 1)
                    link(nc.vector.reciprocal(r, r))
                    link(tt_(t, r, r, ALU.mult))
                    link(tt_(t, t, v, ALU.mult))
                    link(ts_(t, t, -0.5, 1.5, ALU.mult, ALU.add))
                    link(tt_(r, r, t, ALU.mult))
                    stt(out=x1[:, tt, :], in0=x1[:, tt, :], scalar=r, in1=fin_row, op0=ALU.mult, op1=ALU.mult) \
                        .then_inc(S["fin_ready"], 1)

                dve.wait_ge(S["fin_loaded"], 16)
                for tt in range(NT + 1):
                    if tt < NT:
                        dve.wait_ge(pair["ypart_loaded"][tt % 2], 32 * (tt // 2 + 1))
                        link(stt(out=x1[:, tt, :], in0=ypart[:, tt % 2, 0, :], scalar=wk[:, 0, tt:tt + 1],
                                 in1=x1[:, tt, :], op0=ALU.mult, op1=ALU.add))
                        stt(out=x1[:, tt, :], in0=ypart[:, tt % 2, 1, :], scalar=wk[:, 1, tt:tt + 1],
                            in1=x1[:, tt, :], op0=ALU.mult, op1=ALU.add).then_inc(S["parts_added"], 1)
                        dve.wait_ge(S["fx_squares"], tt + 1)
                        ts_(ssq[:, 4, tt:tt + 1], ssq[:, 4, tt:tt + 1], 1.0 / D, EPS, ALU.mult, ALU.add) \
                            .then_inc(S["fx_var"], 1)
                    if tt > 0:
                        scaled(tt - 1)


_INS = ['x_prompt', 'x_sample', 'cache_k', 'cache_v', 'cache_kidx', 'state_conv', 'state_ssm', 'norm_mix_g', 'w_in',
        'conv_w', 'conv_b', 'dt_bias', 'A_log', 'D_skip', 'ssm_norm_g', 'w_ssm_out', 'w_attn_out', 'w_o', 'norm_moe_g',
        'w_router_group', 'b_router_group', 'w_router_expert', 'b_router_expert', 'w1', 'w3', 'w2', 'norm_final_g']
_OUTS = [(1, TP, D), (SB, SQ, D), (1, TP, AKV, HD), (1, TP, AKV, HD), (1, TP, IDIM), (1, CW - 1, CD),
         (1, HEADS, HP, NS), (SB, SQ, AKV, HD), (SB, SQ, AKV, HD), (SB, SQ, IDIM), (SB, CW - 1, CD),
         (SB, HEADS, HP, NS)]


def kernel(**inputs):
    import numpy as _np
    import concourse.bacc as _bacc
    from concourse import mybir as _mybir
    from concourse.bass_utils import run_bass_kernel_spmd as _run

    nc = _bacc.Bacc("TRN2", target_bir_lowering=False, num_devices=1)
    arrays, args = {}, []
    for name in _INS:
        a = _np.ascontiguousarray(inputs[name])
        arrays[f"in_{name}"] = a
        args.append(nc.dram_tensor(f"in_{name}", a.shape, _mybir.dt.from_np(a.dtype), kind="ExternalInput").ap())
    for i, shape in enumerate(_OUTS):
        args.append(nc.dram_tensor(f"out_{i}", shape, _mybir.dt.float32, kind="ExternalOutput").ap())
    hybrid_layer(nc, *args)
    r = _run(nc, [arrays], core_ids=[0])
    return tuple(r.results[0][f"out_{i}"] for i in range(len(_OUTS)))
```

```python
from contextlib import ExitStack

import concourse.bass as bass
from concourse import mybir

F32 = mybir.dt.float32
I32 = mybir.dt.int32
ALU = mybir.AluOpType
ACT = mybir.ActivationFunctionType
AX = mybir.AxisListType

P = 128
D = 1024
KD = D // P
TP = 512
SB, SQ = 8, 16
T = TP + SB * SQ
NT = T // P
SMP = NT - 1
PAST = 1024
KEYS = PAST + SQ
KJ = PAST // P
EPS = 1e-6
INNER, HEADS, HP, GROUPS, NS = 2048, 32, 64, 4, 128
HG = HEADS // GROUPS
CD = INNER + 2 * GROUPS * NS
CT = CD // P
CW = 4
AH, AKV, HD = 16, 2, 64
AR = AH // AKV
IH, IDIM = 8, 64
IDX_SCALE = (IH * IDIM) ** -0.5
TOPK_P, TOPK_S = 128, 256
ROUNDS_P = TOPK_P // 8
ROUNDS = 3 * ROUNDS_P + TOPK_S // 8
TOP_UPTO = (0, 28, 52, 66, ROUNDS)
CHUNK = 64
ATT_SCALE = HD ** -0.5
MG, ME = 4, 8
NE = MG * ME
FF = 256
SLOTS = 64
TAIL = (2 * T - 1) // SLOTS
NB = NE + TAIL
NOWHERE = 1 << 20
Z0 = 0
X0 = INNER
B0 = X0 + INNER
C0 = B0 + GROUPS * NS
DT0 = X0 + CD
Q0 = DT0 + HEADS
K0 = Q0 + AH * HD
V0 = K0 + AKV * HD
QI0 = V0 + AKV * HD
KI0 = QI0 + IH * IDIM
WI0 = KI0 + IDIM
G0 = WI0 + IH
SK, SV, SKI, SWI, SDT, SW = 0, 128, 256, 320, 328, 360
NEG = -1.0e30
NOTADM = -1.0e38
TAKEN = -3.0e38
CUT = -2.0e38


class Banks:

    def __init__(self):
        self.job, self.turn = {}, {}
        self.full, self.free = [0] * 8, [0] * 8
        self.last = [None] * 8

    def add(self, key, pool, readers=1, width=1):
        assert key not in self.job, key
        i = self.turn.get(pool, 0)
        self.turn[pool] = i + 1
        b = pool[i % len(pool)]
        before = sorted({self.last[c] for c in range(b, b + width) if self.last[c]})
        self.full[b] += 1
        self.free[b] += readers
        for c in range(b, b + width):
            self.last[c] = (b, self.free[b])
        self.job[key] = (b, self.full[b], before, self.free[b])


class Ring:

    def __init__(self, slots):
        self.slots, self.job, self.order, self.loads = slots, {}, [], [0] * slots

    def add(self, key, used, parts):
        s = len(self.order) % self.slots
        self.loads[s] += 16 * len(parts)
        self.job[key] = (s, self.loads[s])
        self.order.append((key, used, parts))


def plan_banks():
    b = Banks()
    any8 = tuple(range(8))
    for i in range(2):
        b.add(("par", i), any8)
    for tt in range(NT + 1):
        if tt < NT:
            for c in range(2):
                b.add(("hT", tt, c), any8)
        if tt > 0:
            b.add(("kv", tt - 1), any8)
    for c in range(2):
        for t in range(4 * c, 4 * c + 4):
            b.add(("q", t), any8)
        b.add(("qS", c), any8)
    for t in range(4):
        b.add(("qi", t), any8)
    b.add(("qiS",), any8)
    for i in range(4):
        b.add(("kT", i), any8)
    for i in range(1, 4):
        for h in range(IH):
            b.add(("pd", i, h), any8)
    b.add(("wc",), (3,))
    for i in range(3):
        b.add(("di", i), (0, 1, 2))
    work = (3, 4, 5, 6, 7)
    for s in range(SB + 2):
        if s < SB:
            b.add(("kx", s, 0), work)
            b.add(("kx", s, 1), work)
        if 1 <= s <= SB:
            for c in range(3):
                b.add(("dd", s - 1, c), work)
    for g in range(GROUPS):
        plan_group(b, g)
    for i in range(SMP):
        for k in range(AH + 3):
            if k < AH:
                b.add(("s", i, k), (0, 1, 2))
            if 2 <= k < AH + 2:
                b.add(("pT", i, k - 2), (3, 4, 5))
            if k >= 3 and (k - 3) % AR == 0:
                b.add(("o", i, (k - 3) // AR), (6, 7))
    for s in range(SB + 1):
        if s < SB:
            for c in range(2):
                b.add(("kc", s, c), (6, 7))
        if s >= 1:
            for g in range(AKV):
                for c in range(2):
                    b.add(("pt", s - 1, g, c), (6, 7))
            b.add(("pn", s - 1), (6, 7))
        if s < SB:
            for g in range(AKV):
                b.add(("ds", s, g), (0, 3), width=3)
        if s >= 1:
            b.add(("do", s - 1), (6, 7))
    for n in range(2):
        for what in ("gb", "a", "b") if n == 0 else ("ga", "gb", "a", "b"):
            for c in range(4):
                b.add((what, n, c), (0, 1, 2, 3))
            b.add((what + "S", n), (4, 5, 6, 7))
    for tt in range(NT + 2):
        if tt < NT:
            for n in range(2):
                b.add(("x1", tt, n), any8)
        if tt >= NT:
            b.add(("rt", tt - 2), any8)
        if 1 <= tt <= NT:
            for c in range(2):
                b.add(("h2", tt - 1, c), any8)
        if 2 <= tt < NT:
            b.add(("rt", tt - 2), any8)
    b.add(("rank",), any8)
    b.add(("slots",), any8)
    return b


def plan_group(b, g):
    lo, hi = (0, 1, 2, 3), (4, 5, 6, 7)
    b.add(("cT", g), hi)
    b.add(("xbcS", g, 0), hi)
    for j in range(4):
        b.add(("xbc", g, j), lo)
    if g:
        for i in range(2):
            b.add(("ss", g - 1, i), hi)
    else:
        for tt in range(NT):
            b.add(("ac", tt), hi)
            b.add(("ae", tt), hi, readers=2)
    b.add(("xbcS", g, 1), hi)
    for j in range(4, 6):
        b.add(("xbc", g, j), lo)
    for j in range(4):
        b.add(("z", g, j), lo)
    b.add(("zS", g), hi)
    b.add(("cO", g, 0), hi)
    b.add(("cO", g, 1), hi)
    b.add(("bt", g, 0), hi)
    b.add(("bt", g, 1), hi)
    for step in range(NT + 1):
        if step < NT:
            b.add(("xt", g, step), lo)
            b.add(("cb", g, step), hi)
            for i in range(2):
                b.add(("sg", g, step, i), hi)
        if step > 0:
            tt = step - 1
            if 0 < tt < SMP:
                b.add(("yi", g, tt), lo)
            if tt < SMP:
                b.add(("st", g, tt), hi)
            b.add(("yo", g, tt), lo)
    b.add(("so", g), hi)
    for j in range(4):
        for i in range(2):
            b.add(("s0", g, j, i), lo)
        for i in range(2):
            b.add(("sn", g, j, i), hi)
        b.add(("ys", g, j), lo)
    if g == GROUPS - 1:
        for c in range(4):
            b.add(("ga", 0, c), lo)
            if c == 1:
                for i in range(2):
                    b.add(("ss", g, i), hi)
        b.add(("gaS", 0), hi)


def hybrid_layer(nc, x_prompt, x_sample, cache_k, cache_v, cache_kidx, state_conv, state_ssm,
                 norm_mix_g, w_in, conv_w, conv_b, dt_bias, A_log, D_skip, ssm_norm_g,
                 w_ssm_out, w_attn_out, w_o, norm_moe_g, w_router_group, b_router_group,
                 w_router_expert, b_router_expert, w1, w3, w2, norm_final_g,
                 y_prompt, y_sample, k_prompt, v_prompt, kidx_prompt, conv_prompt, ssm_prompt,
                 k_sample, v_sample, kidx_sample, conv_sample, ssm_sample):
    banks = plan_banks()
    w_in_r = w_in.rearrange("(k p) n -> p k n", p=P)

    ring = Ring(3)

    def cols(a, n, at=0):
        return (lambda s: s[:, :, at:at + n], w_in_r[:, :, a:a + n])

    ring.add(("small",), ("kv", NT - 1), [cols(K0, 256), cols(KI0, 72, SKI), cols(DT0, 32, SDT)])
    for c in range(2):
        ring.add(("wq", c), ("qS", c), [
            (lambda s, k=k, g=g: s[:, k, :].rearrange("p (t g d) -> p g t d", g=AKV, d=HD)[:, g, :, :],
             w_in[k * P:(k + 1) * P, Q0 + g * AR * HD + c * 256:Q0 + g * AR * HD + c * 256 + 256]
             .rearrange("p (t d) -> p t d", d=HD))
            for k in range(KD) for g in range(AKV)])
    ring.add(("wqi",), ("qiS",), [cols(QI0, 512)])
    for g in range(GROUPS):
        ring.add(("wx", g), ("xbc", g, 3), [cols(X0 + 512 * g, 512)])
        ring.add(("wbc", g), ("xbc", g, 5), [cols(B0 + NS * g, NS), cols(C0 + NS * g, NS, NS)])
        ring.add(("wz", g), ("zS", g), [cols(Z0 + 512 * g, 512)])
    wso_r = w_ssm_out.rearrange("(k p) n -> p k n", p=P)
    for n in range(2):
        ring.add(("wga", n), ("gaS", n), [cols(G0 + 512 * n, 512)])
        ring.add(("wgb", n), ("gbS", n), [cols(G0 + D + 512 * n, 512)])
        for c in range(2):
            ring.add(("wso", n, c), ("aS", n), [(lambda s: s[:, :, :], wso_r[:, 8 * c:8 * c + 8, 512 * n:512 * n + 512])])
        ring.add(("wao", n), ("bS", n), [
            (lambda s, g=g: s[g * HD:(g + 1) * HD, :, :],
             w_attn_out[g * AR * HD:(g + 1) * AR * HD, 512 * n:512 * n + 512].rearrange("(t d) n -> d t n", d=HD))
            for g in range(AKV)])
    wo_r = w_o.rearrange("(k p) n -> p k n", p=P)
    for n in range(2):
        ring.add(("wo", n), ("x1", NT - 1, 1), [(lambda s: s[:, :, :], wo_r[:, :, 512 * n:512 * n + 512])])
    with ExitStack() as ctx:
        def sb(name, shape, dtype=F32):
            return ctx.enter_context(nc.sbuf_tensor(name, shape, dtype))

        def sem(name):
            return ctx.enter_context(nc.semaphore(name))

        psum = ctx.enter_context(nc.psum_tensor("psum", [P, 8 * 512], F32))

        ident = sb("ident", [P, P])
        ones = sb("ones", [P, P])
        cum_p, cum_s = sb("cum_p", [P, P]), sb("cum_s", [P, P])
        same = sb("same", [P, P])
        stream = sb("stream", [P, SB])
        adm_idx, adm_att = sb("adm_idx", [P, P]), sb("adm_att", [P, P])
        qsel = sb("qsel", [P, SQ])
        prio = sb("prio", [P, ME])
        count = sb("count", [P, SLOTS])
        entry = sb("entry", [P, 2, NT])
        slot_row = sb("slot_row", [P, NB], I32)
        tail_expert = sb("tail_expert", [P, TAIL], I32)
        beyond = sb("beyond", [P, 1], I32)
        cur_row = sb("cur_row", [P, 1], I32)
        wk = sb("wk", [P, 2, NT])
        pc = sb("pc", [P, 2, P])
        a_row, dtb_row, dsk_row = sb("a_row", [P, HEADS]), sb("dtb_row", [P, HEADS]), sb("dsk_row", [P, HEADS])
        dcol = sb("dcol", [P, HEADS // 2])
        brow = sb("brow", [P, MG + NE])
        cw_col = pc[:, 0, 0:CW * CT].rearrange("p (w c) -> p w c", w=CW)
        cb_col = pc[:, 0, CW * CT:CW * CT + CT]
        gmix = pc[:, 0, 120:128]
        gmoe = pc[:, 1, 0:8]
        gssm = pc[:, 1, 8:24]
        ssq = sb("ssq", [P, 6, 8])

        wring = sb("wring", [P, 3, KD, 512])
        hT = sb("hT", [P, KD, T])
        kvtm = sb("kvtm", [P, NT, SW])
        oT = sb("oT", [P, KD, T])
        hTf = hT[:].rearrange("p k t -> p (k t)")
        oTf = oT[:].rearrange("p k t -> p (k t)")
        arena = sb("arena", [P, 27044])

        class Arena:

            def __init__(self, base, at=0):
                self.base, self.at = base, at

            def take(self, *shape):
                n = 1
                for s in shape:
                    n *= s
                v = self.base[:, self.at:self.at + n]
                self.at += n
                assert self.at <= self.base.shape[1], self.at
                if len(shape) == 1:
                    return v
                names = "abcd"[:len(shape)]
                return v.rearrange(f"p ({' '.join(names)}) -> p {' '.join(names)}",
                                   **{names[i]: shape[i] for i in range(len(shape))})

        keep = Arena(arena)
        kT, qs = keep.take(T), keep.take(SB, KD, SQ)
        bias_p = [None] + [keep.take(P * (i + 1)) for i in range(1, 4)]
        bias_s = keep.take(KEYS)
        ssrow = keep.take(T)
        kept = keep.at
        a1 = Arena(arena, kept)
        xtm, par, junk = a1.take(NT, D), a1.take(2, P), a1.take(D)
        a1 = Arena(arena, a1.at)
        qiT, qis = a1.take(IH // 2, TP), a1.take(SB, IH, SQ)
        kiT = a1.take(2, T)
        wsel, wl, wcol = a1.take(SB, P), a1.take(P), a1.take(SB)
        rel, kx_in, kxT = a1.take(2, KEYS), a1.take(2, KJ, IDIM), a1.take(2, PAST)
        top8 = ssq[:, 5, :]
        a2 = Arena(arena, kept)
        raw, acc = a2.take(2, 667), a2.take(1, 664)
        a2_xs = a2.at
        xsT, bcT, zT = a2.take(4, T), a2.take(2, T), a2.take(4, T)
        yb = oTf.rearrange("p (u j t) -> p u j t", u=2, j=4)
        btm, bms = a2.take(NT, NS), a2.take(SB, NS)
        xdt, xw = a2.take(2, 512), a2.take(2, 512)
        mt, cbs, ebs = a2.take(4, 512), a2.take(2, P), a2.take(2, 512)
        ytmp, stT = a2.take(512), a2.take(512)
        dtv, av, acv, expae, w2v = (a2.take(NT, HEADS) for _ in range(5))
        st0, s0T = a2.take(3, SB, NS), a2.take(SB, P)
        sout = xdt[:, 1, :]
        cin, cst = a2.take(6, P), a2.take(6, 24)
        cgo, crow = a2.take(6, 27), cin
        a3 = Arena(arena, kept)
        sm = a3.take(3, 512)
        a3.at = a2_xs
        a3.take(4, T)
        pT = a3.take(2, 512)
        kz, qz, bexp = a3.take(AKV, TP), a3.take(SB, AKV, P), a3.take(2, KEYS)
        mx, rsum, rinv = a3.take(8), a3.take(8), a3.take(8)
        kb, vb, kcT = a3.take(2, KJ, P), a3.take(2, KJ, P), a3.take(2, PAST)
        pexp, ptS, ptN = a3.take(2, KEYS), a3.take(2, KJ, P), a3.take(2, P)
        vnew = a3.take(SB, P)
        a4 = Arena(arena, 0)
        mrg = a4.take(KD, T)
        rr, rt = a4.take(T), a4.take(T)
        assert a4.at <= a2_xs
        a4.at = a2_xs
        gate = a4.take(2, 4, T)
        yz = a4.take(16, T)
        a5 = Arena(arena, KD * T)
        xres, x1 = a5.take(2, D), a5.take(NT, D)
        h2T, xn = a5.take(KD, T), oTf.rearrange("p (t d) -> p t d", t=NT)
        hg, hgT, ysl = a5.take(2, D), a5.take(2, KD, SLOTS), a5.take(2, D)
        hsil, hetm, heT = a5.take(2, FF), a5.take(2, FF), a5.take(2, 2, SLOTS)
        lg = a5.take(NT, MG + NE)
        rb = [a5.take(NT, ME) for _ in range(5)]
        rc = [a5.take(NT, MG) for _ in range(3)]
        rs1 = a5.take(8, NT)
        hot = a5.take(2, NT, NE)
        cnt = a5.take(NT, NE)
        rank_, tmp_e = a5.take(NT, NE), a5.take(2, NT, NE)
        need, first_x, scan = a5.take(NE), a5.take(NE), a5.take(2, NE)
        rk, ek, xk, qk, bk = (a5.take(2, NT) for _ in range(5))
        fills = a5.take((T - 1) // SLOTS)
        a6 = Arena(arena, a5.at)
        wr = a6.take(KD, MG + NE)
        at_pos, at_blk = a6.take(2, SLOTS), a6.take(2, NB)
        tail_sum = ysl.rearrange("p u d -> p (u d)")[:, 0:2 * TAIL * NE].rearrange("p (i x e) -> p i x e", i=2, e=NE)
        w13 = [hTf[:, 0:KD * 512].rearrange("p (k n) -> p k n", k=KD)] + [wring[:, s] for s in (1, 2, 0)]
        h2f = h2T.rearrange("p k t -> p (k t)")
        w2s = [v.rearrange("p (k n) -> p k n", k=2) for v in
               (arena[:, 0:2 * D], arena[:, 2 * D:4 * D], arena[:, 4 * D:6 * D], h2f[:, 0:2 * D])]
        nothing = ssq[:, 5, 7:8]
        fin_row = h2f[:, 2 * D:3 * D]
        rows_in = [hg[:, 0], hg[:, 1], h2f[:, 3 * D:4 * D], h2f[:, 4 * D:5 * D]]
        ypart = wring.rearrange("p s k n -> p (s k n)")[:, 0:2 * NT * D].rearrange("p (t c d) -> p t c d", t=NT, c=2)

        x_rows = nc.dram_tensor("x_rows", (2 * T, D), F32, kind="Internal").ap()
        y_rows = nc.dram_tensor("y_rows", (2 * T, D), F32, kind="Internal").ap()
        q_spill = nc.dram_tensor("q_spill", (P, KD, TP), F32, kind="Internal").ap()
        y_spill = nc.dram_tensor("y_spill", (P, 16, T), F32, kind="Internal").ap()

        full = [sem(f"full{i}") for i in range(8)]
        free = [sem(f"free{i}") for i in range(8)]
        slot_loaded = [sem(f"slot_loaded{i}") for i in range(3)]
        params_loaded, rows_loaded = sem("params_loaded"), sem("rows_loaded")
        x_loaded = [sem(f"x_loaded{i}") for i in range(NT)]
        consts, out_written = sem("consts"), sem("out_written")
        dve_chain, pool_chain = sem("dve_chain"), sem("pool_chain")

        def bank(key, width=1):
            b = banks.job[key][0]
            return psum[:, b * 512:(b + width) * 512]

        def pbank(i):
            return psum[:, i * 512:(i + 1) * 512]

        def claim(pe, key):
            for b, n in banks.job[key][2]:
                pe.wait_ge(free[b], n)
            return bank(key)

        def filled(ins, key):
            ins.then_inc(full[banks.job[key][0]], 1)

        def wait_full(eng, key):
            b, n, _, _ = banks.job[key]
            eng.wait_ge(full[b], n)

        def release(ins, key):
            ins.then_inc(free[banks.job[key][0]], 1)

        def wait_read(eng, key, short=0):
            b, _, _, n = banks.job[key]
            eng.wait_ge(free[b], n - short)

        def slot(key):
            return wring[:, ring.job[key][0], :, :]

        def wait_chunk(pe, key):
            s, n = ring.job[key]
            pe.wait_ge(slot_loaded[s], n)
            return slot(key)

        S = {name: sem(name) for name in (
            "ident_ready", "pads_zeroed", "x_squares", "x_var", "x_std", "x_scaled",
            "a_row_ready", "wl_ready", "wsel_ready", "rel_used",
            "bias_ready", "dt_exp", "a_exp", "a_ready", "raw_zeroed", "raw_ready", "conv_done",
            "xs_ready", "gathered", "bms_ready", "mt_size", "mt_exp", "xw_ready", "mt_ready",
            "y_gated", "y_squares", "y_gained",
            "q_spilled", "y_spilled", "crow_written", "sout_written", "q_back", "vnew_loaded", "y_back",
            "router_loaded", "fin_loaded", "at_exp", "kz_ready", "p_scaled", "ss_var", "ss_std", "m_ready", "hx_squares",
            "hx_var", "hx_std", "hx_scaled", "r_exp_in", "r_exp", "hot_ready", "at_ready", "at_used",
            "t_full", "t_read", "up_full", "silu_ready", "he_ready", "heT_full", "heT_ready",
            "dn0_full", "dn1_full", "dn0_read", "dn1_read", "xn_stored", "fx_squares", "fx_var", "fx_std",
            "fin_ready", "last_ready", "rms_ready", "fx_scaled", "y_written", "parts_added", "last_chain")}
        w13_loaded = [sem(f"w13_loaded{i}") for i in range(4)]
        st0_loaded = [sem(f"st0_loaded{i}") for i in range(3)]
        st0_written = [sem(f"st0_written{i}") for i in range(3)]
        w2_loaded = [sem(f"w2_loaded{i}") for i in range(4)]
        gathered_rows = [sem(f"gathered_rows{i}") for i in range(4)]
        pair = {name: [sem(f"{name}{i}") for i in range(2)] for name in (
            "kx_loaded", "kb_loaded", "bexp_loaded", "vb_loaded", "xres_loaded", "cin_loaded", "scattered")}
        ypart_loaded = [sem(f"ypart_loaded{i}") for i in range(NT)]

        main = ExitStack()
        block = main.enter_context(nc.Block())
        ST0_USES = [len(range(i, 4 * GROUPS, 3)) for i in range(3)]
        N_OUT = 3 * NT

        @block.sync
        def _(sp):
            def chunks(upto_key):
                while sent[0] < len(ring.order):
                    key, _, parts = ring.order[sent[0]]
                    if sent[0] >= ring.slots:
                        wait_full(sp, ring.order[sent[0] - ring.slots][1])
                    for part, src in parts:
                        sp.dma_start(part(slot(key)), src).then_inc(slot_loaded[ring.job[key][0]], 16)
                    sent[0] += 1
                    if key == upto_key:
                        return

            sent = [0]
            sp.dma_start(xtm[:, 0, :], x_prompt[0, 0:P, :]).then_inc(x_loaded[0], 16)
            for lo, hi, i, src in ((0, 96, 0, conv_w.rearrange("w (c p) -> (w c) p", p=P)),
                                   (96, 120, 0, conv_b.rearrange("(c p) -> c p", p=P)),
                                   (120, 128, 0, norm_mix_g.rearrange("(c p) -> c p", p=P)),
                                   (0, 8, 1, norm_moe_g.rearrange("(c p) -> c p", p=P)),
                                   (8, 24, 1, ssm_norm_g.rearrange("(c p) -> c p", p=P))):
                sp.dma_start(par[lo:hi, i, :], src).then_inc(params_loaded, 16)
            for tt in range(1, SMP):
                sp.dma_start(xtm[:, tt, :], x_prompt[0, tt * P:(tt + 1) * P, :]).then_inc(x_loaded[tt], 16)
                if tt == 1:
                    chunks(("small",))
            sp.dma_start(xtm[:, SMP, :], x_sample.rearrange("b q d -> (b q) d")).then_inc(x_loaded[SMP], 16)
            for dst, src in ((a_row[:], A_log), (dtb_row[:], dt_bias), (dsk_row[:], D_skip),
                             (brow[:, 0:MG], b_router_group), (brow[:, MG:MG + NE], b_router_expert)):
                sp.dma_start(dst, src.rearrange("(o n) -> o n", o=1).broadcast_to([P, src.shape[0]])) \
                    .then_inc(rows_loaded, 16)
            chunks(("wqi",))
            for s in range(SB):
                if s == 0:
                    wait_read(sp, ("hT", NT - 1, 1))
                if s >= 2:
                    wait_full(sp, ("kx", s - 2, 1))
                sp.dma_start(kx_in[:, s % 2, :, :], cache_kidx[s].rearrange("(p j) d -> p j d", j=KJ)) \
                    .then_inc(pair["kx_loaded"][s % 2], 16)
            chunks(("wz", 0))
            for c in range(3):
                wait_read(sp, ("di", c))
            for g in range(GROUPS):
                if g:
                    sp.wait_ge(S["crow_written"], 96 * g)
                for at, n, c in ((0, 4, 512 * g), (4, 1, INNER + NS * g), (5, 1, INNER + (GROUPS + g) * NS)):
                    sp.dma_start(cin[0:24, at:at + n, :],
                                 state_conv[:, :, c:c + n * P].rearrange("b r (c p) -> (b r) c p", p=P)) \
                        .then_inc(pair["cin_loaded"][0], 16)
                chunks(("wz", min(g + 1, GROUPS - 1)) if g + 1 < GROUPS else ("wgb", 0))
                for j in range(4):
                    u = 4 * g + j
                    if u >= 3:
                        sp.wait_ge(st0_written[u % 3], 16 * (u // 3))
                    r = (4 * g + j) * P
                    sp.dma_start(st0[:, u % 3, :, :],
                                 state_ssm.rearrange("b h p n -> (h p) b n")[r:r + P, :, :]) \
                        .then_inc(st0_loaded[u % 3], 16)
            sp.wait_ge(S["q_spilled"], 16)
            sp.wait_ge(S["y_spilled"], 16 * GROUPS)
            wait_read(sp, ("ss", GROUPS - 1, 1))
            for i in range(3):
                sp.wait_ge(st0_written[i], 16 * ST0_USES[i])
            sp.wait_ge(S["crow_written"], 16 * 6 * GROUPS)
            sp.wait_ge(S["sout_written"], 16 * GROUPS)
            sp.dma_start(oT[:, :, 0:TP], q_spill[:, :, :]).then_inc(S["q_back"], 16)
            sp.wait_ge(S["bias_ready"], 4)
            for s in range(SB + 1):
                if s < SB:
                    if s >= 2:
                        wait_full(sp, ("kc", s - 2, 1))
                    sp.dma_start(kb[:, s % 2, :, :], cache_k[s].rearrange("(p j) g d -> p j (g d)", j=KJ)) \
                        .then_inc(pair["kb_loaded"][s % 2], 16)
                    if s >= 2:
                        wait_read(sp, ("ds", s - 2, 1))
                    for t in range(AR):
                        sp.dma_start(bexp[t * SQ:(t + 1) * SQ, s % 2, :], bias_s[s * SQ:(s + 1) * SQ, :]) \
                            .then_inc(pair["bexp_loaded"][s % 2], 16)
                if s >= 1:
                    b = s - 1
                    if b >= 2:
                        wait_full(sp, ("do", b - 2))
                    sp.dma_start(vb[:, b % 2, :, :], cache_v[b].rearrange("(p j) g d -> p j (g d)", j=KJ)) \
                        .then_inc(pair["vb_loaded"][b % 2], 16)
            wait_read(sp, ("do", SB - 1))
            sp.dma_start(yz[:, :, :], y_spill[:, :, :]).then_inc(S["y_back"], 16)
            chunks(("wo", 1))

            def load13(e):
                sp.dma_start(w13[e % 4][:, :, 0:FF], w1[e].rearrange("(k p) f -> p k f", p=P)) \
                    .then_inc(w13_loaded[e % 4], 16)
                sp.dma_start(w13[e % 4][:, :, FF:], w3[e].rearrange("(k p) f -> p k f", p=P)) \
                    .then_inc(w13_loaded[e % 4], 16)

            def load2(e):
                sp.dma_start(w2s[e % 4], w2[e].rearrange("(k p) n -> p k n", p=P)).then_inc(w2_loaded[e % 4], 16)

            sp.wait_ge(S["m_ready"], 2)
            wait_full(sp, ("bS", 1))
            sp.dma_start(wr[:, :, 0:MG], w_router_group.rearrange("(k p) n -> p k n", p=P)).then_inc(S["router_loaded"], 16)
            sp.dma_start(wr[:, :, MG:], w_router_expert.rearrange("(k p) n -> p k n", p=P)).then_inc(S["router_loaded"], 16)
            for tt in range(NT):
                if tt >= 2:
                    wait_read(sp, ("x1", tt - 2, 1))
                src = x_prompt[0, tt * P:(tt + 1) * P, :] if tt < SMP else x_sample.rearrange("b q d -> (b q) d")
                sp.dma_start(xres[:, tt % 2, :], src).then_inc(pair["xres_loaded"][tt % 2], 16)
                if tt == 1:
                    load13(0)
                    load13(1)
            wait_read(sp, ("x1", NT - 1, 1))
            load2(0)
            load13(2)
            load2(1)
            load13(3)
            load2(2)
            wait_full(sp, ("rt", NT - 1))
            load2(3)
            sp.dma_start(fin_row, norm_final_g.rearrange("(o n) -> o n", o=1).broadcast_to([P, D])) \
                .then_inc(S["fin_loaded"], 16)
            for e in range(4, NE):
                sp.wait_ge(S["up_full"], e - 3)
                load13(e)
                sp.wait_ge(S["dn1_full"], e - 3)
                load2(e)
            sp.wait_ge(out_written, 16 * N_OUT)
            for i in range(3):
                sp.wait_ge(st0_written[i], 16 * ST0_USES[i])
            sp.wait_ge(S["crow_written"], 16 * 6 * GROUPS)
            sp.wait_ge(S["sout_written"], 16 * GROUPS)

        @block.gpsimd
        def _(pool):
            n = [0]

            def link(ins):
                n[0] += 1
                ins.then_inc(pool_chain, 1)
                pool.wait_ge(pool_chain, n[0])

            def select(out, in_, fill, pattern, base, cm, op=ALU.is_ge):
                link(nc.gpsimd.affine_select(out=out, in_=in_, compare_op=op, fill=fill, base=base,
                                             pattern=pattern, channel_multiplier=cm))

            link(nc.gpsimd.memset(ident[:], 0.0))
            nc.gpsimd.affine_select(out=ident[:], in_=ident[:], compare_op=ALU.not_equal, fill=1.0, base=0,
                                    pattern=[[-1, P]], channel_multiplier=1).then_inc(S["ident_ready"], 1)
            for t, v in ((ones, 1.0), (cum_p, 1.0), (same, 1.0), (stream, 1.0),
                         (adm_idx, 0.0), (adm_att, 0.0)):
                link(nc.gpsimd.memset(t[:], v))
            select(cum_p[:], cum_p[:], 0.0, [[1, P]], 0, -1)
            for t, w in ((same, SQ), (stream, 1)):
                v = t[:].rearrange("p (b q) -> p b q", q=w)
                select(v, v, 0.0, [[-SQ, SB], [0, w]], 0, 1)
                select(v, v, 0.0, [[SQ, SB], [0, w]], SQ - 1, -1)
            select(cum_s[:], same[:], 0.0, [[1, P]], 0, -1)
            for t, fill in ((adm_idx, NOTADM), (adm_att, NEG)):
                v = t[:].rearrange("p (a k) -> p a k", k=CHUNK)
                select(v, v, fill, [[-CHUNK, 2], [0, CHUNK]], 0, 1)
            nc.gpsimd.iota(prio[:], [[-1, ME]], base=ME, channel_multiplier=0,
                           allow_small_or_imprecise_dtypes=True).then_inc(consts, 1)
            nc.gpsimd.iota(count[:], [[1, SLOTS]], base=0, channel_multiplier=0,
                           allow_small_or_imprecise_dtypes=True).then_inc(consts, 1)
            nc.gpsimd.iota(entry[:], [[T, 2], [P, NT]], base=1, channel_multiplier=1,
                           allow_small_or_imprecise_dtypes=True).then_inc(consts, 1)
            link(nc.gpsimd.memset(qis, 0.0))
            link(nc.gpsimd.memset(kxT, 0.0))
            nc.gpsimd.memset(kiT, 0.0).then_inc(S["pads_zeroed"], 1)
            for tt in range(NT):
                wait_read(pool, ("kv", tt))
                for at, width, dp, ds in ((SK, 128, k_prompt, k_sample), (SV, 128, v_prompt, v_sample),
                                          (SKI, 64, kidx_prompt, kidx_sample)):
                    if tt < SMP:
                        dst = dp[0, tt * P:(tt + 1) * P]
                    else:
                        dst = ds.rearrange("b q g d -> (b q) g d" if width == 128 else "b q d -> (b q) d")
                    if width == 128:
                        dst = dst.rearrange("t g d -> t (g d)")
                    pool.dma_start(dst, kvtm[:, tt, at:at + width]).then_inc(out_written, 16)
            wait_read(pool, ("qS", 1))
            pool.dma_start(q_spill[:, :, :], oT[:, :, 0:TP]).then_inc(S["q_spilled"], 16)
            for c in range(3):
                wait_read(pool, ("di", c))
            for i in range(2):
                link(nc.gpsimd.memset(raw[:, i, 0:3], 0.0))
            nc.gpsimd.memset(cgo[:, 0, 0:3], 0.0).then_inc(S["raw_zeroed"], 1)
            for g in range(GROUPS):
                for j in range(6):
                    u = 6 * g + j
                    pool.wait_ge(S["raw_ready"], u + 1)
                    if j == 0 and g:
                        wait_full(pool, ("cO", g - 1, 1))
                    nc.gpsimd.tensor_copy(cgo[:, j, 0:3], raw[:, u % 2, 512:515])
                    nc.gpsimd.tensor_copy(cgo[:, j, 3:27].rearrange("p (b r) -> p b r", r=3),
                                          raw[:, u % 2, 515:667].rearrange("p (b q) -> p b q", q=19)[:, :, 16:19]) \
                        .then_inc(S["gathered"], 1)
                if g == 0:
                    pool.wait_ge(S["a_exp"], 2)
                else:
                    wait_full(pool, ("sn", g - 1, 3, 1))
                for tt in range(NT):
                    wait_read(pool, ("xt", g, tt))
                    if tt >= 2:
                        wait_full(pool, ("st", g, tt - 2))
                    elif tt == 1 and g:
                        wait_full(pool, ("st", g - 1, SMP - 1))
                    nc.gpsimd.tensor_tensor(
                        xw[:, tt % 2, :].rearrange("p (h d) -> p h d", d=HP),
                        xdt[:, tt % 2, :].rearrange("p (h d) -> p h d", d=HP),
                        w2v[:, tt, HG * g:HG * (g + 1)].rearrange("p (h o) -> p h o", o=1).broadcast_to([P, HG, HP]),
                        ALU.mult).then_inc(S["xw_ready"], 1)
                wait_read(pool, ("bt", g, 1))
                nc.gpsimd.tensor_tensor(bms, btm[:, SMP:SMP + 1, :].broadcast_to([P, SB, NS]),
                                        stream[:].rearrange("p (b o) -> p b o", o=1).broadcast_to([P, SB, NS]),
                                        ALU.mult).then_inc(S["bms_ready"], 1)
                wait_read(pool, ("cO", g, 1))
                for at, n_, c in ((0, 4, 512 * g), (4, 1, INNER + NS * g), (5, 1, INNER + (GROUPS + g) * NS)):
                    pool.dma_start(conv_prompt[0, :, c:c + n_ * P].rearrange("r (c p) -> r c p", p=P),
                                   crow[0:3, at:at + n_, :]).then_inc(S["crow_written"], 16)
                    pool.dma_start(conv_sample[:, :, c:c + n_ * P].rearrange("b r (c p) -> (b r) c p", p=P),
                                   crow[3:27, at:at + n_, :]).then_inc(S["crow_written"], 16)
                wait_read(pool, ("so", g))
                pool.dma_start(ssm_prompt[0].rearrange("h p n -> (h p) n")[g * 512:(g + 1) * 512, :]
                               .rearrange("(j p) n -> p j n", p=P),
                               sout.rearrange("p (j n) -> p j n", n=NS)).then_inc(S["sout_written"], 16)
                for j in range(4):
                    u = 4 * g + j
                    wait_read(pool, ("sn", g, j, 1))
                    pool.dma_start(ssm_sample.rearrange("b h p n -> (h p) b n")[u * P:(u + 1) * P, :, :],
                                   st0[:, u % 3, :, :]).then_inc(st0_written[u % 3], 16)
                pool.wait_ge(S["y_gained"], g + 1)
                pool.dma_start(y_spill[:, 4 * g:4 * g + 4, :], yb[:, g % 2, :, :]).then_inc(S["y_spilled"], 16)
            wait_read(pool, ("ss", GROUPS - 1, 1))
            for i in range(3):
                pool.wait_ge(st0_written[i], 16 * ST0_USES[i])
            for s in range(SB):
                pool.dma_start(vnew[0:SQ, s, :], kvtm[SQ * s:SQ * (s + 1), SMP, SV:SV + P]) \
                    .then_inc(S["vnew_loaded"], 16)
            wait_read(pool, ("x1", NT - 1, 1))
            link(nc.gpsimd.memset(hg, 0.0))
            for tt in range(NT):
                pool.wait_ge(S["hx_scaled"], tt + 1)
                for c in range(2):
                    pool.dma_start(x_rows[c * T + tt * P:c * T + (tt + 1) * P, :], xn[:, tt, :]) \
                        .then_inc(S["xn_stored"], 16)
            pool.wait_ge(S["xn_stored"], 16 * 2 * NT)
            wait_full(pool, ("rt", NT - 1))
            for i in (2, 3):
                link(nc.gpsimd.memset(rows_in[i], 0.0))
            wait_read(pool, ("slots",))

            def gather(e):
                pool.indirect_dma_start(rows_in[e % 4][0:SLOTS, :], None, x_rows[:, :],
                                        bass.IndirectOffsetOnAxis(ap=slot_row[0:SLOTS, e:e + 1], axis=0),
                                        bounds_check=2 * T - 1, oob_is_err=False) \
                    .then_inc(gathered_rows[e % 4], 16)

            for e in range(4):
                gather(e)
            for e in range(NE):
                if e + 4 < NE:
                    pool.wait_ge(S["t_full"], e + 1)
                    gather(e + 4)
                pool.wait_ge(S["dn0_read"], e + 1)
                pool.wait_ge(S["dn1_read"], e + 1)
                pool.indirect_dma_start(y_rows[:, :],
                                        bass.IndirectOffsetOnAxis(ap=slot_row[0:SLOTS, e:e + 1], axis=0),
                                        ysl[0:SLOTS, e % 2, :], None, bounds_check=2 * T - 1, oob_is_err=False) \
                    .then_inc(pair["scattered"][e % 2], 16)
            for i in range(2):
                pool.wait_ge(pair["scattered"][i], 16 * NE // 2)
        def ssd_pe(pe, g, product, turn, prompt, sample):
            mm = nc.tensor.matmul
            pe.wait_ge(pair["cin_loaded"][0], 16 * 3 * (g + 1))
            o = claim(pe, ("cT", g))
            for j in range(6):
                ins = turn(o[:, 24 * j:24 * (j + 1)], cin[0:24, j, :], 24)
            filled(ins, ("cT", g))
            w = wait_chunk(pe, ("wx", g))
            o = claim(pe, ("xbcS", g, 0))
            for j in range(4):
                ins = product(o[:, j * P:(j + 1) * P], w, j * P, P, sample, P)
            filled(ins, ("xbcS", g, 0))
            for j in range(4):
                o = claim(pe, ("xbc", g, j))
                filled(product(o, w, j * P, P, prompt, TP), ("xbc", g, j))
            if g:
                squares_pe(pe, g - 1)
            else:
                pe.wait_ge(S["a_ready"], 1)
                for tt in range(NT):
                    o = claim(pe, ("ac", tt))
                    filled(mm(o[:, 0:HEADS], (cum_p if tt < SMP else cum_s)[:], av[:, tt, :], start=True, stop=True),
                           ("ac", tt))
                    o = claim(pe, ("ae", tt))
                    filled(mm(o[:, 0:HEADS], (ones if tt < SMP else same)[:], av[:, tt, :], start=True, stop=True),
                           ("ae", tt))
            w = wait_chunk(pe, ("wbc", g))
            o = claim(pe, ("xbcS", g, 1))
            for j in range(2):
                ins = product(o[:, j * P:(j + 1) * P], w, j * P, P, sample, P)
            filled(ins, ("xbcS", g, 1))
            for j in range(2):
                o = claim(pe, ("xbc", g, 4 + j))
                filled(product(o, w, j * P, P, prompt, TP), ("xbc", g, 4 + j))
            w = wait_chunk(pe, ("wz", g))
            for j in range(4):
                o = claim(pe, ("z", g, j))
                filled(product(o, w, j * P, P, prompt, TP), ("z", g, j))
            o = claim(pe, ("zS", g))
            for j in range(4):
                ins = product(o[:, j * P:(j + 1) * P], w, j * P, P, sample, P)
            filled(ins, ("zS", g))
            pe.wait_ge(S["gathered"], 6 * (g + 1))
            for c, js in ((0, range(4)), (1, range(4, 6))):
                o = claim(pe, ("cO", g, c))
                for j in js:
                    ins = turn(o[0:27, (j - js[0]) * P:(j - js[0] + 1) * P], cgo[:, j, :])
                filled(ins, ("cO", g, c))
            pe.wait_ge(S["xs_ready"], 6 * (g + 1))
            o = claim(pe, ("bt", g, 0))
            for tt in range(SMP):
                ins = turn(o[:, tt * P:(tt + 1) * P], bcT[:, 0, tt * P:(tt + 1) * P])
            filled(ins, ("bt", g, 0))
            o = claim(pe, ("bt", g, 1))
            filled(turn(o[:, 0:P], bcT[:, 0, TP:T]), ("bt", g, 1))
            for step in range(NT + 1):
                if step < NT:
                    tt = step
                    tok = slice(tt * P, (tt + 1) * P)
                    o = claim(pe, ("xt", g, tt))
                    for j in range(4):
                        ins = turn(o[:, j * P:(j + 1) * P], xsT[:, j, tok])
                    filled(ins, ("xt", g, tt))
                    o = claim(pe, ("cb", g, tt))
                    filled(mm(o[:, 0:P], bcT[:, 0, tok], bcT[:, 1, tok], start=True, stop=True), ("cb", g, tt))
                    for i in range(2):
                        o = claim(pe, ("sg", g, tt, i))
                        for h in range(4):
                            hd = HG * g + 4 * i + h
                            ins = mm(o[:, h * P:(h + 1) * P], av[:, tt, hd:hd + 1].broadcast_to([P, P]),
                                     (cum_p if tt < SMP else cum_s)[:], start=True, stop=True)
                        filled(ins, ("sg", g, tt, i))
                if step == 0:
                    continue
                tt = step - 1
                if 0 < tt < SMP:
                    wait_read(pe, ("st", g, tt - 1))
                    o = claim(pe, ("yi", g, tt))
                    for j in range(4):
                        ins = mm(o[:, j * P:(j + 1) * P], stT[:, j * P:(j + 1) * P], bcT[:, 1, tt * P:(tt + 1) * P],
                                 start=True, stop=True)
                    filled(ins, ("yi", g, tt))
                wait_read(pe, ("xt", g, tt))
                if tt < SMP:
                    wait_read(pe, ("bt", g, 1))
                    pe.wait_ge(S["xw_ready"], NT * g + tt + 1)
                    o = claim(pe, ("st", g, tt))
                    filled(mm(o, btm[:, tt, :], xw[:, tt % 2, :], start=True, stop=True), ("st", g, tt))
                o = claim(pe, ("yo", g, tt))
                for i in range(2):
                    pe.wait_ge(S["mt_ready"], 2 * (NT * g + tt) + i + 1)
                    m = mt[:, (2 * (NT * g + tt) + i) % 4, :]
                    for h in range(4 * i, 4 * i + 4):
                        ins = mm(o[HP * (h % 2):HP * (h % 2) + HP, (h // 2) * P:(h // 2 + 1) * P],
                                 xdt[:, tt % 2, HP * h:HP * (h + 1)], m[:, (h % 4) * P:(h % 4 + 1) * P],
                                 start=True, stop=True)
                filled(ins, ("yo", g, tt))
            wait_read(pe, ("st", g, SMP - 1))
            o = claim(pe, ("so", g))
            for j in range(4):
                ins = turn(o[:, j * P:(j + 1) * P], stT[:, j * P:(j + 1) * P])
            filled(ins, ("so", g))
            pe.wait_ge(S["bms_ready"], g + 1)
            pe.wait_ge(S["xw_ready"], NT * (g + 1))
            for j in range(4):
                u = 4 * g + j
                pe.wait_ge(st0_loaded[u % 3], 16 * (u // 3 + 1))
                for i in range(2):
                    o = claim(pe, ("s0", g, j, i))
                    for b in range(4):
                        ins = turn(o[:, b * P:(b + 1) * P], st0[:, u % 3, 4 * i + b, :])
                    filled(ins, ("s0", g, j, i))
                for i in range(2):
                    o = claim(pe, ("sn", g, j, i))
                    filled(mm(o, xw[:, 0, j * P:(j + 1) * P], bms[:, 4 * i:4 * i + 4, :].rearrange("p b n -> p (b n)"),
                              start=True, stop=True), ("sn", g, j, i))
                wait_read(pe, ("s0", g, j, 1))
                o = claim(pe, ("ys", g, j))
                for b in range(SB):
                    ins = mm(o[:, b * SQ:(b + 1) * SQ], s0T[:, b, :], bcT[:, 1, TP + b * SQ:TP + (b + 1) * SQ],
                             start=True, stop=True)
                filled(ins, ("ys", g, j))
            if g == GROUPS - 1:
                w = wait_chunk(pe, ("wga", 0))
                for j in range(4):
                    o = claim(pe, ("ga", 0, j))
                    filled(product(o, w, j * P, P, prompt, TP), ("ga", 0, j))
                    if j == 1:
                        squares_pe(pe, g)
                o = claim(pe, ("gaS", 0))
                for j in range(4):
                    ins = product(o[:, j * P:(j + 1) * P], w, j * P, P, sample, P)
                filled(ins, ("gaS", 0))

        def squares_pe(pe, g):
            mm = nc.tensor.matmul
            pe.wait_ge(S["y_squares"], g + 1)
            for i, (a, b) in enumerate(((0, TP), (TP, T))):
                o = claim(pe, ("ss", g, i))
                for j in range(4):
                    ins = mm(o[:, 0:b - a], ones[:], zT[:, j, a:b], start=j == 0, stop=j == 3)
                filled(ins, ("ss", g, i))

        def attention_pe(pe, turn):
            mm = nc.tensor.matmul
            pe.wait_ge(S["kz_ready"], 1)
            for i in range(SMP):
                n = P * (i + 1)
                for k in range(AH + 3):
                    if k < AH:
                        t, g = k // AKV, k % AKV
                        o = claim(pe, ("s", i, k))
                        filled(mm(o[:, 0:n], oT[:, t, i * P:(i + 1) * P], kz[:, g, 0:n], start=True, stop=True),
                               ("s", i, k))
                    if 2 <= k < AH + 2:
                        u = AH * i + k - 2
                        pe.wait_ge(S["p_scaled"], u + 1)
                        o = claim(pe, ("pT", i, k - 2))
                        for c in range(i + 1):
                            ins = turn(o[:, c * P:(c + 1) * P], sm[:, u % 3, c * P:(c + 1) * P])
                        filled(ins, ("pT", i, k - 2))
                    if k >= 3:
                        u = AH * i + k - 3
                        t, g = (k - 3) // AKV, (k - 3) % AKV
                        half = (k - 3) // AR
                        if (k - 3) % AR == 0:
                            oo = claim(pe, ("o", i, half))
                        wait_read(pe, ("pT", i, k - 3))
                        for c in range(i + 1):
                            ins = mm(oo[HD * g:HD * (g + 1), (t % 4) * P:(t % 4 + 1) * P],
                                     kvtm[:, c, SV + g * HD:SV + (g + 1) * HD], pT[:, u % 2, c * P:(c + 1) * P],
                                     start=c == 0, stop=c == i)
                        if (k - 3) % AR == AR - 1:
                            filled(ins, ("o", i, half))
            pe.wait_ge(S["kz_ready"], 2)
            for s in range(SB + 1):
                if s < SB:
                    pe.wait_ge(pair["kb_loaded"][s % 2], 16 * (s // 2 + 1))
                    for c in range(2):
                        o = claim(pe, ("kc", s, c))
                        for j in range(4):
                            ins = turn(o[:, j * P:(j + 1) * P], kb[:, s % 2, 4 * c + j, :])
                        filled(ins, ("kc", s, c))
                b = s - 1
                for g in range(AKV):
                    u = AKV * b + g
                    if s >= 1:
                        pe.wait_ge(S["p_scaled"], AH * SMP + u + 1)
                        pj = pexp[:, u % 2, 0:PAST].rearrange("p (k j) -> p j k", j=KJ)
                        for c in range(2):
                            o = claim(pe, ("pt", b, g, c))
                            for j in range(4):
                                ins = turn(o[:, j * P:(j + 1) * P], pj[:, 4 * c + j, :])
                            filled(ins, ("pt", b, g, c))
                if s >= 1:
                    o = claim(pe, ("pn", b))
                    for g in range(AKV):
                        ins = turn(o[0:SQ, g * P:(g + 1) * P], pexp[:, (AKV * b + g) % 2, PAST:KEYS])
                    filled(ins, ("pn", b))
                if s < SB:
                    wait_read(pe, ("kc", s, 0))
                    wait_read(pe, ("kc", s, 1))
                    for g in range(AKV):
                        claim(pe, ("ds", s, g))
                        o = bank(("ds", s, g), 3)[:, 0:KEYS]
                        for c in range(3):
                            lo, hi = c * 512, min((c + 1) * 512, KEYS)
                            rhs = kcT[:, s % 2, lo:hi] if c < 2 else kT[:, TP + s * SQ:TP + (s + 1) * SQ]
                            ins = mm(o[:, lo:hi], qz[:, s, g, :], rhs, start=True, stop=True)
                        filled(ins, ("ds", s, g))
                if s < 1:
                    continue
                pe.wait_ge(pair["vb_loaded"][b % 2], 16 * (b // 2 + 1))
                if b == 0:
                    pe.wait_ge(S["vnew_loaded"], 16 * SB)
                o = claim(pe, ("do", b))
                for g in range(AKV):
                    u = AKV * b + g
                    for c in range(2):
                        wait_read(pe, ("pt", b, g, c))
                    cols_ = slice(g * HD, (g + 1) * HD)
                    for j in range(KJ):
                        mm(o[cols_, 0:P], vb[:, b % 2, j, cols_], ptS[:, u % 2, j, :], start=j == 0, stop=False)
                    wait_read(pe, ("pn", b))
                    ins = mm(o[cols_, 0:P], vnew[0:SQ, b, cols_], ptN[0:SQ, g, :], start=False, stop=True)
                filled(ins, ("do", b))

        @block.tensor
        def _(pe):
            mm = nc.tensor.matmul

            def product(out, chunk, m0, m, rhs, n, ks=KD, first=True, last=True):
                for k in range(ks):
                    ins = mm(out, chunk[:, k, m0:m0 + m], rhs(k), start=first and k == 0, stop=last and k == ks - 1)
                return ins

            def turn(out, in_, rows=P):
                return nc.tensor.transpose(out, in_, ident[0:rows, 0:rows])

            prompt = lambda k: hT[:, k, 0:TP]
            sample = lambda k: hT[:, k, TP:T]

            pe.wait_ge(S["ident_ready"], 1)
            pe.wait_ge(params_loaded, 16 * 5)
            o = claim(pe, ("par", 0))
            filled(turn(o[:, 0:P], par[:, 0, :]), ("par", 0))
            o = claim(pe, ("par", 1))
            filled(turn(o[:, 0:24], par[0:24, 1, :], 24), ("par", 1))
            for step in range(NT + 1):
                if step < NT:
                    pe.wait_ge(S["x_scaled"], step + 1)
                    for c in range(2):
                        o = claim(pe, ("hT", step, c))
                        for k in range(4):
                            ins = turn(o[:, k * P:(k + 1) * P], xtm[:, step, (4 * c + k) * P:(4 * c + k + 1) * P])
                        filled(ins, ("hT", step, c))
                if step > 0:
                    tt = step - 1
                    w = wait_chunk(pe, ("small",)) if tt == 0 else slot(("small",))
                    wait_read(pe, ("hT", tt, 1))
                    o = claim(pe, ("kv", tt))
                    for k in range(KD):
                        ins = mm(o[:, 0:SW], hT[:, k, tt * P:(tt + 1) * P], w[:, k, 0:SW], start=k == 0, stop=k == KD - 1)
                    filled(ins, ("kv", tt))
            pe.wait_ge(consts, 3)
            for c in range(2):
                w = wait_chunk(pe, ("wq", c))
                for t in range(4):
                    o = claim(pe, ("q", 4 * c + t))
                    filled(product(o, w, t * P, P, prompt, TP), ("q", 4 * c + t))
                o = claim(pe, ("qS", c))
                for t in range(4):
                    ins = product(o[:, t * P:(t + 1) * P], w, t * P, P, sample, P)
                filled(ins, ("qS", c))
            w = wait_chunk(pe, ("wqi",))
            for t in range(4):
                o = claim(pe, ("qi", t))
                filled(product(o, w, t * P, P, prompt, TP), ("qi", t))
            o = claim(pe, ("qiS",))
            for t in range(4):
                ins = product(o[:, t * P:(t + 1) * P], w, t * P, P, sample, P)
            filled(ins, ("qiS",))
            wait_read(pe, ("kv", NT - 1))
            o = claim(pe, ("kT", 0))
            for tt in range(SMP):
                ins = turn(o[:, tt * P:(tt + 1) * P], kvtm[:, tt, SK:SK + P])
            filled(ins, ("kT", 0))
            o = claim(pe, ("kT", 1))
            filled(turn(o[:, 0:P], kvtm[:, SMP, SK:SK + P]), ("kT", 1))
            o = claim(pe, ("kT", 2))
            for tt in range(SMP):
                ki = kvtm[:, tt, SKI:SKI + IDIM]
                turn(o[0:HD, tt * P:(tt + 1) * P], ki)
                ins = mm(o[HD:P, tt * P:(tt + 1) * P], ki, ident[:], start=True, stop=True)
            filled(ins, ("kT", 2))
            o = claim(pe, ("kT", 3))
            filled(turn(o[0:HD, 0:P], kvtm[:, SMP, SKI:SKI + IDIM]), ("kT", 3))
            wait_read(pe, ("kT", 3))
            for i in range(1, 4):
                for h in range(IH):
                    o = claim(pe, ("pd", i, h))
                    filled(mm(o[:, 0:P * (i + 1)], qiT[:, h // 2, i * P:(i + 1) * P], kiT[:, h % 2, 0:P * (i + 1)],
                              start=True, stop=True), ("pd", i, h))
            pe.wait_ge(S["wl_ready"], 1)
            o = claim(pe, ("wc",))
            filled(mm(o[:, 0:SB], wl, stream[:], start=True, stop=True), ("wc",))
            di = [claim(pe, ("di", i)) for i in range(3)]
            pe.wait_ge(S["wsel_ready"], 1)
            for s in range(SB + 2):
                if s < SB:
                    pe.wait_ge(pair["kx_loaded"][s % 2], 16 * (s // 2 + 1))
                    for c in range(2):
                        o = claim(pe, ("kx", s, c))
                        for j in range(4):
                            ins = turn(o[0:IDIM, j * P:(j + 1) * P], kx_in[:, s % 2, 4 * c + j, :])
                        filled(ins, ("kx", s, c))
                if 1 <= s <= SB:
                    b = s - 1
                    wait_read(pe, ("kx", b, 0))
                    wait_read(pe, ("kx", b, 1))
                    for c in range(3):
                        o = claim(pe, ("dd", b, c))
                        rhs = kxT[:, b % 2, c * 512:(c + 1) * 512] if c < 2 else \
                            kiT[:, 0, TP + b * SQ:TP + (b + 1) * SQ]
                        filled(mm(o[:, 0:rhs.shape[1]], qis[:, b].rearrange("d h q -> d (h q)"), rhs,
                                  start=True, stop=True), ("dd", b, c))
                if s >= 2:
                    b = s - 2
                    wait_read(pe, ("dd", b, 2))
                    for c in range(3):
                        w_ = 512 if c < 2 else SQ
                        ins = mm(di[c][:, 0:w_], wsel[:, b, :], rel[:, b % 2, c * 512:c * 512 + w_],
                                 start=b == 0, stop=b == SB - 1, skip_group_check=True)
                        if b == SB - 1:
                            filled(ins, ("di", c))
            for g in range(GROUPS):
                ssd_pe(pe, g, product, turn, prompt, sample)
            attention_pe(pe, turn)
            for n in range(2):
                for what in ("gb", "a", "b") if n == 0 else ("ga", "gb", "a", "b"):
                    if what[0] == "g":
                        ws = [wait_chunk(pe, ("w" + what, n))]
                        rp, rs = [prompt], [sample]
                    elif what == "a":
                        ws = [wait_chunk(pe, ("wso", n, c)) for c in range(2)]
                        rp = [lambda k: yz[:, k, 0:TP], lambda k: yz[:, 8 + k, 0:TP]]
                        rs = [lambda k: yz[:, k, TP:T], lambda k: yz[:, 8 + k, TP:T]]
                        pe.wait_ge(S["y_back"], 16)
                    else:
                        ws = [wait_chunk(pe, ("wao", n))]
                        rp, rs = [lambda k: oT[:, k, 0:TP]], [lambda k: oT[:, k, TP:T]]
                        wait_read(pe, ("do", SB - 1))
                    for j in range(4):
                        o = claim(pe, (what, n, j))
                        for i, w in enumerate(ws):
                            ins = product(o, w, j * P, P, rp[i], TP, first=i == 0, last=i == len(ws) - 1)
                        filled(ins, (what, n, j))
                    o = claim(pe, (what + "S", n))
                    for j in range(4):
                        for i, w in enumerate(ws):
                            ins = product(o[:, j * P:(j + 1) * P], w, j * P, P, rs[i], P, first=i == 0,
                                          last=i == len(ws) - 1)
                    filled(ins, (what + "S", n))
            ws = [wait_chunk(pe, ("wo", n)) for n in range(2)]
            pe.wait_ge(S["m_ready"], 2)

            def router(tt):
                if tt == 0:
                    pe.wait_ge(S["router_loaded"], 32)
                wait_read(pe, ("h2", tt, 1))
                o = claim(pe, ("rt", tt))
                for k in range(KD):
                    ins = mm(o[:, 0:MG + NE], h2T[:, k, tt * P:(tt + 1) * P], wr[:, k, :], start=k == 0, stop=k == KD - 1)
                filled(ins, ("rt", tt))

            for tt in range(NT + 2):
                if tt < NT:
                    for n in range(2):
                        o = claim(pe, ("x1", tt, n))
                        for k in range(KD):
                            ins = mm(o, mrg[:, k, tt * P:(tt + 1) * P], ws[n][:, k, :], start=k == 0, stop=k == KD - 1)
                        filled(ins, ("x1", tt, n))
                if tt >= NT:
                    router(tt - 2)
                if 1 <= tt <= NT:
                    pe.wait_ge(S["hx_scaled"], tt)
                    for c in range(2):
                        o = claim(pe, ("h2", tt - 1, c))
                        for k in range(4):
                            ins = turn(o[:, k * P:(k + 1) * P], xn[:, tt - 1, (4 * c + k) * P:(4 * c + k + 1) * P])
                        filled(ins, ("h2", tt - 1, c))
                if 2 <= tt < NT:
                    router(tt - 2)
            pe.wait_ge(S["hot_ready"], 1)
            o = claim(pe, ("rank",))
            mm(o[:, 0:NE], cum_p[:], cnt[:, 0, :], start=True, stop=True)
            for t in range(NT):
                later = NT - t
                mm(o[:, (t + 1) * NE:(NT + 1) * NE].rearrange("p (t e) -> p t e", e=NE), ones[:],
                   cnt[:, t:t + 1, :].broadcast_to([P, later, NE]), start=t == 0, stop=False, skip_group_check=True)
            ins = mm(o[:, NE:NT * NE], cum_p[:], cnt[:, 1:NT, :].rearrange("p t e -> p (t e)"), start=False, stop=True,
                     skip_group_check=True)
            filled(ins, ("rank",))
            o = claim(pe, ("slots",))
            for i in range(2 * NT):
                pe.wait_ge(S["at_ready"], i + 1)
                ins = mm(o[0:SLOTS, 0:NB], at_pos[:, i % 2, :], at_blk[:, i % 2, :], start=i == 0, stop=i == 2 * NT - 1)
                if i < 2 * NT - 1:
                    ins.then_inc(S["at_used"], 1)
            filled(ins, ("slots",))
            for b in range(8):
                pe.wait_ge(free[b], banks.free[b])

            def turned(e):
                pe.wait_ge(gathered_rows[e % 4], 16 * (e // 4 + 1))
                if e >= 2:
                    pe.wait_ge(S["t_read"], e - 1)
                o = pbank(e % 2)
                for k in range(KD):
                    ins = nc.tensor.transpose(o[:, k * SLOTS:(k + 1) * SLOTS], rows_in[e % 4][0:SLOTS, k * P:(k + 1) * P],
                                              ident[0:SLOTS, 0:SLOTS])
                ins.then_inc(S["t_full"], 1)

            def up(e):
                pe.wait_ge(S["t_read"], e + 1)
                pe.wait_ge(w13_loaded[e % 4], 32 * (e // 4 + 1))
                if e >= 2:
                    pe.wait_ge(S["heT_ready"], e - 1)
                for k in range(KD):
                    ins = mm(pbank(2 + e % 2)[0:SLOTS, :], hgT[:, e % 2, k, :], w13[e % 4][:, k, :], start=k == 0,
                             stop=k == KD - 1)
                ins.then_inc(S["up_full"], 1)

            def hidden_turned(e):
                pe.wait_ge(S["he_ready"], e + 1)
                for k in range(2):
                    ins = nc.tensor.transpose(pbank(2 + e % 2)[:, k * SLOTS:(k + 1) * SLOTS],
                                              hetm[0:SLOTS, e % 2, k * P:(k + 1) * P], ident[0:SLOTS, 0:SLOTS])
                ins.then_inc(S["heT_full"], 1)

            def down(e):
                pe.wait_ge(S["heT_ready"], e + 1)
                pe.wait_ge(w2_loaded[e % 4], 16 * (e // 4 + 1))
                if e >= 2:
                    pe.wait_ge(S["dn0_read"], e - 1)
                    pe.wait_ge(S["dn1_read"], e - 1)
                for m in range(2):
                    for k in range(2):
                        ins = mm(pbank(4 + 2 * (e % 2) + m)[0:SLOTS, :], heT[:, e % 2, k, :],
                                 w2s[e % 4][:, k, 512 * m:512 * m + 512], start=k == 0, stop=k == 1)
                    ins.then_inc(S["dn0_full" if m == 0 else "dn1_full"], 1)

            turned(0)
            turned(1)
            up(0)
            hidden_turned(0)
            for e in range(NE):
                if e + 2 < NE:
                    turned(e + 2)
                if e + 1 < NE:
                    up(e + 1)
                down(e)
                if e + 1 < NE:
                    hidden_turned(e + 1)

        def ssd_act(act, g, fn, copy):
            if g:
                act.wait_ge(S["y_gated"], g)
            copy(("cT", g), cst, bank(("cT", g))[:, 0:144].rearrange("p (j r) -> p j r", r=24))
            for j in range(7):
                if j == 4 and g == 0:
                    for tt in range(NT):
                        wait_read(act, ("ae", tt), 1)
                        release(fn(expae[:, tt, :], bank(("ae", tt))[:, 0:HEADS], ACT.Exp), ("ae", tt))
                    fn(w2v, w2v, ACT.Exp).then_inc(S["a_exp"], 1)
                if j < 6:
                    u = 6 * g + j
                    r = raw[:, u % 2, :]
                    rsm = r[:, 515:667].rearrange("p (b q) -> p b q", q=19)
                    if u < 2:
                        act.wait_ge(S["raw_zeroed"], 1)
                    else:
                        act.wait_ge(S["conv_done"], u - 1)
                        act.wait_ge(S["gathered"], u - 1)
                    c = j // 4
                    copy(("xbc", g, j), r[:, 3:515], bank(("xbc", g, j)))
                    wait_full(act, ("xbcS", g, c))
                    ins = fn(rsm[:, :, 3:19], bank(("xbcS", g, c))[:, (j - 4 * c) * P:(j - 4 * c + 1) * P]
                             .rearrange("p (b q) -> p b q", q=SQ), ACT.Copy)
                    if j in (3, 5):
                        release(ins, ("xbcS", g, c))
                    wait_read(act, ("cT", g))
                    fn(rsm[:, :, 0:3], cst[:, j, :].rearrange("p (b r) -> p b r", r=3), ACT.Copy) \
                        .then_inc(S["raw_ready"], 1)
                if j > 0:
                    u = 6 * g + j - 1
                    ct = 4 * g + j - 1 if j < 5 else 16 + g if j == 5 else 20 + g
                    dst = xsT[:, j - 1, :] if j < 5 else bcT[:, j - 5, :]
                    act.wait_ge(S["conv_done"], u + 1)
                    fn(dst[:, 0:TP], acc[:, 0, 0:TP], ACT.Silu, bias=cb_col[:, ct:ct + 1])
                    fn(dst[:, TP:T].rearrange("p (b q) -> p b q", q=SQ),
                       acc[:, 0, 512:664].rearrange("p (b q) -> p b q", q=19)[:, :, 3:19], ACT.Silu,
                       bias=cb_col[:, ct:ct + 1]).then_inc(S["xs_ready"], 1)
            if g:
                wait_full(act, ("ss", g - 1, 1))
            for j in range(4):
                wait_full(act, ("z", g, j))
                release(fn(zT[:, j, 0:TP], bank(("z", g, j)), ACT.Silu), ("z", g, j))
            wait_full(act, ("zS", g))
            release(fn(zT[:, :, TP:T], bank(("zS", g)).rearrange("p (j q) -> p j q", j=4), ACT.Silu), ("zS", g))
            if g:
                act.wait_ge(S["crow_written"], 96 * g)
            for c, w in ((0, 4), (1, 2)):
                copy(("cO", g, c), crow[0:27, 4 * c:4 * c + w, :],
                     bank(("cO", g, c))[0:27, 0:w * P].rearrange("p (j n) -> p j n", n=P))
            if g:
                act.wait_ge(S["bms_ready"], g)
            copy(("bt", g, 0), btm[:, 0:4, :], bank(("bt", g, 0)).rearrange("p (t n) -> p t n", n=P))
            copy(("bt", g, 1), btm[:, SMP, :], bank(("bt", g, 1))[:, 0:P])
            for tt in range(NT):
                k = NT * g + tt
                for i in range(2):
                    u = 2 * k + i
                    wait_full(act, ("sg", g, tt, i))
                    if k >= 2:
                        wait_full(act, ("yo", (k - 2) // NT, (k - 2) % NT))
                    for h in range(4):
                        hd = HG * g + 4 * i + h
                        ins = fn(mt[:, u % 4, h * P:(h + 1) * P], bank(("sg", g, tt, i))[:, h * P:(h + 1) * P],
                                 ACT.Relu, bias=acv[:, tt, hd:hd + 1], scale=-1.0)
                    ins.then_inc(S["mt_size"], 1)
                for i in range(2):
                    u = 2 * k + i
                    act.wait_ge(S["mt_size"], u + 1)
                    fn(mt[:, u % 4, :], mt[:, u % 4, :], ACT.Exp, scale=-1.0).then_inc(S["mt_exp"], 1)
                if tt >= 2:
                    wait_read(act, ("yo", g, tt - 2))
                elif g:
                    wait_read(act, ("yo", g - 1, tt + 3))
                for i in range(2):
                    dst = ebs[:, k % 2, 2 * i * P:2 * (i + 1) * P].rearrange("p (j l) -> p j l", l=P)
                    src = bank(("sg", g, tt, i)).rearrange("p (j o l) -> p o j l", o=2, l=P)
                    fn(dst[0:HP], src[0:HP, 0], ACT.Exp)
                    release(fn(dst[HP:P], src[HP:P, 1], ACT.Exp), ("sg", g, tt, i))
            if g:
                act.wait_ge(S["sout_written"], 16 * g)
            act.wait_ge(S["xw_ready"], NT * g + SMP)
            copy(("so", g), sout, bank(("so", g)))
            for j in range(4):
                for i in range(2):
                    if (g or j) and i == 0:
                        wait_full(act, ("ys", g, j - 1) if j else ("ys", g - 1, 3))
                    copy(("s0", g, j, i), s0T[:, 4 * i:4 * i + 4, :],
                         bank(("s0", g, j, i)).rearrange("p (b q) -> p b q", b=4))
            act.wait_ge(S["y_gated"], g + 1)
            fn(zT, yb[:, g % 2, :, :], ACT.Square).then_inc(S["y_squares"], 1)
            act.wait_ge(S["y_squares"], g + 1)
            for j in range(4):
                ins = fn(yb[:, g % 2, j, :], yb[:, g % 2, j, :], ACT.Copy, scale=gssm[:, 4 * g + j:4 * g + j + 1])
            ins.then_inc(S["y_gained"], 1)
            if g == GROUPS - 1:
                gate_act(act, "ga", 0, fn)

        def gate_act(act, what, m, fn):
            i = ("ga", "gb").index(what)
            for j in range(4):
                wait_full(act, (what, m, j))
                release(fn(gate[:, i, j, 0:TP], bank((what, m, j)), ACT.Sigmoid), (what, m, j))
            wait_full(act, (what + "S", m))
            release(fn(gate[:, i, :, TP:T], bank((what + "S", m)).rearrange("p (j q) -> p j q", j=4), ACT.Sigmoid),
                    (what + "S", m))

        @block.scalar
        def _(act):
            fn = nc.scalar.activation

            def copy(key, out, in_):
                wait_full(act, key)
                release(fn(out, in_, ACT.Copy), key)

            for tt in range(NT):
                act.wait_ge(x_loaded[tt], 16)
                if tt:
                    act.wait_ge(S["x_squares"], tt)
                fn(junk, xtm[:, tt, :], ACT.Square, accum_out=ssq[:, 0, tt:tt + 1]).then_inc(S["x_squares"], 1)
                act.wait_ge(S["x_var"], tt + 1)
                fn(ssq[:, 1, tt:tt + 1], ssq[:, 0, tt:tt + 1], ACT.Sqrt).then_inc(S["x_std"], 1)
                if tt == 0:
                    copy(("par", 0), pc[:, 0, :], bank(("par", 0))[:, 0:P])
                    copy(("par", 1), pc[:, 1, 0:24], bank(("par", 1))[:, 0:24])
            for tt in range(NT):
                copy(("kv", tt), kvtm[:, tt, :], bank(("kv", tt))[:, 0:SW])
            act.wait_ge(rows_loaded, 16 * 5)
            fn(a_row[:], a_row[:], ACT.Exp).then_inc(S["a_row_ready"], 1)
            for c in range(2):
                for t in range(4 * c, 4 * c + 4):
                    copy(("q", t), oT[:, t, 0:TP], bank(("q", t)))
                wait_full(act, ("qS", c))
                for t in range(4):
                    ins = fn(qs[:, :, 4 * c + t, :],
                             bank(("qS", c))[:, t * P:(t + 1) * P].rearrange("p (b q) -> p b q", q=SQ), ACT.Copy)
                release(ins, ("qS", c))
            for t in range(4):
                copy(("qi", t), qiT[:, t, :], bank(("qi", t)))
            act.wait_ge(S["pads_zeroed"], 1)
            wait_full(act, ("qiS",))
            for h in range(IH):
                ins = fn(qis[0:HD, :, h, :],
                         bank(("qiS",))[HD * (h % 2):HD * (h % 2) + HD, (h // 2) * P:(h // 2 + 1) * P]
                         .rearrange("p (b q) -> p b q", q=SQ), ACT.Copy)
            release(ins, ("qiS",))
            copy(("kT", 0), kT[:, 0:TP], bank(("kT", 0)))
            copy(("kT", 1), kT[:, TP:T], bank(("kT", 1))[:, 0:P])
            wait_full(act, ("kT", 2))
            fn(kiT[0:HD, 0, 0:TP], bank(("kT", 2))[0:HD, :], ACT.Copy)
            release(fn(kiT[HD:P, 1, 0:TP], bank(("kT", 2))[HD:P, :], ACT.Copy), ("kT", 2))
            copy(("kT", 3), kiT[0:HD, 0, TP:T], bank(("kT", 3))[0:HD, 0:P])
            for i in range(1, 4):
                for h in range(IH):
                    u, w = IH * (i - 1) + h, P * (i + 1)
                    wait_full(act, ("pd", i, h))
                    if u >= 2:
                        act.wait_ge(S["rel_used"], u - 1)
                    release(fn(rel[:, u % 2, 0:w], bank(("pd", i, h))[:, 0:w], ACT.Relu), ("pd", i, h))
            copy(("wc",), wcol, bank(("wc",))[:, 0:SB])
            act.wait_ge(S["rel_used"], 3 * IH)
            for s in range(SB + 1):
                if s < SB:
                    for c in range(2):
                        copy(("kx", s, c), kxT[0:IDIM, s % 2, :].rearrange("d (p j) -> d j p", j=KJ)[:, 4 * c:4 * c + 4, :],
                             bank(("kx", s, c))[0:IDIM, :].rearrange("d (j p) -> d j p", j=4))
                if s >= 1:
                    b = s - 1
                    for c in range(3):
                        w = 512 if c < 2 else SQ
                        wait_full(act, ("dd", b, c))
                        release(fn(rel[:, b % 2, 512 * c:512 * c + w], bank(("dd", b, c))[:, 0:w], ACT.Relu), ("dd", b, c))
            act.wait_ge(S["dt_exp"], 1)
            fn(w2v, w2v, ACT.Exp, scale=-1.0).then_inc(S["a_exp"], 1)
            for g in range(GROUPS):
                ssd_act(act, g, fn, copy)
            for i in range(SMP):
                w = P * (i + 1)
                for k in range(AH + 3):
                    if k < AH:
                        u = AH * i + k
                        wait_read(act, ("s", i, k))
                        fn(sm[:, u % 3, 0:w], sm[:, u % 3, 0:w], ACT.Exp, bias=mx[:, u % 8:u % 8 + 1], scale=-1.0,
                           accum_out=rsum[:, u % 8:u % 8 + 1]).then_inc(S["at_exp"], 1)
                    if 2 <= k < AH + 2:
                        u = AH * i + k - 2
                        copy(("pT", i, k - 2), pT[:, u % 2, 0:w], bank(("pT", i, k - 2))[:, 0:w])
                    if k >= 3 and (k - 3) % AR == AR - 1:
                        c = (k - 3) // AR
                        copy(("o", i, c), oT[:, 4 * c:4 * c + 4, i * P:(i + 1) * P],
                             bank(("o", i, c)).rearrange("p (t q) -> p t q", t=4))
            for s in range(SB + 1):
                if s < SB:
                    copy(("kc", s, 1), kcT[:, s % 2, :].rearrange("d (p j) -> d j p", j=KJ)[:, 4:8, :],
                         bank(("kc", s, 1)).rearrange("d (j p) -> d j p", j=4))
                if s >= 1:
                    for g in range(AKV):
                        copy(("pt", s - 1, g, 1), ptS[:, g, 4:8, :],
                             bank(("pt", s - 1, g, 1)).rearrange("p (j q) -> p j q", j=4))
                    copy(("pn", s - 1), ptN[0:SQ, :, :],
                         bank(("pn", s - 1))[0:SQ, 0:AKV * P].rearrange("p (g q) -> p g q", g=AKV))
                for g in range(AKV):
                    u = AKV * s + g
                    if s < SB:
                        v = AH * SMP + u
                        wait_read(act, ("ds", s, g))
                        fn(pexp[:, u % 2, :], pexp[:, u % 2, :], ACT.Exp, bias=mx[:, v % 8:v % 8 + 1], scale=-1.0,
                           accum_out=rsum[:, v % 8:v % 8 + 1]).then_inc(S["at_exp"], 1)
                if s >= 1:
                    copy(("do", s - 1), oT[:, :, TP + (s - 1) * SQ:TP + s * SQ],
                         bank(("do", s - 1))[:, 0:P].rearrange("p (t q) -> p t q", q=SQ))
            act.wait_ge(S["ss_var"], 1)
            fn(rt, rt, ACT.Sqrt).then_inc(S["ss_std"], 1)
            for m in range(2):
                for what in ("ga", "gb")[1 - m:]:
                    if m:
                        wait_read(act, (("aS", "bS")[what == "gb"], 0))
                        act.wait_ge(S["m_ready"], 1)
                    gate_act(act, what, m, fn)
            for tt in range(NT):
                wait_read(act, ("x1", tt, 1))
                fn(xn[:, tt, :], x1[:, tt, :], ACT.Square, accum_out=ssq[:, 2, tt:tt + 1]).then_inc(S["hx_squares"], 1)
                act.wait_ge(S["hx_var"], tt + 1)
                fn(ssq[:, 3, tt:tt + 1], ssq[:, 2, tt:tt + 1], ACT.Sqrt).then_inc(S["hx_std"], 1)
            for i in range(2):
                act.wait_ge(S["r_exp_in"], i + 1)
                e = rc[2] if i == 0 else rs1[:, 4, :]
                fn(e, e, ACT.Exp).then_inc(S["r_exp"], 1)
            for e in range(-1, NE):
                if e + 1 < NE:
                    u = e + 1
                    act.wait_ge(S["up_full"], u + 1)
                    fn(hsil[0:SLOTS, u % 2], pbank(2 + u % 2)[0:SLOTS, 0:FF], ACT.Silu) \
                        .then_inc(S["silu_ready"], 1)
                    act.wait_ge(S["heT_full"], u + 1)
                    fn(heT[:, u % 2], pbank(2 + u % 2)[:, 0:2 * SLOTS].rearrange("p (j q) -> p j q", j=2), ACT.Copy) \
                        .then_inc(S["heT_ready"], 1)
                if e >= 0:
                    act.wait_ge(S["dn0_full"], e + 1)
                    if e >= 2:
                        act.wait_ge(pair["scattered"][e % 2], 16 * (e // 2))
                    fn(ysl[0:SLOTS, e % 2, 0:512], pbank(4 + 2 * (e % 2))[0:SLOTS, :], ACT.Copy).then_inc(S["dn0_read"], 1)

        def ssd_dve(dve, g, link, over, top):
            tt_, ts_, stt = nc.vector.tensor_tensor, nc.vector.tensor_scalar, nc.vector.scalar_tensor_tensor
            heads = slice(HG * g, HG * (g + 1))
            y = yb[:, g % 2, :, :]
            for j in range(6):
                u = 6 * g + j
                ct = 4 * g + j if j < 4 else 16 + g if j == 4 else 20 + g
                dve.wait_ge(S["raw_ready"], u + 1)
                if u:
                    dve.wait_ge(S["xs_ready"], u)
                a, r = acc[:, 0, :], raw[:, u % 2, :]
                link(ts_(a, r[:, 0:664], cw_col[:, 0, ct:ct + 1], None, ALU.mult))
                for w in range(1, CW):
                    ins = stt(out=a, in0=r[:, w:w + 664], scalar=cw_col[:, w, ct:ct + 1], in1=a, op0=ALU.mult, op1=ALU.add)
                    if w < CW - 1:
                        link(ins)
                ins.then_inc(S["conv_done"], 1)
                if j == 2 and g == 0:
                    for tt in range(NT):
                        wait_full(dve, ("ac", tt))
                        release(nc.vector.tensor_copy(acv[:, tt, :], bank(("ac", tt))[:, 0:HEADS]), ("ac", tt))
                        wait_full(dve, ("ae", tt))
                        wait_read(dve, ("ac", tt))
                        release(tt_(w2v[:, tt, :], bank(("ae", tt))[:, 0:HEADS], acv[:, tt, :], ALU.subtract), ("ae", tt))
                if j == 3 and g:
                    squares_dve(dve, g - 1)
                a, b = TOP_UPTO[g], TOP_UPTO[g + 1]
                top(a + (b - a) * min(j, 5) // 5, a + (b - a) * min(j + 1, 5) // 5)
            for step in range(NT + 1):
                if step < NT:
                    tt = step
                    k = NT * g + tt
                    wait_full(dve, ("xt", g, tt))
                    if tt >= 2:
                        wait_full(dve, ("yo", g, tt - 2))
                    elif tt == 0 and g:
                        wait_full(dve, ("ys", g - 1, 3))
                    elif tt == 1 and g:
                        dve.wait_ge(S["sout_written"], 16 * g)
                    xp = bank(("xt", g, tt)).rearrange("p (h d) -> p h d", d=HP)
                    if k >= 2:
                        dve.wait_ge(S["xw_ready"], k - 1)
                    release(tt_(xdt[:, tt % 2, :].rearrange("p (h d) -> p h d", d=HP), xp, over(dtv[:, tt, heads], HP),
                                ALU.mult), ("xt", g, tt))
                    wait_full(dve, ("cb", g, tt))
                    if k >= 2:
                        dve.wait_ge(S["mt_ready"], 2 * (k - 1))
                    release(tt_(cbs[:, k % 2, :], bank(("cb", g, tt))[:, 0:P], (cum_p if tt < SMP else cum_s)[:], ALU.mult),
                            ("cb", g, tt))
                if step > 0:
                    tile_dve(dve, g, step - 1, link, over)
                if step < NT:
                    wait_read(dve, ("cb", g, tt))
                    for i in range(2):
                        dve.wait_ge(S["mt_exp"], 2 * k + i + 1)
                        m = mt[:, (2 * k + i) % 4, :].rearrange("p (h l) -> p h l", h=4)
                        tt_(m, m, cbs[:, k % 2, :].rearrange("p (o l) -> p o l", o=1).broadcast_to([P, 4, P]), ALU.mult) \
                            .then_inc(S["mt_ready"], 1)
            k = NT * g + SMP
            for i in range(2):
                wait_read(dve, ("sg", g, SMP, i))
            wait_read(dve, ("yo", g, SMP))
            for j in range(4):
                u = 4 * g + j
                dec = ebs[:, k % 2, j * P:(j + 1) * P].rearrange("p (b q) -> p b q", q=SQ)[:, :, SQ - 1:SQ]
                for i in range(2):
                    wait_full(dve, ("sn", g, j, i))
                    sv = st0[:, u % 3, 4 * i:4 * i + 4, :]
                    link(tt_(sv, sv, dec[:, 4 * i:4 * i + 4, :].broadcast_to([P, 4, NS]), ALU.mult))
                    release(tt_(sv, sv, bank(("sn", g, j, i)).rearrange("p (b n) -> p b n", n=NS), ALU.add),
                            ("sn", g, j, i))
                wait_full(dve, ("ys", g, j))
                release(tt_(ytmp[:, 0:P], bank(("ys", g, j))[:, 0:P], ebs[:, k % 2, j * P:(j + 1) * P], ALU.mult),
                        ("ys", g, j))
                wait_read(dve, ("ys", g, j))
                link(tt_(y[:, j, TP:T], y[:, j, TP:T], ytmp[:, 0:P], ALU.add))
            for j in range(4):
                link(stt(out=y[:, j, :], in0=xsT[:, j, :], scalar=dcol[:, 4 * g + j:4 * g + j + 1], in1=y[:, j, :],
                         op0=ALU.mult, op1=ALU.add))
            wait_read(dve, ("zS", g))
            tt_(y, y, zT, ALU.mult).then_inc(S["y_gated"], 1)
            if g == GROUPS - 1:
                squares_dve(dve, g)

        def tile_dve(dve, g, tt, link, over):
            tt_ = nc.vector.tensor_tensor
            heads = slice(HG * g, HG * (g + 1))
            k = NT * g + tt
            if tt == 0:
                if g == 0:
                    dve.wait_ge(S["q_spilled"], 16)
                elif g >= 2:
                    dve.wait_ge(S["y_spilled"], 16 * (g - 1))
            yv = yb[:, g % 2, :, tt * P:(tt + 1) * P]
            if 0 < tt < SMP:
                wait_full(dve, ("yi", g, tt))
                for i in range(2):
                    wait_read(dve, ("sg", g, tt, i))
                wait_read(dve, ("yo", g, tt - 1))
                release(tt_(ytmp, bank(("yi", g, tt)), ebs[:, k % 2, :], ALU.mult), ("yi", g, tt))
            if tt < SMP:
                wait_full(dve, ("st", g, tt))
                if tt == 0:
                    ins = nc.vector.tensor_copy(stT, bank(("st", g, tt)))
                else:
                    sv = stT.rearrange("p (h d) -> p h d", d=HP)
                    link(tt_(sv, sv, over(expae[:, tt, heads], HP), ALU.mult))
                    ins = tt_(stT, stT, bank(("st", g, tt)), ALU.add)
                release(ins, ("st", g, tt))
                wait_read(dve, ("st", g, tt))
            wait_full(dve, ("yo", g, tt))
            yo = bank(("yo", g, tt)).rearrange("p (j l) -> p j l", j=4)
            if 0 < tt < SMP:
                wait_read(dve, ("yi", g, tt))
                ins = tt_(yv, yo, ytmp.rearrange("p (j l) -> p j l", j=4), ALU.add)
            else:
                ins = nc.vector.tensor_copy(yv, yo)
            release(ins, ("yo", g, tt))

        def squares_dve(dve, g):
            tt_ = nc.vector.tensor_tensor
            for i, (a, b) in enumerate(((0, TP), (TP, T))):
                wait_full(dve, ("ss", g, i))
                src = bank(("ss", g, i))[:, 0:b - a]
                if g == 0:
                    ins = nc.vector.tensor_copy(ssrow[:, a:b], src)
                else:
                    ins = tt_(ssrow[:, a:b], ssrow[:, a:b], src, ALU.add)
                release(ins, ("ss", g, i))
                wait_read(dve, ("ss", g, i))

        def attention_dve(dve, link, over):
            tt_, ts_, copy = nc.vector.tensor_tensor, nc.vector.tensor_scalar, nc.vector.tensor_copy
            dve.wait_ge(S["q_back"], 16)
            link(nc.vector.memset(kz, 0.0))
            for g in range(AKV):
                rows = slice(HD * g, HD * (g + 1))
                ins = copy(kz[rows, g, :], kT[rows, 0:TP])
                if g == 0:
                    link(ins)
            ins.then_inc(S["kz_ready"], 1)
            link(nc.vector.memset(qz, 0.0))
            for g in range(AKV):
                rows = slice(HD * g, HD * (g + 1))
                ins = copy(qz[rows, :, g, :], qs[rows].rearrange("d s t q -> d s (t q)"))
                if g == 0:
                    link(ins)
            ins.then_inc(S["kz_ready"], 1)

            def least(key, out, scores, bias, u):
                release(nc.vector.tensor_tensor_reduce(out=out, in0=scores, in1=bias, scale=-ATT_SCALE, scalar=3.0e38,
                                                       op0=ALU.add, op1=ALU.min, accum_out=mx[:, u % 8:u % 8 + 1]), key)

            def scaled(p, u):
                dve.wait_ge(S["at_exp"], u + 1)
                r = rinv[:, u % 8:u % 8 + 1]
                link(nc.vector.reciprocal(r, rsum[:, u % 8:u % 8 + 1]))
                ts_(p, p, r, None, ALU.mult).then_inc(S["p_scaled"], 1)

            for i in range(SMP):
                w = P * (i + 1)
                bias = adm_att[:] if i == 0 else bias_p[i]
                for k in range(AH + 1):
                    u = AH * i + k
                    if k < AH:
                        wait_full(dve, ("s", i, k))
                        least(("s", i, k), sm[:, u % 3, 0:w], bank(("s", i, k))[:, 0:w], bias, u)
                    if k >= 1:
                        scaled(sm[:, (u - 1) % 3, 0:w], u - 1)

            def keys(s):
                wait_full(dve, ("kc", s, 0))
                release(copy(kcT[:, s % 2, :].rearrange("d (p j) -> d j p", j=KJ)[:, 0:4, :],
                             bank(("kc", s, 0)).rearrange("d (j p) -> d j p", j=4)), ("kc", s, 0))

            keys(0)
            for s in range(SB + 1):
                if s >= 1:
                    for g in range(AKV):
                        key = ("pt", s - 1, g, 0)
                        wait_full(dve, key)
                        release(copy(ptS[:, g, 0:4, :], bank(key).rearrange("p (j q) -> p j q", j=4)), key)
                for g in range(AKV):
                    u = AKV * s + g
                    if s < SB:
                        wait_full(dve, ("ds", s, g))
                        if s == 0:
                            wait_full(dve, ("s", SMP - 1, AH - 1))
                        else:
                            wait_full(dve, ("pn", s - 1))
                        if g == 0:
                            dve.wait_ge(pair["bexp_loaded"][s % 2], 16 * AR * (s // 2 + 1))
                        least(("ds", s, g), pexp[:, u % 2, :], bank(("ds", s, g), 3)[:, 0:KEYS], bexp[:, s % 2, :],
                              AH * SMP + u)
                if s < SB:
                    for g in range(AKV):
                        u = AKV * s + g
                        scaled(pexp[:, u % 2, :], AH * SMP + u)
                        if g == 0 and s + 1 < SB:
                            keys(s + 1)

        def logits_dve(dve, tt):
            wait_full(dve, ("rt", tt))
            release(nc.vector.tensor_tensor(lg[:, tt, :], bank(("rt", tt))[:, 0:MG + NE], brow[:], ALU.add), ("rt", tt))

        def route(dve, link, over):
            tt_, ts_, stt, red = (nc.vector.tensor_tensor, nc.vector.tensor_scalar, nc.vector.scalar_tensor_tensor,
                                  nc.vector.tensor_reduce)
            gl = lg[:, :, 0:MG]
            el = lg[:, :, MG:].rearrange("p t (g e) -> p t g e", g=MG)
            gmax, gsum, m1, m2, ex, den, top_ = (rs1[:, i, :] for i in range(7))

            def first(mask, vals, best, pr, k):
                link(tt_(mask, vals, over(best, k), ALU.is_equal))
                link(tt_(mask, mask, pr.rearrange("p (o e) -> p o e", o=1).broadcast_to([P, NT, k]), ALU.mult))
                link(red(top_, mask, AX.X, ALU.max))
                link(tt_(mask, mask, over(top_, k), ALU.is_equal))

            link(ts_(fills, count[:, 0:(T - 1) // SLOTS], float(SLOTS), float(SLOTS), ALU.mult, ALU.add))
            link(red(gmax, gl, AX.X, ALU.max))
            tt_(rc[2], gl, over(gmax, MG), ALU.subtract).then_inc(S["r_exp_in"], 1)
            first(rc[0], gl, gmax, prio[:, ME - MG:ME], MG)
            own = tmp_e[:, 0].rearrange("p t (g e) -> p t g e", g=MG)
            link(tt_(own, el, rc[0].rearrange("p t (g o) -> p t g o", o=1).broadcast_to([P, NT, MG, ME]), ALU.mult))
            link(red(rb[0], own.rearrange("p t g e -> p t e g"), AX.X, ALU.add))
            link(red(m1, rb[0], AX.X, ALU.max))
            first(rb[2], rb[0], m1, prio[:], ME)
            link(stt(out=rb[3], in0=rb[2], scalar=NEG, in1=rb[0], op0=ALU.mult, op1=ALU.add))
            link(red(m2, rb[3], AX.X, ALU.max))
            first(rb[4], rb[3], m2, prio[:], ME)
            tt_(ex, m2, m1, ALU.subtract).then_inc(S["r_exp_in"], 1)
            for c, m in ((0, rb[2]), (1, rb[4])):
                link(tt_(hot[:, c].rearrange("p t (g e) -> p t g e", g=MG),
                         m.rearrange("p t (o e) -> p t o e", o=1).broadcast_to([P, NT, MG, ME]),
                         rc[0].rearrange("p t (g o) -> p t g o", o=1).broadcast_to([P, NT, MG, ME]), ALU.mult))
            tt_(cnt, hot[:, 0], hot[:, 1], ALU.add).then_inc(S["hot_ready"], 1)
            dve.wait_ge(S["r_exp"], 2)
            link(red(gsum, rc[2], AX.X, ALU.add))
            link(ts_(den, ex, 1.0, None, ALU.add))
            link(tt_(den, den, gsum, ALU.mult))
            link(nc.vector.reciprocal(den, den))
            link(tt_(ex, ex, den, ALU.mult))
            link(nc.vector.tensor_copy(wk[:, 0, :], den))
            link(nc.vector.tensor_copy(wk[:, 1, :], ex))
            wait_full(dve, ("rank",))
            link(nc.vector.tensor_copy(rank_, bank(("rank",))[:, 0:NT * NE].rearrange("p (t e) -> p t e", e=NE)))
            tot = bank(("rank",))[:, NT * NE:(NT + 1) * NE]
            steps = (T - 1) // SLOTS
            times = fills.rearrange("p (o m) -> p o m", o=1)
            over_ = tmp_e.rearrange("p c t e -> p (c t e)")[:, 0:NE * steps].rearrange("p (e m) -> p e m", m=steps)
            release(tt_(over_, over(tot, steps), times.broadcast_to([P, NE, steps]), ALU.is_gt), ("rank",))
            wait_read(dve, ("rank",))
            link(red(need, over_, AX.X, ALU.add))
            link(nc.vector.tensor_copy(scan[:, 0], need))
            for i, d in enumerate((1, 2, 4, 8, 16)):
                s, t = scan[:, i % 2], scan[:, (i + 1) % 2]
                link(nc.vector.tensor_copy(t[:, 0:d], s[:, 0:d]))
                link(tt_(t[:, d:NE], s[:, d:NE], s[:, 0:NE - d], ALU.add))
            upto = scan[:, 1]
            link(tt_(first_x, upto, need, ALU.subtract))
            link(nc.vector.tensor_copy(beyond[:], upto[:, NE - 1:NE]))

            def per_choice(out, table):
                link(tt_(tmp_e.rearrange("p c t e -> p (c t) e"), hot.rearrange("p c t e -> p (c t) e"), table, ALU.mult))
                link(red(out, tmp_e, AX.X, ALU.add))

            def rows(ap):
                return ap.rearrange("p (o e) -> p o e", o=1).broadcast_to([P, 2 * NT, NE])

            for c in range(2):
                link(tt_(tmp_e[:, c], hot[:, c], rank_, ALU.mult))
            link(red(rk, tmp_e, AX.X, ALU.add))
            per_choice(ek, rows(count[:, 0:NE]))
            per_choice(xk, rows(first_x))
            over_ = tmp_e.rearrange("p c t e -> p (c t e)")[:, 0:2 * NT * steps].rearrange("p (c m) -> p c m", m=steps)
            link(tt_(over_, over(rk.rearrange("p c t -> p (c t)"), steps), times.broadcast_to([P, 2 * NT, steps]),
                     ALU.is_gt))
            link(red(qk.rearrange("p c t -> p (c t)"), over_, AX.X, ALU.add))
            link(stt(out=rk, in0=qk, scalar=-float(SLOTS), in1=rk, op0=ALU.mult, op1=ALU.add))
            link(ts_(rk, rk, 1.0, None, ALU.subtract))
            link(tt_(xk, xk, qk, ALU.add))
            link(tt_(xk, xk, ek, ALU.subtract))
            link(ts_(xk, xk, float(NE - 1), None, ALU.add))
            link(ts_(qk, qk, 1.0, None, ALU.min))
            link(tt_(xk, xk, qk, ALU.mult))
            link(tt_(bk, ek, xk, ALU.add))
            for i in range(2 * NT):
                c, tt = i // NT, i % NT
                if i >= 2:
                    dve.wait_ge(S["at_used"], i - 1)
                ts_(at_pos[:, i % 2, :], count[:], rk[:, c, tt:tt + 1], None, ALU.is_equal)
                ts_(at_blk[:, i % 2, :], count[:, 0:NB], bk[:, c, tt:tt + 1], entry[:, c, tt:tt + 1], ALU.is_equal,
                    ALU.mult).then_inc(S["at_ready"], 1)
            wait_full(dve, ("slots",))
            o = bank(("slots",))[0:SLOTS, 0:NB]
            nowhere = tmp_e.rearrange("p c t e -> p (c t e)")[0:SLOTS, 0:NB]
            link(ts_(nowhere, o, 0.0, float(NOWHERE), ALU.is_equal, ALU.mult))
            release(stt(out=slot_row[0:SLOTS, :], in0=o, scalar=-1.0, in1=nowhere, op0=ALU.add, op1=ALU.add), ("slots",))
            xs = count[:, 0:TAIL].rearrange("p (x o) -> p x o", o=1).broadcast_to([P, TAIL, NE])

            def per_block(ap):
                return ap.rearrange("p (o e) -> p o e", o=1).broadcast_to([P, TAIL, NE])

            link(tt_(tail_sum[:, 0], per_block(first_x), xs, ALU.is_le))
            link(tt_(tail_sum[:, 1], per_block(upto), xs, ALU.is_gt))
            link(tt_(tail_sum[:, 0], tail_sum[:, 0], tail_sum[:, 1], ALU.mult))
            link(tt_(tail_sum[:, 0], tail_sum[:, 0], per_block(count[:, 0:NE]), ALU.mult))
            rs_tail = tail_sum[:, 1, 0, 0:TAIL]
            link(red(rs_tail, tail_sum[:, 0], AX.X, ALU.add))
            link(nc.vector.tensor_copy(tail_expert[:], rs_tail))

        @block.vector
        def _(dve):
            n = [0]
            tt_ = nc.vector.tensor_tensor
            ts_ = nc.vector.tensor_scalar
            stt = nc.vector.scalar_tensor_tensor

            def link(ins):
                n[0] += 1
                ins.then_inc(dve_chain, 1)
                dve.wait_ge(dve_chain, n[0])

            def newton(r, v, tmp):
                link(tt_(tmp, r, r, ALU.mult))
                link(tt_(tmp, tmp, v, ALU.mult))
                link(ts_(tmp, tmp, -0.5, 1.5, ALU.mult, ALU.add))
                link(tt_(r, r, tmp, ALU.mult))

            def over(ap, k):
                return ap.rearrange("p (n o) -> p n o", o=1).broadcast_to([P, ap.shape[1], k])

            for tt in range(NT + 1):
                if tt < NT:
                    var, r = ssq[:, 0, tt:tt + 1], ssq[:, 1, tt:tt + 1]
                    dve.wait_ge(S["x_squares"], tt + 1)
                    ts_(var, var, 1.0 / D, EPS, ALU.mult, ALU.add).then_inc(S["x_var"], 1)
                    dve.wait_ge(S["x_std"], tt + 1)
                    link(nc.vector.reciprocal(r, r))
                    newton(r, var, ssq[:, 2, tt:tt + 1])
                    ts_(xtm[:, tt, :], xtm[:, tt, :], r, None, ALU.mult).then_inc(S["x_scaled"], 1)
                if tt == 1:
                    wait_read(dve, ("par", 1))
                if tt > 0:
                    for c in range(2):
                        key = ("hT", tt - 1, c)
                        wait_full(dve, key)
                        release(tt_(hT[:, 4 * c:4 * c + 4, (tt - 1) * P:tt * P],
                                    bank(key).rearrange("p (k q) -> p k q", k=4), over(gmix[:, 4 * c:4 * c + 4], P),
                                    ALU.mult), key)
            dve.wait_ge(consts, 3)
            dve.wait_ge(S["ident_ready"], 1)
            link(nc.vector.tensor_reduce(qsel[:], ident[:].rearrange("p (b q) -> p q b", q=SQ), AX.X, ALU.add))
            dve.wait_ge(S["a_row_ready"], 1)
            link(ts_(a_row[:], a_row[:], -1.0, None, ALU.mult))
            pairs = dsk_row[:].rearrange("p (j i) -> p i j", i=2)
            link(nc.vector.tensor_copy(dcol[0:HP, :], pairs[0:HP, 0, :]))
            link(nc.vector.tensor_copy(dcol[HP:P, :], pairs[HP:P, 1, :]))
            wait_read(dve, ("kv", NT - 1))
            link(ts_(kvtm[:, :, SWI:SDT], kvtm[:, :, SWI:SDT], IDX_SCALE, None, ALU.mult))
            tt_(wl.rearrange("p (h q) -> p h q", q=SQ), over(kvtm[:, SMP, SWI:SDT], SQ),
                qsel[:].rearrange("p (o q) -> p o q", o=1).broadcast_to([P, IH, SQ]), ALU.mult).then_inc(S["wl_ready"], 1)
            for i in range(1, 4):
                w = P * (i + 1)
                for h in range(IH):
                    u = IH * (i - 1) + h
                    wait_read(dve, ("pd", i, h))
                    wt = kvtm[:, i, SWI + h:SWI + h + 1]
                    if h == 0:
                        ins = ts_(bias_p[i], rel[:, u % 2, 0:w], wt, None, ALU.mult)
                    else:
                        ins = stt(out=bias_p[i], in0=rel[:, u % 2, 0:w], scalar=wt, in1=bias_p[i], op0=ALU.mult,
                                  op1=ALU.add)
                    ins.then_inc(S["rel_used"], 1)
                    dve.wait_ge(S["rel_used"], u + 1)
                link(tt_(bias_p[i][:, w - P:w], bias_p[i][:, w - P:w], adm_idx[:], ALU.add))
            link(nc.vector.memset(wsel, 0.0))
            wait_read(dve, ("wc",))
            for b in range(SB):
                ins = ts_(wsel[:, b, b * SQ:(b + 1) * SQ], qsel[:], wcol[:, b:b + 1], None, ALU.mult)
            ins.then_inc(S["wsel_ready"], 1)

            def top(a, b):
                for k in range(a, min(b, ROUNDS)):
                    i = min(k // ROUNDS_P, 3)
                    scores = bias_p[i + 1] if i < 3 else bias_s
                    link(nc.vector.max(top8, scores))
                    link(nc.vector.match_replace(scores, top8, scores, TAKEN))
                    if k in (ROUNDS_P - 1, 2 * ROUNDS_P - 1, 3 * ROUNDS_P - 1, ROUNDS - 1):
                        ts_(scores, scores, CUT, NEG, ALU.is_gt, ALU.mult).then_inc(S["bias_ready"], 1)

            for c in range(3):
                w = 512 if c < 2 else SQ
                wait_full(dve, ("di", c))
                release(nc.vector.tensor_copy(bias_s[:, 512 * c:512 * c + w], bank(("di", c))[:, 0:w]), ("di", c))
            wait_read(dve, ("di", 2))
            tmp = st0[:, 0, :, :].rearrange("p b n -> p (b n)")
            tm = [tmp[:, i * NT * HEADS:(i + 1) * NT * HEADS].rearrange("p (t h) -> p t h", h=HEADS) for i in range(4)]
            link(tt_(dtv, kvtm[:, :, SDT:SW], dtb_row[:].rearrange("p (o h) -> p o h", o=1).broadcast_to([P, NT, HEADS]),
                     ALU.add))
            link(ts_(w2v, dtv, -1.0, None, ALU.mult))
            tt_(w2v, w2v, dtv, ALU.max).then_inc(S["dt_exp"], 1)
            dve.wait_ge(S["a_exp"], 1)
            link(ts_(tm[0], w2v, 2.0, None, ALU.add))
            link(nc.vector.reciprocal(tm[0], tm[0]))
            link(tt_(tm[0], w2v, tm[0], ALU.mult))
            link(tt_(tm[1], tm[0], tm[0], ALU.mult))
            link(ts_(tm[2], tm[1], 2.0 / 17, 2.0 / 15, ALU.mult, ALU.add))
            for m in (13, 11, 9, 7, 5, 3, 1):
                link(tt_(tm[2], tm[2], tm[1], ALU.mult))
                link(ts_(tm[2], tm[2], 2.0 / m, None, ALU.add))
            link(tt_(tm[2], tm[2], tm[0], ALU.mult))
            link(stt(out=dtv, in0=dtv, scalar=0.0, in1=tm[2], op0=ALU.max, op1=ALU.add))
            tt_(av, dtv, a_row[:].rearrange("p (o h) -> p o h", o=1).broadcast_to([P, NT, HEADS]), ALU.mult) \
                .then_inc(S["a_ready"], 1)
            for g in range(GROUPS):
                ssd_dve(dve, g, link, over, top)
            attention_dve(dve, link, over)
            wait_full(dve, ("do", SB - 1))
            wait_read(dve, ("do", SB - 1))
            link(ts_(rr, ssrow, 1.0 / INNER, EPS, ALU.mult, ALU.add))
            nc.vector.tensor_copy(rt, rr).then_inc(S["ss_var"], 1)
            dve.wait_ge(S["ss_std"], 1)
            link(nc.vector.reciprocal(rt, rt))
            newton(rt, rr, mrg[:, 0, :])
            for m in range(2):
                wait_read(dve, ("gaS", m))
                link(tt_(gate[:, 0], gate[:, 0], rt.rearrange("p (o t) -> p o t", o=1).broadcast_to([P, 4, T]), ALU.mult))
                for j in range(4):
                    wait_full(dve, ("a", m, j))
                    release(tt_(mrg[:, 4 * m + j, 0:TP], bank(("a", m, j)), gate[:, 0, j, 0:TP], ALU.mult), ("a", m, j))
                wait_full(dve, ("aS", m))
                release(tt_(mrg[:, 4 * m:4 * m + 4, TP:T], bank(("aS", m)).rearrange("p (j q) -> p j q", j=4),
                            gate[:, 0, :, TP:T], ALU.mult), ("aS", m))
                wait_read(dve, ("gbS", m))
                for j in range(4):
                    wait_full(dve, ("b", m, j))
                    release(tt_(gate[:, 1, j, 0:TP], bank(("b", m, j)), gate[:, 1, j, 0:TP], ALU.mult), ("b", m, j))
                wait_full(dve, ("bS", m))
                release(tt_(gate[:, 1, :, TP:T], bank(("bS", m)).rearrange("p (j q) -> p j q", j=4),
                            gate[:, 1, :, TP:T], ALU.mult), ("bS", m))
                wait_read(dve, ("bS", m))
                tt_(mrg[:, 4 * m:4 * m + 4, :], mrg[:, 4 * m:4 * m + 4, :], gate[:, 1], ALU.add).then_inc(S["m_ready"], 1)
            for tt in range(NT + 2):
                if tt < NT:
                    dve.wait_ge(pair["xres_loaded"][tt % 2], 16 * (tt // 2 + 1))
                    for m in range(2):
                        wait_full(dve, ("x1", tt, m))
                        release(tt_(x1[:, tt, 512 * m:512 * m + 512], bank(("x1", tt, m)),
                                    xres[:, tt % 2, 512 * m:512 * m + 512], ALU.add), ("x1", tt, m))
                    var, r, tmp_ = (ssq[:, i, tt:tt + 1] for i in (2, 3, 4))
                    dve.wait_ge(S["hx_squares"], tt + 1)
                    ts_(var, var, 1.0 / D, EPS, ALU.mult, ALU.add).then_inc(S["hx_var"], 1)
                    dve.wait_ge(S["hx_std"], tt + 1)
                    link(nc.vector.reciprocal(r, r))
                    newton(r, var, tmp_)
                    ts_(xn[:, tt, :], x1[:, tt, :], r, None, ALU.mult).then_inc(S["hx_scaled"], 1)
                if tt >= NT:
                    logits_dve(dve, tt - 2)
                if 1 <= tt <= NT:
                    for c in range(2):
                        key = ("h2", tt - 1, c)
                        wait_full(dve, key)
                        release(tt_(h2T[:, 4 * c:4 * c + 4, (tt - 1) * P:tt * P],
                                    bank(key).rearrange("p (k q) -> p k q", k=4), over(gmoe[:, 4 * c:4 * c + 4], P),
                                    ALU.mult), key)
                if 2 <= tt < NT:
                    logits_dve(dve, tt - 2)
            wait_read(dve, ("rt", NT - 1))
            route(dve, link, over)
            for e in range(-2, NE):
                if e + 2 < NE:
                    u = e + 2
                    dve.wait_ge(S["t_full"], u + 1)
                    tt_(hgT[:, u % 2], pbank(u % 2).rearrange("p (k q) -> p k q", k=KD), over(gmoe, SLOTS), ALU.mult) \
                        .then_inc(S["t_read"], 1)
                if 0 <= e + 1 < NE:
                    u = e + 1
                    dve.wait_ge(S["silu_ready"], u + 1)
                    tt_(hetm[0:SLOTS, u % 2], pbank(2 + u % 2)[0:SLOTS, FF:2 * FF], hsil[0:SLOTS, u % 2],
                        ALU.mult).then_inc(S["he_ready"], 1)
                if e >= 0:
                    dve.wait_ge(S["dn1_full"], e + 1)
                    if e >= 2:
                        dve.wait_ge(pair["scattered"][e % 2], 16 * (e // 2))
                    nc.vector.tensor_copy(ysl[0:SLOTS, e % 2, 512:1024], pbank(5 + 2 * (e % 2))[0:SLOTS, :]) \
                        .then_inc(S["dn1_read"], 1)

        main.close()

        needed = nc.values_load(beyond[0:1, 0:1], min_val=0, max_val=TAIL)
        V = {name: sem(name) for name in ("ov_step", "ov_passed", "ov_idx", "ov_gathered", "ov_weights", "ov_turned",
                                          "ov_hT", "ov_up",
                                          "ov_silu", "ov_he", "ov_down", "ov_y", "ov_scattered")}
        with nc.If(needed > 0):
            with nc.Block() as block:
                @block.sync
                def _(sp):
                    with sp.Fori(0, TAIL) as x:
                        sp.wait_ge(V["ov_step"], x + 1)
                        e = sp.value_load(tail_expert[0:1, bass.ds(x, 1)], min_val=0, max_val=NE - 1)
                        for out, src in ((w13[0][:, :, 0:FF], w1), (w13[0][:, :, FF:], w3), (w2s[0], w2)):
                            sp.dma_start(out, src[bass.ds(e, 1)].rearrange("e (k p) f -> p (e k) f", p=P)) \
                                .then_inc(V["ov_weights"], 16)

                @block.gpsimd
                def _(pool):
                    def pass_on():
                        return nc.gpsimd.tensor_tensor(nothing[0:1, :], count[0:1, 0:1], count[0:1, 0:1], ALU.add)

                    pass_on().then_inc(V["ov_step"], 1)
                    with pool.Fori(0, TAIL) as x:
                        pool.wait_ge(V["ov_idx"], x + 1)
                        pass_on().then_inc(V["ov_passed"], 1)
                        pool.indirect_dma_start(hg[0:SLOTS, 0, :], None, x_rows[:, :],
                                                bass.IndirectOffsetOnAxis(ap=cur_row[0:SLOTS, 0:1], axis=0),
                                                bounds_check=2 * T - 1, oob_is_err=False).then_inc(V["ov_gathered"], 16)
                        pool.wait_ge(V["ov_y"], x + 1)
                        pool.wait_ge(V["ov_passed"], 2 * x + 1)
                        pass_on().then_inc(V["ov_passed"], 1)
                        pool.indirect_dma_start(y_rows[:, :], bass.IndirectOffsetOnAxis(ap=cur_row[0:SLOTS, 0:1], axis=0),
                                                ysl[0:SLOTS, 0, :], None, bounds_check=2 * T - 1, oob_is_err=False) \
                            .then_inc(V["ov_scattered"], 16)
                        pool.wait_ge(V["ov_scattered"], 16 * x + 16)
                        pool.wait_ge(V["ov_passed"], 2 * x + 2)
                        pass_on().then_inc(V["ov_step"], 1)

                @block.tensor
                def _(pe):
                    with pe.Fori(0, TAIL) as x:
                        pe.wait_ge(V["ov_gathered"], 16 * x + 16)
                        pe.wait_ge(consts, 3)
                        for k in range(KD):
                            ins = nc.tensor.transpose(psum[:, k * P:(k + 1) * P], hg[:, 0, k * P:(k + 1) * P], ident[:])
                        ins.then_inc(V["ov_turned"], 1)
                        pe.wait_ge(V["ov_hT"], x + 1)
                        pe.wait_ge(V["ov_weights"], 48 * x + 48)
                        for j in range(4):
                            for k in range(KD):
                                ins = nc.tensor.matmul(pbank(2)[:, j * SLOTS:(j + 1) * SLOTS],
                                                       w13[0][:, k, j * P:(j + 1) * P], hgT[:, 0, k, :],
                                                       start=k == 0, stop=k == KD - 1)
                        ins.then_inc(V["ov_up"], 1)
                        pe.wait_ge(V["ov_he"], x + 1)
                        for m in range(2):
                            for k in range(2):
                                ins = nc.tensor.matmul(pbank(4 + m)[0:SLOTS, :], heT[:, 0, k, :],
                                                       w2s[0][:, k, 512 * m:512 * m + 512], start=k == 0, stop=k == 1)
                        ins.then_inc(V["ov_down"], 1)

                @block.scalar
                def _(act):
                    with act.Fori(0, TAIL) as x:
                        act.wait_ge(V["ov_up"], x + 1)
                        nc.scalar.activation(hsil[:, 1, 0:2 * SLOTS], pbank(2)[:, 0:2 * SLOTS], ACT.Silu).then_inc(V["ov_silu"], 1)

                @block.vector
                def _(dve):
                    with dve.Fori(0, TAIL) as x:
                        dve.wait_ge(V["ov_step"], x + 1)
                        nc.vector.tensor_copy(cur_row[0:SLOTS, :], slot_row[0:SLOTS, bass.ds(x + NE, 1)]) \
                            .then_inc(V["ov_idx"], 1)
                        dve.wait_ge(V["ov_turned"], x + 1)
                        nc.vector.tensor_tensor(hgT[:, 0], psum[:, 0:KD * P].rearrange("p (k q) -> p k q", k=KD)[:, :, 0:SLOTS],
                                                gmoe.rearrange("p (k o) -> p k o", o=1).broadcast_to([P, KD, SLOTS]),
                                                ALU.mult).then_inc(V["ov_hT"], 1)
                        dve.wait_ge(V["ov_silu"], x + 1)
                        nc.vector.tensor_tensor(heT[:, 0].rearrange("p j q -> p (j q)"), pbank(2)[:, 2 * SLOTS:4 * SLOTS],
                                                hsil[:, 1, 0:2 * SLOTS], ALU.mult) \
                            .then_inc(V["ov_he"], 1)
                        dve.wait_ge(V["ov_down"], x + 1)
                        nc.vector.tensor_copy(ysl[0:SLOTS, 0, :], psum[0:SLOTS, 4 * 512:6 * 512]).then_inc(V["ov_y"], 1)

        with nc.Block() as block:
            @block.sync
            def _(sp):
                for tt in range(NT):
                    for c in range(2):
                        sp.dma_start(ypart[:, tt, c, :], y_rows[c * T + tt * P:c * T + (tt + 1) * P, :]) \
                            .then_inc(ypart_loaded[tt], 16)
                for tt in range(NT):
                    sp.wait_ge(S["fin_ready" if tt < NT - 1 else "last_ready"], tt + 1 if tt < NT - 1 else 1)
                    dst = y_prompt[0, tt * P:(tt + 1) * P, :] if tt < SMP else y_sample.rearrange("b q d -> (b q) d")
                    sp.dma_start(dst, x1[:, tt, :]).then_inc(S["y_written"], 16)
                sp.wait_ge(S["y_written"], 16 * NT)

            @block.gpsimd
            def _(pool):
                pool.wait_ge(S["fin_loaded"], 16)
                for tt in range(NT - 1):
                    pool.wait_ge(S["fx_scaled"], tt + 1)
                    nc.gpsimd.tensor_tensor(x1[:, tt, :], xn[:, tt, :], fin_row, ALU.mult).then_inc(S["fin_ready"], 1)

            @block.scalar
            def _(act):
                def over_rms(tt):
                    act.wait_ge(S["rms_ready"], tt + 1)
                    nc.scalar.activation(xn[:, tt, :], x1[:, tt, :], ACT.Copy, scale=ssq[:, 5, tt:tt + 1]) \
                        .then_inc(S["fx_scaled"], 1)

                for step in range(NT + 2):
                    if step < NT:
                        act.wait_ge(S["parts_added"], step + 1)
                        nc.scalar.activation(xn[:, step, :], x1[:, step, :], ACT.Square,
                                             accum_out=ssq[:, 4, step:step + 1]).then_inc(S["fx_squares"], 1)
                    if 1 <= step <= NT:
                        tt = step - 1
                        act.wait_ge(S["fx_var"], tt + 1)
                        nc.scalar.activation(ssq[:, 5, tt:tt + 1], ssq[:, 4, tt:tt + 1], ACT.Sqrt).then_inc(S["fx_std"], 1)
                    if 2 <= step < NT + 1:
                        over_rms(step - 2)

            @block.vector
            def _(dve):
                n = [0]
                stt, tt_, ts_ = nc.vector.scalar_tensor_tensor, nc.vector.tensor_tensor, nc.vector.tensor_scalar

                def link(ins):
                    n[0] += 1
                    ins.then_inc(S["last_chain"], 1)
                    dve.wait_ge(S["last_chain"], n[0])

                def scaled(tt):
                    v, r, t = ssq[:, 4, tt:tt + 1], ssq[:, 5, tt:tt + 1], ssq[:, 2, tt:tt + 1]
                    dve.wait_ge(S["fx_std"], tt + 1)
                    link(nc.vector.reciprocal(r, r))
                    link(tt_(t, r, r, ALU.mult))
                    link(tt_(t, t, v, ALU.mult))
                    link(ts_(t, t, -0.5, 1.5, ALU.mult, ALU.add))
                    if tt < NT - 1:
                        tt_(r, r, t, ALU.mult).then_inc(S["rms_ready"], 1)
                        return
                    link(tt_(r, r, t, ALU.mult))
                    stt(out=x1[:, tt, :], in0=x1[:, tt, :], scalar=r, in1=fin_row, op0=ALU.mult, op1=ALU.mult) \
                        .then_inc(S["last_ready"], 1)

                dve.wait_ge(S["fin_loaded"], 16)
                for step in range(NT + 2):
                    if step < NT:
                        dve.wait_ge(ypart_loaded[step], 32)
                        link(stt(out=x1[:, step, :], in0=ypart[:, step, 0, :], scalar=wk[:, 0, step:step + 1],
                                 in1=x1[:, step, :], op0=ALU.mult, op1=ALU.add))
                        stt(out=x1[:, step, :], in0=ypart[:, step, 1, :], scalar=wk[:, 1, step:step + 1],
                            in1=x1[:, step, :], op0=ALU.mult, op1=ALU.add).then_inc(S["parts_added"], 1)
                    if 1 <= step <= NT:
                        tt = step - 1
                        dve.wait_ge(S["fx_squares"], tt + 1)
                        ts_(ssq[:, 4, tt:tt + 1], ssq[:, 4, tt:tt + 1], 1.0 / D, EPS, ALU.mult, ALU.add) \
                            .then_inc(S["fx_var"], 1)
                    if step >= 2:
                        scaled(step - 2)


_INS = ['x_prompt', 'x_sample', 'cache_k', 'cache_v', 'cache_kidx', 'state_conv', 'state_ssm', 'norm_mix_g', 'w_in',
        'conv_w', 'conv_b', 'dt_bias', 'A_log', 'D_skip', 'ssm_norm_g', 'w_ssm_out', 'w_attn_out', 'w_o', 'norm_moe_g',
        'w_router_group', 'b_router_group', 'w_router_expert', 'b_router_expert', 'w1', 'w3', 'w2', 'norm_final_g']
_OUTS = [(1, TP, D), (SB, SQ, D), (1, TP, AKV, HD), (1, TP, AKV, HD), (1, TP, IDIM), (1, CW - 1, CD),
         (1, HEADS, HP, NS), (SB, SQ, AKV, HD), (SB, SQ, AKV, HD), (SB, SQ, IDIM), (SB, CW - 1, CD),
         (SB, HEADS, HP, NS)]


def kernel(**inputs):
    import numpy as _np
    import concourse.bacc as _bacc
    from concourse import mybir as _mybir
    from concourse.bass_utils import run_bass_kernel_spmd as _run

    nc = _bacc.Bacc("TRN2", target_bir_lowering=False, num_devices=1)
    arrays, args = {}, []
    for name in _INS:
        a = _np.ascontiguousarray(inputs[name])
        arrays[f"in_{name}"] = a
        args.append(nc.dram_tensor(f"in_{name}", a.shape, _mybir.dt.from_np(a.dtype), kind="ExternalInput").ap())
    for i, shape in enumerate(_OUTS):
        args.append(nc.dram_tensor(f"out_{i}", shape, _mybir.dt.float32, kind="ExternalOutput").ap())
    hybrid_layer(nc, *args)
    r = _run(nc, [arrays], core_ids=[0])
    return tuple(r.results[0][f"out_{i}"] for i in range(len(_OUTS)))
```
